# Optimizing a Trainium2 kernel written in Bass

```python
import math
import jax, jax.numpy as jnp
from jax import lax
import numpy as np

D_MODEL = 1024
BATCH = 1
SEQ = 256
DEPTH = 1
DEC_BATCH = 8
DEC_SEQ = 1
PAST_LEN = 2048
PAGE_SIZE = 128

HEAD_DIM = 64
N_HEADS_A = 8
N_KV_A = 2
GROUP_A = N_HEADS_A // N_KV_A
N_IDX_HEADS = 8
IDX_DIM = 64
N_HEADS_B = 8
WIDTH_A = N_HEADS_A * HEAD_DIM
WIDTH_B = N_HEADS_B * HEAD_DIM
TOPK_MAX = 256
N_BUCKETS = 32
MAX_DISTANCE = 128
N_GROUPS = 4
EXPERTS_PER_GROUP = 8
TOP_E = 2
D_EXPERT = 256
Q_BLOCK = 128
EPS = 1e-6
SPLIT_WIDTHS = (WIDTH_A, N_KV_A * HEAD_DIM, N_KV_A * HEAD_DIM, N_IDX_HEADS * IDX_DIM, N_IDX_HEADS, IDX_DIM,
                WIDTH_B, WIDTH_B, WIDTH_B, D_MODEL, D_MODEL)
D_IN = sum(SPLIT_WIDTHS)

kernel_name = "hybrid_dsa_stickbreak_hmoe_step"

def _rmsnorm(x, g):
    xf = x.astype(jnp.float32)
    y = xf * lax.rsqrt(jnp.mean(xf * xf, axis=-1, keepdims=True) + EPS)
    return (y * g.astype(jnp.float32)).astype(x.dtype)

def _t5_bucket(dist):
    n = jnp.maximum(dist, 0)
    max_exact = N_BUCKETS // 2
    nf = jnp.maximum(n, max_exact).astype(jnp.float32)
    large = max_exact + (jnp.log(nf / max_exact) / math.log(MAX_DISTANCE / max_exact)
                         * (N_BUCKETS - max_exact)).astype(jnp.int32)
    return jnp.where(n < max_exact, n, jnp.minimum(large, N_BUCKETS - 1))

def _take_rows(rows, idx):
    return jax.vmap(lambda r, i: r[i])(rows, idx)

def _project(xn, w_in):
    B, T, _ = xn.shape
    points = [int(p) for p in np.cumsum(SPLIT_WIDTHS)[:-1]]
    qa, ka, va, qi, wi, ki, qb, kb, vb, ga, gb = jnp.split(xn @ w_in, points, axis=-1)
    return (qa.reshape(B, T, N_HEADS_A, HEAD_DIM), ka.reshape(B, T, N_KV_A, HEAD_DIM),
            va.reshape(B, T, N_KV_A, HEAD_DIM), qi.reshape(B, T, N_IDX_HEADS, IDX_DIM),
            wi * N_IDX_HEADS ** -0.5, ki,
            qb.reshape(B, T, N_HEADS_B, HEAD_DIM), kb.reshape(B, T, N_HEADS_B, HEAD_DIM),
            vb.reshape(B, T, N_HEADS_B, HEAD_DIM), jax.nn.sigmoid(ga), jax.nn.sigmoid(gb))

def _dsa_attend(q, q_i, w_i, k_i, fetch, q_pos, bias_table, n_top):
    B, Q = q.shape[:2]
    L = k_i.shape[1]
    rel = jax.nn.relu(jnp.einsum('bqhd,bsd->bqhs', q_i, k_i) * IDX_DIM ** -0.5)
    score = jnp.einsum('bqhs,bqh->bqs', rel, w_i).astype(jnp.float32)
    causal = jnp.arange(L, dtype=jnp.int32)[None, :] <= q_pos[:, None]
    score = jnp.where(causal[None], score, -jnp.inf)
    _, sel = lax.top_k(score, n_top)
    k_sel, v_sel = fetch(sel)
    dist = q_pos[None, :, None] - sel
    bias = bias_table[_t5_bucket(dist)].astype(jnp.float32)
    bias = bias.reshape(B, Q, n_top, N_KV_A, GROUP_A).transpose(0, 1, 3, 4, 2)
    qg = q.reshape(B, Q, N_KV_A, GROUP_A, HEAD_DIM)
    logits = jnp.einsum('bqcgd,bqncd->bqcgn', qg, k_sel).astype(jnp.float32) * HEAD_DIM ** -0.5 + bias
    logits = jnp.where((dist >= 0)[:, :, None, None, :], logits, -jnp.inf)
    p = jax.nn.softmax(logits, axis=-1).astype(v_sel.dtype)
    o = jnp.einsum('bqcgn,bqncd->bqcgd', p, v_sel)
    return o.reshape(B, Q, WIDTH_A)

def _stick_breaking(q, k, v, q_pos):
    B, Q = q.shape[:2]
    L = k.shape[1]
    z = jnp.einsum('bqhd,bshd->bhqs', q, k).astype(jnp.float32) * HEAD_DIM ** -0.5
    strict = (jnp.arange(L, dtype=jnp.int32)[None, :] < q_pos[:, None])[None, None]
    log_keep = jnp.where(strict, jax.nn.log_sigmoid(-z), 0.0)
    after = lax.cumsum(log_keep, axis=3, reverse=True) - log_keep
    a = jnp.where(strict, jnp.exp(jax.nn.log_sigmoid(z) + after), 0.0)
    o = jnp.einsum('bhqs,bshd->bqhd', a.astype(v.dtype), v)
    return o.reshape(B, Q, WIDTH_B)

def _hier_moe(xn, w_rg, b_rg, w_re, b_re, w_gate, w_up, w_down):
    shp = xn.shape
    t = xn.reshape(-1, D_MODEL)
    p_group = jax.nn.softmax((t @ w_rg).astype(jnp.float32) + b_rg.astype(jnp.float32), axis=-1)
    g_w, g_idx = lax.top_k(p_group, 1)
    logit_e = jnp.einsum('nd,gde->nge', t, w_re).astype(jnp.float32) + b_re.astype(jnp.float32)
    logit_e = jnp.take_along_axis(logit_e, g_idx[:, :, None], axis=1)[:, 0]
    e_w, e_idx = lax.top_k(jax.nn.softmax(logit_e, axis=-1), TOP_E)
    e_w = e_w / jnp.sum(e_w, axis=-1, keepdims=True) * g_w
    within = jnp.sum(jax.nn.one_hot(e_idx, EXPERTS_PER_GROUP, dtype=jnp.float32) * e_w[..., None], axis=1)
    combine = (jax.nn.one_hot(g_idx[:, 0], N_GROUPS, dtype=jnp.float32)[:, :, None]
               * within[:, None, :]).astype(xn.dtype)
    y = jnp.zeros_like(t)
    for g in range(N_GROUPS):
        hid = jax.nn.silu(jnp.einsum('nd,edf->nef', t, w_gate[g])) * jnp.einsum('nd,edf->nef', t, w_up[g])
        y = y + jnp.einsum('nef,efd->nd', hid * combine[:, g, :, None], w_down[g])
    return y.reshape(shp)

def _merge_and_ffn(x, o_a, o_b, g_a, g_b, w_proj_a, w_proj_b, w_out, ln2_g, w_rg, b_rg, w_re, b_re,
                   w_gate, w_up, w_down):
    mixed = g_a * (o_a @ w_proj_a) + g_b * (o_b @ w_proj_b)
    h = x + mixed @ w_out
    return h + _hier_moe(_rmsnorm(h, ln2_g), w_rg, b_rg, w_re, b_re, w_gate, w_up, w_down)

def _prompt_mixers(q_a, k_a, v_a, q_i, w_i, k_i, q_b, k_b, v_b, bias_table):
    B, S = q_a.shape[:2]
    nb = S // Q_BLOCK
    n_top = min(TOPK_MAX, S // 4)

    def fetch(sel):
        return _take_rows(k_a, sel), _take_rows(v_a, sel)

    def blocks(a):
        return a.reshape((B, nb, Q_BLOCK) + a.shape[2:]).swapaxes(0, 1)

    def body(args):
        i, qa, qi, wi, qb = args
        pos = i * Q_BLOCK + jnp.arange(Q_BLOCK, dtype=jnp.int32)
        return (_dsa_attend(qa, qi, wi, k_i, fetch, pos, bias_table, n_top),
                _stick_breaking(qb, k_b, v_b, pos))

    o_a, o_b = lax.map(body, (jnp.arange(nb, dtype=jnp.int32), blocks(q_a), blocks(q_i), blocks(w_i), blocks(q_b)))
    return o_a.swapaxes(0, 1).reshape(B, S, WIDTH_A), o_b.swapaxes(0, 1).reshape(B, S, WIDTH_B)

def _sample_mixers(q_a, k_a, v_a, q_i, w_i, k_i, q_b, k_b, v_b,
                   cache_k_a, cache_v_a, cache_kidx_a, cache_k_b, cache_v_b, page_table, bias_table):
    Bd, T = q_a.shape[:2]
    n_top = min(TOPK_MAX, (PAST_LEN + T) // 4)
    pos = PAST_LEN + jnp.arange(T, dtype=jnp.int32)

    def gather_all(cache):
        return cache[page_table].reshape((Bd, PAST_LEN) + cache.shape[2:])

    k_i_all = jnp.concatenate([gather_all(cache_kidx_a), k_i], axis=1)

    def fetch(sel):
        s_past = jnp.minimum(sel, PAST_LEN - 1)
        phys = jax.vmap(lambda pt, p: pt[p])(page_table, s_past // PAGE_SIZE)
        off = s_past % PAGE_SIZE
        s_new = jnp.clip(sel - PAST_LEN, 0, T - 1)
        is_new = (sel >= PAST_LEN)[..., None, None]
        k_sel = jnp.where(is_new, _take_rows(k_a, s_new), cache_k_a[phys, off])
        v_sel = jnp.where(is_new, _take_rows(v_a, s_new), cache_v_a[phys, off])
        return k_sel, v_sel

    o_a = _dsa_attend(q_a, q_i, w_i, k_i_all, fetch, pos, bias_table, n_top)
    k_b_all = jnp.concatenate([gather_all(cache_k_b), k_b], axis=1)
    v_b_all = jnp.concatenate([gather_all(cache_v_b), v_b], axis=1)
    o_b = _stick_breaking(q_b, k_b_all, v_b_all, pos)
    return o_a, o_b

def setup_inputs(seed: int = 0) -> dict:
    key = jax.random.key(seed)
    ks = jax.random.split(key, 24)
    n_pages = PAST_LEN // PAGE_SIZE
    n_used = DEC_BATCH * n_pages
    n_pool = n_used + n_used // 4

    def nrm(k, shape, scale=1.0):
        return jax.random.normal(k, shape, jnp.float32) * scale

    page_table = jax.random.permutation(ks[7], n_pool)[:n_used].reshape(DEC_BATCH, n_pages).astype(jnp.int32)
    return {
        'x_prompt': nrm(ks[0], (BATCH, SEQ, D_MODEL)),
        'x_sample': nrm(ks[1], (DEC_BATCH, DEC_SEQ, D_MODEL)),
        'cache_k_a': nrm(ks[2], (DEPTH, n_pool, PAGE_SIZE, N_KV_A, HEAD_DIM)),
        'cache_v_a': nrm(ks[3], (DEPTH, n_pool, PAGE_SIZE, N_KV_A, HEAD_DIM)),
        'cache_kidx_a': nrm(ks[4], (DEPTH, n_pool, PAGE_SIZE, IDX_DIM)),
        'cache_k_b': nrm(ks[5], (DEPTH, n_pool, PAGE_SIZE, N_HEADS_B, HEAD_DIM)),
        'cache_v_b': nrm(ks[6], (DEPTH, n_pool, PAGE_SIZE, N_HEADS_B, HEAD_DIM)),
        'page_table': page_table,
        'rel_bias_table': nrm(ks[8], (N_BUCKETS, N_HEADS_A), 0.5),
        'ln1_g': 1.0 + nrm(ks[9], (DEPTH, D_MODEL), 0.02),
        'w_in': nrm(ks[10], (DEPTH, D_MODEL, D_IN), D_MODEL ** -0.5),
        'w_proj_a': nrm(ks[11], (DEPTH, WIDTH_A, D_MODEL), WIDTH_A ** -0.5),
        'w_proj_b': nrm(ks[12], (DEPTH, WIDTH_B, D_MODEL), WIDTH_B ** -0.5),
        'w_out': nrm(ks[13], (DEPTH, D_MODEL, D_MODEL), D_MODEL ** -0.5),
        'ln2_g': 1.0 + nrm(ks[14], (DEPTH, D_MODEL), 0.02),
        'w_router_group': nrm(ks[15], (DEPTH, D_MODEL, N_GROUPS), D_MODEL ** -0.5),
        'b_router_group': nrm(ks[16], (DEPTH, N_GROUPS), 0.01),
        'w_router_expert': nrm(ks[17], (DEPTH, N_GROUPS, D_MODEL, EXPERTS_PER_GROUP), D_MODEL ** -0.5),
        'b_router_expert': nrm(ks[18], (DEPTH, N_GROUPS, EXPERTS_PER_GROUP), 0.01),
        'w_gate': nrm(ks[19], (DEPTH, N_GROUPS, EXPERTS_PER_GROUP, D_MODEL, D_EXPERT), D_MODEL ** -0.5),
        'w_up': nrm(ks[20], (DEPTH, N_GROUPS, EXPERTS_PER_GROUP, D_MODEL, D_EXPERT), D_MODEL ** -0.5),
        'w_down': nrm(ks[21], (DEPTH, N_GROUPS, EXPERTS_PER_GROUP, D_EXPERT, D_MODEL), D_EXPERT ** -0.5),
        'ln_f_g': 1.0 + nrm(ks[22], (D_MODEL,), 0.02),
    }

def reference(x_prompt, x_sample, cache_k_a, cache_v_a, cache_kidx_a, cache_k_b, cache_v_b, page_table,
              rel_bias_table, ln1_g, w_in, w_proj_a, w_proj_b, w_out, ln2_g, w_router_group, b_router_group,
              w_router_expert, b_router_expert, w_gate, w_up, w_down, ln_f_g):
    xp, xs = x_prompt, x_sample
    kap, vap, kip, kbp, vbp = [], [], [], [], []
    kas, vas, kis, kbs, vbs = [], [], [], [], []
    for l in range(DEPTH):
        ffn_w = (w_proj_a[l], w_proj_b[l], w_out[l], ln2_g[l], w_router_group[l], b_router_group[l],
                 w_router_expert[l], b_router_expert[l], w_gate[l], w_up[l], w_down[l])
        qa, ka, va, qi, wi, ki, qb, kb, vb, ga, gb = _project(_rmsnorm(xp, ln1_g[l]), w_in[l])
        o_a, o_b = _prompt_mixers(qa, ka, va, qi, wi, ki, qb, kb, vb, rel_bias_table)
        xp = _merge_and_ffn(xp, o_a, o_b, ga, gb, *ffn_w)
        kap.append(ka); vap.append(va); kip.append(ki); kbp.append(kb); vbp.append(vb)
        qa, ka, va, qi, wi, ki, qb, kb, vb, ga, gb = _project(_rmsnorm(xs, ln1_g[l]), w_in[l])
        o_a, o_b = _sample_mixers(qa, ka, va, qi, wi, ki, qb, kb, vb, cache_k_a[l], cache_v_a[l],
                                  cache_kidx_a[l], cache_k_b[l], cache_v_b[l], page_table, rel_bias_table)
        xs = _merge_and_ffn(xs, o_a, o_b, ga, gb, *ffn_w)
        kas.append(ka); vas.append(va); kis.append(ki); kbs.append(kb); vbs.append(vb)
    y_prompt = _rmsnorm(xp, ln_f_g)
    y_sample = _rmsnorm(xs, ln_f_g)
    return (y_prompt, y_sample,
            jnp.stack(kap), jnp.stack(vap), jnp.stack(kip), jnp.stack(kbp), jnp.stack(vbp),
            jnp.stack(kas), jnp.stack(vas), jnp.stack(kis), jnp.stack(kbs), jnp.stack(vbs))


_drawn_inputs = setup_inputs


def setup_inputs(seed=0):
    import zlib

    import numpy as np

    out = dict(_drawn_inputs(seed))
    spreads = {}
    factors = {'b_router_group': 7.074, 'b_router_expert': 3.785, 'ln_f_g': 2.803}
    for name, (base, spread) in spreads.items():
        noise = np.random.default_rng([zlib.crc32(name.encode()), seed]).standard_normal(out[name].shape)
        drawn = base * np.exp(spread * noise) if base else spread * noise
        out[name] = __import__('jax').numpy.asarray(drawn.astype(out[name].dtype))
    for name, factor in factors.items():
        out[name] = (out[name] * factor).astype(out[name].dtype)
    return out
```

```python
from contextlib import ExitStack

import numpy as np

import concourse.bass as bass
from concourse import mybir

F32 = mybir.dt.float32
I32 = mybir.dt.int32
ALU = mybir.AluOpType
ACT = mybir.ActivationFunctionType
AX_X = mybir.AxisListType.X

P = 128
D = 1024
KC = D // P
NP_TOK = 256
NS = 8
T = NP_TOK + NS
TILES = [(0, P), (P, P), (2 * P, NS)]
H = 8
HD = 64
PAST = 2048
PAGE = 128
R = PAST // P
RB = PAGE // R
TOPK_P = NP_TOK // 4
TOPK_S = 256
NB = 32
NE = 32
NG = 4
EG = 8
DE = 256
CAP = 64
NOVF = 2 * T // (CAP + 1)
NOVF += NOVF % 2
PAIR = 2 * CAP
NPAIR = (NE + NOVF) // 2
EPS = 1e-6
NEG = -1e30
GONE = -3e38

O_QA, O_KA, O_VA, O_QI, O_WI, O_KI, O_QB, O_KB, O_GA = 0, 512, 640, 768, 1280, 1288, 1352, 1864, 2888
G0W = O_QB - O_QI
D_IN = 4936


def bucket(dist):
    n = np.maximum(np.asarray(dist), 0)
    nf = np.maximum(n, NB // 2).astype(np.float32)
    big = NB // 2 + (np.log(nf / np.float32(16)) / np.float32(np.log(8.0)) * np.float32(16)).astype(np.int32)
    return np.where(n < NB // 2, n, np.minimum(big, NB - 1))


def shape_constants():
    i = np.arange(P)
    parts = {
        "ident": np.eye(P),
        "after": -(i[:, None] > i[None, :]).astype(float),
        "negones": -np.ones((P, P)),
        "before": (i[:, None] < i[None, :]).astype(float),
        "ones": np.ones((P, P)),
        "strict": np.where(i[:, None] < np.arange(2 * P)[None, :], 0.0, NEG),
        "expand": (np.arange(NS)[:, None] == np.arange(NS * H)[None, :] // H).astype(float),
        "same_h": (np.arange(NS * H)[:, None] % H == np.arange(H)[None, :]).astype(float),
        "same_b": (np.arange(NS * H)[:, None] // H == np.arange(NS)[None, :]).astype(float),
        "segment": np.tile((np.arange(H * R) % R != 0).astype(float), (P, 1)),
        "iota_g": np.tile(np.arange(NG, dtype=float), (P, 3)),
        "iota_8": np.tile(np.arange(EG, dtype=float), (P, 3)),
        "iota_e": np.tile(np.arange(NE, dtype=float), (P, 1)),
        "iota_blk": np.tile(np.repeat(np.arange(NOVF, dtype=float), NE), (1, 1)),
        "iota_e_blk": np.tile(np.arange(NE, dtype=float), (1, NOVF)),
        "row_block": (i % RB).astype(float)[:, None],
        "causal": np.where(np.arange(3 * P)[None, :] - P <= i[:, None], 0.0, NEG),
        "half": np.full((P, 3), -0.5),
        "zeros": np.zeros((P, P)),
        "bucket0": np.concatenate([np.ones((1, NS)), np.zeros((NB - 1, NS))]),
    }
    dist = NP_TOK - 1 - np.arange(2 * NP_TOK)
    hot = (bucket(dist)[None, :] == np.arange(NB)[:, None]) & (dist >= 0)[None, :]
    parts["prompt_buckets"] = np.concatenate([hot.astype(float), np.where(dist < 0, NEG, 0.0)[None, :]])
    at, cols = {}, 0
    for name, a in parts.items():
        at[name] = (cols, a.shape[0], a.shape[1])
        cols += a.shape[1]
    packed = np.zeros((P, cols), np.float32)
    for name, a in parts.items():
        c, r, n = at[name]
        packed[:r, c:c + n] = a
    s = np.arange(P)[None, :] * R + np.arange(R)[:, None]
    sample = (bucket(PAST - s.reshape(-1))[None, :] == np.arange(NB)[:, None]).astype(np.float32)
    ids = (np.arange(3)[None, :] * P + i[:, None]).astype(np.int32)
    return at, packed, sample, ids


def decoder_step(nc, a, out, CONST_AT):
    ctx = ExitStack()
    with ctx:
        def sb(name, shape, dt=F32):
            return ctx.enter_context(nc.sbuf_tensor(name, shape, dt))

        def sem(name):
            return ctx.enter_context(nc.semaphore(name))

        consts = sb("consts", [P, a["shape_consts"].shape[1]])

        def const(name):
            c, r, n = CONST_AT[name]
            return consts[0:r, c:c + n]

        ident = const("ident")
        x_rows = sb("x_rows", [P, 3, D])
        xT = sb("xT", [P, KC, T])
        g1T = sb("g1T", [P, KC])
        rows_kva = sb("rows_kva", [P, 3, 2 * P])
        rows_ki = sb("rows_ki", [P, 3, HD])
        rows_vb = sb("rows_vb", [P, 3, H * HD])
        oaT = sb("oaT", [P, 4, T])
        obT = sb("obT", [P, 4, T])
        wi_rows = sb("wi_rows", [P, 3, H])
        small = sb("small", [P, 64])
        page_idx = sb("page_idx", [P, NS], I32)
        unit_idx = sb("unit_idx", [P, 4, NS], I32)
        page_of = sb("page_of", [P, NS], I32)

        RING = 2 * 4 * 4 * H * HD
        arena = sb("arena", [P, RING + 40 * T])
        k_ring = arena[:, 0:RING // 2].rearrange("p (u r n) -> p u r n", u=4, r=4)
        v_ring = arena[:, RING // 2:RING].rearrange("p (u r n) -> p u r n", u=4, r=4)
        projected = arena[:, RING:RING + 24 * T].rearrange("p (c t) -> p c t", t=T)
        kbT, vbT = projected[:, 0:4, :], projected[:, 4:8, :]
        gates = projected[:, 8:24, :]
        qaT = arena[:, RING + 24 * T:RING + 28 * T].rearrange("p (c t) -> p c t", t=T)
        qiT = arena[:, RING + 28 * T:RING + 32 * T].rearrange("p (c t) -> p c t", t=T)
        qbT = arena[:, RING + 32 * T:RING + 36 * T].rearrange("p (c t) -> p c t", t=T)
        kaT = arena[:, RING + 36 * T:RING + 37 * T]
        vaT = arena[:, RING + 37 * T:RING + 38 * T]
        kiT = arena[:, RING + 38 * T:RING + 39 * T]
        w_a = arena[:, RING // 2:RING // 2 + KC * 512].rearrange("p (k n) -> p k n", k=KC)
        w_b = arena[:, RING // 2 + KC * 512:RING].rearrange("p (k n) -> p k n", k=KC)
        kidx_ring = arena[:, 0:2 * R * HD].rearrange("p (s n) -> p s n", s=2)
        ka_ring = arena[:, 2 * R * HD:2 * R * HD + 2 * R * P].rearrange("p (s n) -> p s n", s=2)

        temp = sb("temp", [P, 12288])
        w_ki = sb("w_ki", [P, KC, H + HD])
        xn_rows = temp[:, 0:3 * D].rearrange("p (t n) -> p t n", t=3)
        sample_buckets = temp[0:NB, 3072:3072 + PAST]
        kT_s = temp[:, 5120:6144].rearrange("p (s n) -> p s n", s=2)
        relu_s = temp[0:64, 0:2048].rearrange("p (j n) -> p j n", j=4)
        score_s = temp[0:NS, 6144:6144 + PAST + 8]
        logit_s = temp[0:64, 0:PAST + 8]
        qiPad = temp[:, 8208:8208 + NS * 64].rearrange("p (b m) -> p b m", b=NS)
        qaPad = temp[:, 8720:8720 + NS * 64].rearrange("p (b m) -> p b m", b=NS)
        qiAll = temp[0:HD, 9232:9296]
        qaAll = temp[:, 9296:9360]
        relu_new = temp[0:64, 9360:9368]
        tmp64 = temp[0:64, 9368:9376]
        wcol = temp[0:64, 9376:9377]
        w_blk = temp[0:64, 9384:9392]
        tmp8 = temp[0:NS, 9392:9400]
        top8 = temp[0:NS, 9400:9408]
        bias_bh = temp[0:NB, 9408:9472]
        rows_kb = temp[:, 9472:9472 + 3 * H * HD].rearrange("p (t n) -> p t n", t=3)
        taken_s = temp[0:NS, 3072:3072 + PAST + 8]
        mx_s, sum_s, inv_s = temp[0:64, 12112:12113], temp[0:64, 12113:12114], temp[0:64, 12114:12115]
        new_p = temp[0:64, 12120:12128]
        pT_s = temp[:, 11008:12032].rearrange("p (r m) -> p r m", r=R)
        new_pT = temp[0:NS, 12032:12096]
        relu_p = temp[:, 0:2048].rearrange("p (h s) -> p h s", h=H)
        prob_p = temp[:, 2056:4104].rearrange("p (h s) -> p h s", h=H)
        bias_p = temp[:, 5128:8200].rearrange("p (h j) -> p h j", h=H)
        pT_p = temp[:, 8200:9224].rearrange("p (s n) -> p s n", s=2)
        score_p = temp[:, 4104:4360]
        kept_p = temp[:, 4360:4616]
        o_rows = temp[:, 4616:5128]
        stat_p = sb("stat_p", [P, 64])
        mx_p, sum_p, inv_p, top_p = stat_p[:, 0:8], stat_p[:, 8:16], stat_p[:, 16:24], stat_p[:, 24:32]
        wi_scaled = stat_p[:, 32:48].rearrange("p (t h) -> p t h", t=2)
        kaSwap = arena[:, RING + 39 * T:RING + 40 * T]
        table33 = sb("table33", [NB + 1, H])
        bias_row = sb("bias_row", [H, 2 * NP_TOK])
        bias_dram = nc.dram_tensor("bias_dram", [H * P * 2 * NP_TOK], F32).ap()
        z_p = temp[:, 0:1536]
        e_p = temp[:, 1536:3072]
        q_row = temp[0:NS, 8200:8712]
        q_all = temp[:, 3072:7168].rearrange("p (b n) -> p b n", b=NS)
        z_s, e_s, incl_s, a_s = (temp[:, 7168 + k * H * R:7168 + (k + 1) * H * R] for k in range(4))
        later_s = temp[:, 7680:7688]
        w_pa = arena[:, RING // 2:RING // 2 + 4 * D].rearrange("p (k n) -> p k n", k=4)
        w_pb = arena[:, RING // 2 + 4 * D:RING].rearrange("p (k n) -> p k n", k=4)
        w_o = temp[:, 0:KC * D].rearrange("p (k n) -> p k n", k=KC)
        hT_s = temp[:, 9216:9280].rearrange("p (c n) -> p c n", c=KC)
        mixT = xT
        junk_rows = temp[:, 8192:9216]
        late = arena[:, RING + 32 * T:RING + 40 * T]
        part = late[:, 0:2 * T].rearrange("p (k t) -> p k t", k=2)
        g2_all, gf_all = temp[:, 10240:11264], temp[:, 11264:12288]
        x2_rows = temp[:, 0:3 * D].rearrange("p (t n) -> p t n", t=3)
        w_r = late[:, 528:816].rearrange("p (k e) -> p k e", k=KC)
        b_r = late[:, 816:852]
        rt = late[:, 856:856 + 1152]
        at = [0]

        def piece(n):
            at[0] += n
            return rt[:, at[0] - n:at[0]]

        lg = piece(3 * (NG + NE)).rearrange("p (t n) -> p t n", t=3)
        one_g, eq_g, exp_g = (piece(3 * NG).rearrange("p (t n) -> p t n", t=3) for _ in range(3))
        le, one_1, one_2, eq_e = (piece(3 * EG).rearrange("p (t n) -> p t n", t=3) for _ in range(4))
        mask_1, mask_2, mask_12, ROW = (piece(3 * NE).rearrange("p (t n) -> p t n", t=3) for _ in range(4))
        top_g, top_1, top_2, g_w, e_2, wt_1, wt_2 = (piece(3) for _ in range(7))
        extra, upto, before_e, base_e = (piece(NE) for _ in range(4))
        row_f = piece(6).rearrange("p (k t) -> p k t", k=2)
        blk = rt[0:1, 1152 - NOVF:1152]
        row_i, low_i, high_i, addr_i = (sb(n, [P, 2, 3], I32) for n in ("row_i", "low_i", "high_i", "addr_i"))
        tok_i = sb("tok_i", [P, 3], I32)
        slot_tok = sb("slot_tok", [PAIR, NPAIR], I32)
        zero_i = sb("zero_i", [PAIR, NPAIR], I32)
        ovf_i = sb("ovf_i", [1, NOVF + 1], I32)
        blk_tmp = bias_row[0:1, 0:2 * NOVF * NE]
        SLOT = 3 * 8 * DE
        slots = [arena[:, k * SLOT:(k + 1) * SLOT] for k in range(4)]
        xg = [temp[:, 3072 + k * D:3072 + (k + 1) * D] for k in range(2)]
        xgT = [temp[:, 5120 + k * D:5120 + (k + 1) * D].rearrange("p (c n) -> p c n", c=KC) for k in range(2)]
        y_sb = [temp[:, 7168 + k * D:7168 + (k + 1) * D] for k in range(2)]
        act_e = w_ki[:, 0:8, :].rearrange("p k n -> p (k n)")[:, 0:4 * CAP].rearrange("p (k n) -> p k n", k=2)
        hid = w_ki[:, 0:8, :].rearrange("p k n -> p (k n)")[:, 4 * CAP:8 * CAP].rearrange("p (k n) -> p k n", k=2)
        y_1 = arena[:, 0:3 * D].rearrange("p (t n) -> p t n", t=3)
        y_2 = arena[:, 3 * D:6 * D].rearrange("p (t n) -> p t n", t=3)
        x2_dram = nc.dram_tensor("x2_dram", [T, D], F32).ap()
        table_dram = nc.dram_tensor("table_dram", [PAIR * NPAIR, 1], I32).ap()
        y_dram = nc.dram_tensor("y_dram", [PAIR * NPAIR, D], F32).ap()
        ssq, ms, rstd = small[:, 0:3], small[:, 3:6], small[:, 6:9]

        PS = ctx.enter_context(nc.psum_tensor("PS", [P, 8, 512], F32))
        ACC = 4

        s_const, s_x, s_g1, s_tab = sem("s_const"), sem("s_x"), sem("s_g1"), sem("s_tab")
        s_wki, s_wa, s_wb = sem("s_wki"), sem("s_wa"), sem("s_wb")
        s_kidx = [sem(f"s_kidx{i}") for i in range(2)]
        s_ka = [sem(f"s_ka{i}") for i in range(2)]
        s_page, s_idx = sem("s_page"), sem("s_idx")
        s_prep, s_ssq, s_ms, s_rstd, s_xn = sem("s_prep"), sem("s_ssq"), sem("s_ms"), sem("s_rstd"), sem("s_xn")
        s_xtr, s_xT = sem("s_xtr"), sem("s_xT")
        s_proj, s_evac = sem("s_proj"), sem("s_evac")
        s_tr, s_trf = sem("s_tr"), sem("s_trf")
        s_wexp, s_wcol, s_qipad, s_qapad = sem("s_wexp"), sem("s_wcol"), sem("s_qipad"), sem("s_qapad")
        s_kT_used = sem("s_kT_used")
        s_relc, s_sc, s_scc = sem("s_relc"), sem("s_sc"), sem("s_scc")
        s_lg, s_lgc, s_top = sem("s_lg"), sem("s_lgc"), sem("s_top")
        s_chain = sem("s_chain")
        s_rows, s_rowsT, s_out = sem("s_rows"), sem("s_rowsT"), sem("s_out")

        s_tab33, s_ones33, s_brow, s_browc, s_bdram, s_biasp = (sem(n) for n in (
            "s_tab33", "s_ones33", "s_brow", "s_browc", "s_bdram", "s_biasp"))
        s_taken, s_nm, s_mx, s_exp_s, s_prob_s = (sem(n) for n in (
            "s_taken", "s_nm", "s_mx", "s_exp_s", "s_prob_s"))
        s_swap, s_ip, s_ipr, s_sp, s_lp, s_lpb, s_mxp, s_ep, s_avp, s_onorm, s_oaT = (sem(n) for n in (
            "s_swap", "s_ip", "s_ipr", "s_sp", "s_lp", "s_lpb", "s_mxp", "s_ep", "s_avp", "s_onorm", "s_oaT"))
        s_pT_used = sem("s_pT_used")
        s_zp, s_zpc, s_lnp, s_spp, s_aft, s_tp, s_ap, s_obp, s_obT = (sem(n) for n in (
            "s_zp", "s_zpc", "s_lnp", "s_spp", "s_aft", "s_tp", "s_ap", "s_obp", "s_obT"))

        s_k = [sem(f"s_k{u}") for u in range(4)]
        s_v = [sem(f"s_v{u}") for u in range(4)]
        s_va = [sem(f"s_va{u}") for u in range(4)]
        s_qall, s_qallc, s_mul, s_kused, s_ls, s_sps, s_scan, s_tot, s_ts, s_as, s_vused, s_obs = (sem(n) for n in (
            "s_qall", "s_qallc", "s_mul", "s_kused", "s_ls", "s_sps", "s_scan", "s_tot", "s_ts", "s_as", "s_vused",
            "s_obs"))
        s_vaused, s_oas = sem("s_vaused"), sem("s_oas")

        s_wp, s_wo, s_gains, s_wr, s_gexp, s_gp1, s_gate, s_pab, s_mixa, s_mix = (sem(n) for n in (
            "s_wp", "s_wo", "s_gains", "s_wr", "s_gexp", "s_gp1", "s_gate", "s_pab", "s_mixa", "s_mix"))
        s_h, s_hs, s_hsc, s_hst, s_hadd = (sem(n) for n in ("s_h", "s_hs", "s_hsc", "s_hst", "s_hadd"))
        s_ssq2, s_ms2, s_rstd2, s_x2, s_x2d, s_x2tr, s_x2T = (sem(n) for n in (
            "s_ssq2", "s_ms2", "s_rstd2", "s_x2", "s_x2d", "s_x2tr", "s_x2T"))
        s_rl, s_rd, s_re, s_rank, s_rowi, s_tokz, s_zero, s_tokid, s_scat, s_slot, s_ovf = (sem(n) for n in (
            "s_rl", "s_rd", "s_re", "s_rank", "s_rowi", "s_tokz", "s_zero", "s_tokid", "s_scat", "s_slot", "s_ovf"))
        s_we = [sem(f"s_we{k}") for k in range(4)]
        s_xg = [sem(f"s_xg{k}") for k in range(2)]
        s_yout = [sem(f"s_yout{k}") for k in range(2)]
        s_gtr, s_gT, s_gu, s_gexp2, s_act, s_hid, s_down, s_ycopy = (sem(n) for n in (
            "s_gtr", "s_gT", "s_gu", "s_gexp2", "s_act", "s_hid", "s_down", "s_ycopy"))
        s_y0 = sem("s_y0")
        s_y12, s_fin, s_ssq3, s_ms3, s_rstd3, s_yo, s_done = (sem(n) for n in (
            "s_y12", "s_fin", "s_ssq3", "s_ms3", "s_rstd3", "s_yo", "s_done"))

        w_in = a["w_in"][0].rearrange("(k p) n -> p k n", p=P)
        we_gate = a["w_gate"].rearrange("o g e d f -> (o g e) d f")
        we_up = a["w_up"].rearrange("o g e d f -> (o g e) d f")
        we_down = a["w_down"].rearrange("o g e f d -> (o g e) f d")
        kidx_rows = a["cache_kidx_a"][0].rearrange("n (q r) d -> (n q) (r d)", r=R)
        ka_rows = a["cache_k_a"][0].rearrange("n (q r) h d -> (n q) (r h d)", r=R)
        va_rows = a["cache_v_a"][0].rearrange("n (q r) h d -> (n q) (r h d)", r=R)
        kb_rows = a["cache_k_b"][0].rearrange("n (q r) h d -> (n q) (r h d)", r=4)
        vb_rows = a["cache_v_b"][0].rearrange("n (q r) h d -> (n q) (r h d)", r=4)

        M_KIDX = 1
        M_KA = M_KIDX + 2 * NS + 2
        M_ROWS = M_KA + 4 * NS + 1
        M_SOFT = M_ROWS + 12
        M_PR = M_SOFT + 3
        M_QROW = M_PR + 10
        M_MERGE = M_QROW + 1
        NLOOP = 3
        N_PEEL = 15
        block = ctx.enter_context(nc.Block())

        @block.sync
        def _(sp):
            sp.dma_start(x_rows[:, 0:2, :], a["x_prompt"][0].rearrange("(t p) d -> p t d", p=P)).then_inc(s_x, 16)
            sp.dma_start(x_rows[0:NS, 2, :], a["x_sample"].rearrange("b o d -> (b o) d")).then_inc(s_x, 16)
            sp.dma_start(page_of[:, :], a["pages"]).then_inc(s_page, 16)
            sp.dma_start(consts[:, :], a["shape_consts"]).then_inc(s_const, 16)
            sp.dma_start(w_a[:, :, :], w_in[:, :, O_QI:O_QI + 512]).then_inc(s_wa, 16)
            sp.dma_start(w_ki[:, :, :], w_in[:, :, O_WI:O_QB]).then_inc(s_wki, 16)
            sp.dma_start(w_b[:, :, :], w_in[:, :, O_QA:O_QA + 512]).then_inc(s_wb, 16)
            for b in range(NS):
                sp.dma_start(bias_bh[:, b * H:(b + 1) * H], a["rel_bias_table"]).then_inc(s_tab, 16)
            sp.dma_start(sample_buckets, a["sample_buckets"]).then_inc(s_tab, 16)
            sp.dma_start(table33[0:NB, :], a["rel_bias_table"]).then_inc(s_tab33, 16)
            sp.wait_ge(s_const, 16)
            sp.dma_start(y_dram[NE * CAP:PAIR * NPAIR, :].rearrange("(p j) (k n) -> p (j k) n", p=P, n=P),
                         const("zeros").unsqueeze(1).to_broadcast([P, NOVF * CAP * D // P // P, P])).then_inc(s_y0, 16)
            sp.wait_ge(s_proj, 4)
            sp.dma_start(w_a[:, :, 0:256], w_in[:, :, O_KA:O_KA + 256]).then_inc(s_wa, 16)
            sp.wait_ge(s_proj, 9)
            sp.dma_start(w_b[:, :, :], w_in[:, :, O_QB:O_QB + 512]).then_inc(s_wb, 16)
            with sp.Fori(0, NLOOP) as i:
                sp.wait_ge(s_proj, i * 8 + 11)
                sp.dma_start(w_a[:, :, :], w_in[:, :, bass.ds(i * 1024 + O_KB, 512)]).then_inc(s_wa, 16)
                sp.wait_ge(s_proj, i * 8 + 15)
                sp.dma_start(w_b[:, :, :], w_in[:, :, bass.ds(i * 1024 + O_KB + 512, 512)]).then_inc(s_wb, 16)
            row = 2 * NP_TOK
            sp.wait_ge(s_browc, 1)
            sp.dma_start(bias_dram.rearrange("(h p j) -> h p j", h=H, p=P),
                         bias_row[:, :].unsqueeze(1).to_broadcast([H, P, row])).then_inc(s_bdram, 16)
            sp.wait_ge(s_bdram, 16)
            sp.wait_ge(s_prob_s, 1)
            for par in range(2):
                src = bass.AP(bias_dram.tensor, par * P * row + P - 1, [[row - 1, P], [2 * P * row, 4], [1, 3 * P]])
                sp.dma_start(bias_p[:, par * 4:par * 4 + 4, :], src).then_inc(s_biasp, 16)

            sp.dma_start(tok_i[:, :], a["token_ids"]).then_inc(s_tokid, 16)
            sp.wait_ge(s_zero, 1)
            sp.dma_start(table_dram.rearrange("(p t) o -> p (t o)", p=PAIR), zero_i[:, :]).then_inc(s_tokz, 16)

            def expert(e, k):
                gate = slots[k][:, 0:8 * DE].rearrange("p (c f) -> p c f", c=KC)
                up = slots[k][:, 8 * DE:16 * DE].rearrange("p (c f) -> p c f", c=KC)
                down = slots[k][:, 16 * DE:24 * DE].rearrange("p (c d) -> p c d", c=2)
                sp.dma_start(gate, we_gate[e].rearrange("o (p c) f -> (o p) c f", p=P)).then_inc(s_we[k], 16)
                sp.dma_start(up, we_up[e].rearrange("o (p c) f -> (o p) c f", p=P)).then_inc(s_we[k], 16)
                sp.dma_start(down, we_down[e].rearrange("o (c p) d -> (o p) c d", p=P)).then_inc(s_we[k], 16)

            sp.wait_ge(s_vused, 4 * NS)
            sp.dma_start(w_pa, a["w_proj_a"][0].rearrange("(k p) n -> p k n", p=P)).then_inc(s_wp, 16)
            sp.dma_start(w_pb, a["w_proj_b"][0].rearrange("(k p) n -> p k n", p=P)).then_inc(s_wp, 16)
            sp.wait_ge(s_as, NS)
            for g in range(NG):
                sp.dma_start(w_r[:, :, NG + g * EG:NG + (g + 1) * EG],
                             a["w_router_expert"][0, g].rearrange("(k p) e -> p k e", p=P)).then_inc(s_wr, 16)
            sp.dma_start(w_r[:, :, 0:NG], a["w_router_group"][0].rearrange("(k p) g -> p k g", p=P)).then_inc(s_wr, 16)
            sp.dma_start(b_r[:, 0:NG], a["b_router_group"].to_broadcast([P, NG])).then_inc(s_wr, 16)
            sp.dma_start(b_r[:, NG:NG + NE], a["b_router_expert"].rearrange("o g e -> o (g e)").to_broadcast([P, NE])
                         ).then_inc(s_wr, 16)
            sp.dma_start(w_o, a["w_out"][0].rearrange("(k p) n -> p k n", p=P)).then_inc(s_wo, 16)
            sp.wait_ge(s_oas, 4)
            sp.wait_ge(s_out, 160)
            sp.dma_start(g2_all, a["ln2_g"].to_broadcast([P, D])).then_inc(s_gains, 16)
            sp.dma_start(gf_all, a["ln_f_g"].unsqueeze(0).to_broadcast([P, D])).then_inc(s_gains, 16)
            expert(slice(0, 1), 0)
            sp.wait_ge(s_pab, 2 * KC)
            expert(slice(1, 2), 1)
            sp.wait_ge(s_mix, KC)
            expert(slice(2, 3), 2)
            expert(slice(3, 4), 3)
            with sp.Fori(1, NE // 4) as i:
                for k in range(4):
                    sp.wait_ge(s_down, i * 4 + (k - 3))
                    expert(bass.ds(i * 4 + k, 1), k)
            sp.wait_ge(s_ovf, 2)
            n_extra = sp.value_load(ovf_i[0:1, 0:1], min_val=0, max_val=NOVF)
            with sp.If(n_extra > 0):
                for j in range(NOVF):
                    sp.wait_ge(s_down, NE + j - 3)
                    e = sp.value_load(ovf_i[0:1, 1 + j:2 + j], min_val=0, max_val=NE - 1)
                    expert(bass.ds(e, 1), j % 4)

        @block.gpsimd
        def _(pool):
            def fetch(dst, src, idx, landed):
                pool.indirect_dma_start(out=dst, out_offset=None, in_=src,
                                        in_offset=bass.IndirectOffsetOnAxis(ap=idx, axis=0)).then_inc(landed, 16)

            pool.wait_ge(s_idx, 1)
            for b in range(2):
                fetch(kidx_ring[:, b, :], kidx_rows, page_idx[:, b:b + 1], s_kidx[b])
            pool.wait_ge(s_ms, 1)
            nc.gpsimd.tensor_tensor(rstd, ms, const("half"), ALU.pow).then_inc(s_rstd, 1)
            for b in range(2):
                fetch(ka_ring[:, b, :], ka_rows, page_idx[:, b:b + 1], s_ka[b])
            for b in range(2, NS):
                pool.wait_ge(s_tr, M_KIDX + 2 * (b - 1))
                fetch(kidx_ring[:, b % 2, :], kidx_rows, page_idx[:, b:b + 1], s_kidx[b % 2])
            for b in range(2, NS):
                pool.wait_ge(s_tr, M_KA + 4 * (b - 1))
                fetch(ka_ring[:, b % 2, :], ka_rows, page_idx[:, b:b + 1], s_ka[b % 2])

            pool.wait_ge(s_tr, M_KA + 4 * NS)
            for b in range(NS):
                for u in range(4):
                    if b:
                        pool.wait_ge(s_kused, 4 * (b - 1) + u + 1)
                    fetch(k_ring[:, u].rearrange("p r n -> p (r n)"), kb_rows, unit_idx[:, u, b:b + 1], s_k[u])
                if b == 0:
                    pool.wait_ge(s_proj, N_PEEL + 8 * NLOOP)
                for u in range(4):
                    if b:
                        pool.wait_ge(s_vused, 4 * (b - 1) + u + 1)
                    fetch(v_ring[:, u].rearrange("p r n -> p (r n)"), vb_rows, unit_idx[:, u, b:b + 1], s_v[u])
            for b in range(NS):
                if b < 4:
                    pool.wait_ge(s_kused, 4 * (NS - 1) + b + 1)
                else:
                    pool.wait_ge(s_vaused, b - 3)
                fetch(k_ring[:, b % 4].rearrange("p r n -> p (r n)"), va_rows, page_idx[:, b:b + 1], s_va[b % 4])

            nc.gpsimd.memset(zero_i[:, :], 0).then_inc(s_zero, 1)
            pool.wait_ge(s_ms2, 1)
            nc.gpsimd.tensor_tensor(rstd, ms, const("half"), ALU.pow).then_inc(s_rstd2, 1)
            pool.wait_ge(s_tokz, 16)
            pool.wait_ge(s_tokid, 16)
            pool.wait_ge(s_rowi, 1)
            for k in range(2):
                for t, (_, n) in enumerate(TILES):
                    pool.indirect_dma_start(out=table_dram,
                                            out_offset=bass.IndirectOffsetOnAxis(ap=addr_i[0:n, k, t:t + 1], axis=0),
                                            in_=tok_i[0:n, t:t + 1], in_offset=None).then_inc(s_scat, 16)
            pool.wait_ge(s_scat, 96)
            pool.dma_start(slot_tok[:, :], table_dram.rearrange("(p t) o -> p (t o)", p=PAIR)).then_inc(s_slot, 16)
            pool.wait_ge(s_slot, 16)
            pool.wait_ge(s_x2d, 48)

            def gather(t):
                if t >= 2:
                    pool.wait_ge(s_gtr, t - 1)
                fetch(xg[t % 2][0:PAIR, :], x2_dram, slot_tok[:, t:t + 1], s_xg[t % 2])

            for t in range(NE // 2):
                gather(t)
            pool.wait_ge(s_ovf, 2)
            n_extra = pool.value_load(ovf_i[0:1, 0:1], min_val=0, max_val=NOVF)
            with pool.If(n_extra > 0):
                for t in range(NE // 2, NPAIR):
                    gather(t)
                for k in range(2):
                    pool.wait_ge(s_yout[k], 16 * (NPAIR // 2 + (NPAIR % 2) * (1 - k)))
            for k in range(2):
                pool.wait_ge(s_yout[k], 16 * (NE // 4))
            for k, y in enumerate((y_1, y_2)):
                for t, (_, n) in enumerate(TILES):
                    fetch(y[0:n, t, :], y_dram, row_i[0:n, k, t:t + 1], s_y12)
            pool.wait_ge(s_ms3, 1)
            nc.gpsimd.tensor_tensor(rstd, ms, const("half"), ALU.pow).then_inc(s_rstd3, 1)

        @block.tensor
        def _(pe):
            def chunk(w, c0, bank, m=P):
                for k in range(KC):
                    last = nc.tensor.matmul(PS[0:m, bank, 0:T], w[:, k, c0:c0 + m], xT[:, k, :],
                                            start=(k == 0), stop=(k == KC - 1))
                return last

            pe.wait_ge(s_const, 16)
            for g in range(4):
                t, half = g // 2, g % 2
                pe.wait_ge(s_xn, t + 1)
                if g >= 2:
                    pe.wait_ge(s_xT, g - 1)
                for c in range(4):
                    d0 = (half * 4 + c) * P
                    last = nc.tensor.transpose(PS[:, 2 + g % 2, c * P:(c + 1) * P], xn_rows[:, t, d0:d0 + P], ident)
                last.then_inc(s_xtr, 1)
            pe.wait_ge(s_xn, 3)
            pe.wait_ge(s_xT, 3)
            for c in range(KC):
                last = nc.tensor.transpose(PS[:, 2, c * NS:(c + 1) * NS],
                                           xn_rows[0:NS, 2, c * P:(c + 1) * P], ident[0:NS, 0:NS])
            last.then_inc(s_xtr, 1)

            pe.wait_ge(s_xT, 5)
            pe.wait_ge(s_wa, 16)
            for n in range(4):
                if n >= 2:
                    pe.wait_ge(s_evac, n - 1)
                chunk(w_a, n * P, n % 2).then_inc(s_proj, 1)
            pe.wait_ge(s_wki, 16)
            pe.wait_ge(s_evac, 3)
            chunk(w_ki, H, 0, HD).then_inc(s_proj, 1)
            for t, (t0, n) in enumerate(TILES):
                for k in range(KC):
                    last = nc.tensor.matmul(PS[0:n, 2, t * H:(t + 1) * H], xT[:, k, t0:t0 + n], w_ki[:, k, 0:H],
                                            start=(k == 0), stop=(k == KC - 1))
            last.then_inc(s_tr, 1)
            pe.wait_ge(s_trf, 1)
            nc.tensor.matmul(PS[0:64, ACC, 0:H], const("expand"), wi_rows[0:NS, 2, :], start=True, stop=True
                             ).then_inc(s_wexp, 1)

            def group(w, n0, count):
                for c in range(count):
                    n = n0 + c
                    pe.wait_ge(s_evac, n - 1)
                    chunk(w, c * P, n % 2).then_inc(s_proj, 1)

            pe.wait_ge(s_wb, 16)
            group(w_b, 5, 4)
            pe.wait_ge(s_wa, 32)
            group(w_a, 9, 2)

            pe.wait_ge(s_qipad, 1)
            pe.wait_ge(s_wcol, 1)
            for b in range(NS):
                pe.wait_ge(s_kidx[b % 2], 16 * (b // 2 + 1))
                for half in range(2):
                    m = M_KIDX + 2 * b + half
                    if m >= 2:
                        pe.wait_ge(s_trf, m - 1)
                    for q in range(4):
                        c = (half * 4 + q) * P
                        last = nc.tensor.transpose(PS[:, 2 + m % 2, q * P:(q + 1) * P],
                                                   kidx_ring[:, b % 2, c:c + P], ident)
                    last.then_inc(s_tr, 1)
                for half in range(2):
                    m = M_KIDX + 2 * b + half
                    pe.wait_ge(s_trf, m + 1)
                    for e in range(2):
                        last = nc.tensor.matmul(PS[0:64, ACC + half * 2 + e, :], qiPad[e * HD:(e + 1) * HD, b, :],
                                                kT_s[e * HD:(e + 1) * HD, m % 2, :],
                                                start=(b == 0), stop=(b == NS - 1))
                    last.then_inc(s_kT_used, 1)
            m = M_KIDX + 2 * NS
            pe.wait_ge(s_trf, m - 1)
            nc.tensor.matmul(PS[0:64, 2 + m % 2, 0:NS], qiAll, kiT[0:HD, NP_TOK:T], start=True, stop=True
                             ).then_inc(s_tr, 1)
            m += 1
            for j in range(4):
                pe.wait_ge(s_relc, j + 1)
                nc.tensor.matmul(PS[0:NS, ACC + j, :], w_blk, relu_s[:, j, :], start=True, stop=True
                                 ).then_inc(s_sc, 1)
            pe.wait_ge(s_trf, m)
            nc.tensor.matmul(PS[0:NS, 2 + m % 2, 0:NS], w_blk, relu_new, start=True, stop=True).then_inc(s_tr, 1)

            pe.wait_ge(s_qapad, 1)
            pe.wait_ge(s_tab, 16 * (NS + 1))
            pe.wait_ge(s_scc, 4)
            for j in range(4):
                nc.tensor.matmul(PS[0:64, ACC + j, :], bias_bh, sample_buckets[:, j * 512:(j + 1) * 512],
                                 start=True, stop=False)

            def turn_ka(b, j):
                m = M_KA + 4 * b + j
                pe.wait_ge(s_trf, m - 1)
                for r in range(4):
                    c = (j * 4 + r) * P
                    last = nc.tensor.transpose(PS[:, 2 + m % 2, r * P:(r + 1) * P], ka_ring[:, b % 2, c:c + P], ident)
                last.then_inc(s_tr, 1)

            for b in range(NS):
                pe.wait_ge(s_ka[b % 2], 16 * (b // 2 + 1))
                turn_ka(b, 0)
                for j in range(4):
                    if j < 3:
                        turn_ka(b, j + 1)
                    m = M_KA + 4 * b + j
                    pe.wait_ge(s_trf, m + 1)
                    nc.tensor.matmul(PS[0:64, ACC + j, :], qaPad[:, b, :], kT_s[:, m % 2, :],
                                     start=False, stop=(b == NS - 1)).then_inc(s_kT_used, 1)
            m = M_KA + 4 * NS
            pe.wait_ge(s_trf, m - 1)
            nc.tensor.matmul(PS[0:64, 2 + m % 2, 0:NS], bias_bh, const("bucket0"), start=True, stop=False)
            nc.tensor.matmul(PS[0:64, 2 + m % 2, 0:NS], qaAll, kaT[:, NP_TOK:T], start=False, stop=True
                             ).then_inc(s_tr, 1)

            pe.wait_ge(s_wb, 32)
            group(w_b, 11, 4)
            with pe.Fori(0, NLOOP) as i:
                for w, s_w, half in ((w_a, s_wa, 0), (w_b, s_wb, 1)):
                    pe.wait_ge(s_w, i * 16 + 48)
                    for c in range(4):
                        n = N_PEEL + 4 * half + c
                        pe.wait_ge(s_evac, i * 8 + (n - 1))
                        chunk(w, c * P, n % 2).then_inc(s_proj, 1)

            m = M_ROWS
            pe.wait_ge(s_evac, N_PEEL + 8)
            for srcs in ([kaT, vaT], [kbT[:, c, :] for c in range(4)], [vbT[:, c, :] for c in range(4)], [kiT]):
                rows = HD if srcs[0] is kiT else P
                for t0, n in TILES:
                    pe.wait_ge(s_trf, m - 1)
                    for c, src in enumerate(srcs):
                        last = nc.tensor.transpose(PS[0:n, 2 + m % 2, c * P:c * P + rows], src[0:rows, t0:t0 + n],
                                                   ident[0:rows, 0:rows])
                    last.then_inc(s_tr, 1)
                    m += 1

            pe.wait_ge(s_tab33, 16)
            pe.wait_ge(s_ones33, 1)
            nc.tensor.matmul(PS[0:H, 0, :], table33[:, :], const("prompt_buckets"), start=True, stop=True
                             ).then_inc(s_brow, 1)

            pe.wait_ge(s_taken, 1)
            pe.wait_ge(s_lgc, 4)
            for j in range(4):
                nc.tensor.matmul(PS[0:64, ACC + j, :], const("expand"), taken_s[:, j * 512:(j + 1) * 512],
                                 start=True, stop=True).then_inc(s_nm, 1)
            pe.wait_ge(s_browc, 1)
            nc.tensor.matmul(PS[0:64, 0, 0:2], const("expand"), taken_s[:, PAST:PAST + 2], start=True, stop=True
                             ).then_inc(s_nm, 1)
            pe.wait_ge(s_prob_s, 1)
            for g in range(2):
                m = M_SOFT + g
                pe.wait_ge(s_trf, m - 1)
                for r in range(8):
                    c = (g * 8 + r) * P
                    last = nc.tensor.transpose(PS[:, 2 + m % 2, r * 64:(r + 1) * 64], logit_s[:, c:c + P],
                                               ident[0:64, 0:64])
                last.then_inc(s_tr, 1)
            m = M_SOFT + 2
            pe.wait_ge(s_trf, m - 1)
            nc.tensor.transpose(PS[0:NS, 2 + m % 2, 0:64], new_p, ident[0:64, 0:64]).then_inc(s_tr, 1)

            pe.wait_ge(s_swap, 1)
            for i in range(2):
                q0 = i * P
                pe.wait_ge(s_mx, 1)
                if i:
                    pe.wait_ge(s_lpb, 4)
                for ho in range(H):
                    par, c = ho // 4, ho % 4
                    half = slice(par * HD, (par + 1) * HD)
                    last = nc.tensor.matmul(PS[:, ACC + ho // 2, ho % 2 * 256:(ho % 2 + 1) * 256],
                                            qiT[half, c, q0:q0 + P], kiT[half, 0:NP_TOK], start=True, stop=True)
                    if ho % 2:
                        last.then_inc(s_ip, 1)
                for ho in range(H):
                    par, c = ho // 4, ho % 4
                    half = slice(par * HD, (par + 1) * HD)
                    keys = kaT if c // 2 == par else kaSwap
                    if ho % 2 == 0:
                        pe.wait_ge(s_ipr, i * 4 + ho // 2 + 1)
                    last = nc.tensor.matmul(PS[:, ACC + ho // 2, ho % 2 * 256:(ho % 2 + 1) * 256],
                                            qaT[half, c, q0:q0 + P], keys[half, 0:NP_TOK], start=True, stop=True)
                    if ho % 2:
                        last.then_inc(s_lp, 1)

                def turn_p(g):
                    m = M_PR + 5 * i + g
                    pe.wait_ge(s_trf, m - 1)
                    pe.wait_ge(s_ep, i * H + 2 * g + 2)
                    for k in range(4):
                        last = nc.tensor.transpose(PS[:, 2 + m % 2, k * P:(k + 1) * P],
                                                   prob_p[:, 2 * g + k // 2, k % 2 * P:(k % 2 + 1) * P], ident)
                    last.then_inc(s_tr, 1)

                turn_p(0)
                if i:
                    pe.wait_ge(s_onorm, 1)
                for g in range(4):
                    if g < 3:
                        turn_p(g + 1)
                    m = M_PR + 5 * i + g
                    pe.wait_ge(s_trf, m + 1)
                    for k in range(4):
                        ho, chunk_s = 2 * g + k // 2, k % 2
                        h = 2 * (ho % 4) + ho // 4
                        last = nc.tensor.matmul(PS[:, 1, h * HD:(h + 1) * HD], pT_p[:, m % 2, k * P:(k + 1) * P],
                                                rows_kva[:, chunk_s, P + h // 4 * HD:P + h // 4 * HD + HD],
                                                start=(chunk_s == 0), stop=(chunk_s == 1))
                    last.then_inc(s_pT_used, 1)
                m = M_PR + 5 * i + 4
                pe.wait_ge(s_onorm, i + 1)
                pe.wait_ge(s_trf, m - 1)
                for c in range(4):
                    last = nc.tensor.transpose(PS[:, 2 + m % 2, c * P:(c + 1) * P], o_rows[:, c * P:(c + 1) * P], ident)
                last.then_inc(s_tr, 1)

            for par in range(2):
                half = slice(par * HD, (par + 1) * HD)
                pe.wait_ge(s_lpb, 8)
                if par:
                    pe.wait_ge(s_tp, 1)
                for c in range(4):
                    nc.tensor.matmul(PS[:, ACC + c // 2, c % 2 * 256:(c % 2 + 1) * 256], kbT[half, c, 0:P],
                                     qbT[half, c, 0:NP_TOK], start=True, stop=True)
                for c in range(4):
                    last = nc.tensor.matmul(PS[:, ACC + 2, c * P:(c + 1) * P], kbT[half, c, P:2 * P],
                                            qbT[half, c, P:2 * P], start=True, stop=True)
                last.then_inc(s_zp, 1)
                pe.wait_ge(s_spp, par + 1)
                late = e_p[:, 1024:1536].rearrange("p (c q) -> p c q", c=4)
                for k in range(2):
                    bank = PS[:, ACC + k, :]
                    nc.tensor.matmul(bank, const("after"), e_p[:, k * 512:(k + 1) * 512], start=True, stop=False)
                    nc.tensor.matmul(bank.rearrange("p (c q) -> p c q", c=2)[:, :, P:2 * P], const("negones"),
                                     late[:, 2 * k:2 * k + 2, :], start=False, stop=True)
                nc.tensor.matmul(PS[:, ACC + 2, :], const("after"), e_p[:, 1024:1536], start=True, stop=True
                                 ).then_inc(s_aft, 1)
                pe.wait_ge(s_ap, par + 1)
                pe.wait_ge(s_onorm, 2)
                if par:
                    pe.wait_ge(s_obT, 1)
                for c in range(4):
                    h = 2 * c + par
                    o = PS[half, c // 2, c % 2 * 256:(c % 2 + 1) * 256]
                    nc.tensor.matmul(o, rows_vb[:, 0, h * HD:(h + 1) * HD], z_p[:, c * 256:(c + 1) * 256],
                                     start=True, stop=False)
                    last = nc.tensor.matmul(o[:, P:2 * P], rows_vb[:, 1, h * HD:(h + 1) * HD],
                                            z_p[:, 1024 + c * P:1024 + (c + 1) * P], start=False, stop=True)
                last.then_inc(s_obp, 1)

            m = M_QROW
            pe.wait_ge(s_trf, m - 1)
            for c in range(4):
                last = nc.tensor.transpose(PS[0:NS, 2 + m % 2, c * P:(c + 1) * P], qbT[:, c, NP_TOK:T], ident)
            last.then_inc(s_tr, 1)
            pe.wait_ge(s_trf, m + 1)
            pe.wait_ge(s_obT, 2)
            for b in range(NS):
                if b >= 2:
                    pe.wait_ge(s_qallc, b - 1)
                nc.tensor.matmul(PS[:, b % 2, :], ident[0:NS, b:b + 1].to_broadcast([NS, P]), q_row,
                                 start=True, stop=True).then_inc(s_qall, 1)
            pe.wait_ge(s_tp, 2)
            with pe.Fori(0, NS) as b:
                pe.wait_ge(s_scan, b + 1)
                nc.tensor.matmul(PS[:, ACC, 0:H], const("after"), incl_s.rearrange("p (h r) -> p h r", r=R)[:, :, R - 1],
                                 start=True, stop=True).then_inc(s_tot, 1)
                pe.wait_ge(s_as, b + 1)
                a_hr = a_s.rearrange("p (h r) -> p h r", r=R)
                for u in range(4):
                    pe.wait_ge(s_v[u], b * 16 + 16)
                    for c in range(4):
                        for r in range(4):
                            last = nc.tensor.matmul(PS[:, ACC + 1, bass.ds(b * 32 + u * 8 + c * 2, 2)],
                                                    v_ring[:, u, r, c * P:(c + 1) * P],
                                                    a_hr[:, 2 * c:2 * c + 2, 4 * u + r], start=(r == 0), stop=(r == 3))
                    last.then_inc(s_vused, 1)

            nc.tensor.matmul(PS[:, ACC + 2, 0:64], rows_kva[0:NS, 2, P:2 * P], new_pT, start=True, stop=False)
            for b in range(NS):
                pe.wait_ge(s_va[b % 4], 16 * (b // 4 + 1))
                for r in range(R):
                    last = nc.tensor.matmul(PS[:, ACC + 2, b * H:(b + 1) * H],
                                            k_ring[:, b % 4].rearrange("p r n -> p (r n)")[:, r * P:(r + 1) * P],
                                            pT_s[:, r, b * H:(b + 1) * H], start=False, stop=(r == R - 1 and b == NS - 1))
                last.then_inc(s_vaused, 1)

            pe.wait_ge(s_wp, 32)
            pe.wait_ge(s_oas, 4)
            pe.wait_ge(s_obs, 2 * NS)
            for c in range(KC):
                if c >= 2:
                    pe.wait_ge(s_mixa, 2 * (c - 1))
                for w, o, bank in ((w_pa, oaT, 0), (w_pb, obT, 2)):
                    for k in range(4):
                        last = nc.tensor.matmul(PS[:, bank + c % 2, 0:T], w[:, k, c * P:(c + 1) * P], o[:, k, :],
                                                start=(k == 0), stop=(k == 3))
                    last.then_inc(s_pab, 1)
            pe.wait_ge(s_wo, 16)
            pe.wait_ge(s_mix, KC)
            for t in range(2):
                for n in range(2):
                    for k in range(KC):
                        last = nc.tensor.matmul(PS[:, ACC + 2 * t + n, :], mixT[:, k, t * P:(t + 1) * P],
                                                w_o[:, k, n * 512:(n + 1) * 512], start=(k == 0), stop=(k == KC - 1))
                    last.then_inc(s_h, 1)
            for c in range(KC):
                for k in range(KC):
                    last = nc.tensor.matmul(PS[:, 0, c * NS:(c + 1) * NS], w_o[:, k, c * P:(c + 1) * P],
                                            mixT[:, k, NP_TOK:T], start=(k == 0), stop=(k == KC - 1))
            last.then_inc(s_hs, 1)
            pe.wait_ge(s_hsc, 1)
            for c in range(KC):
                last = nc.tensor.transpose(PS[0:NS, 2 + c // 4, c % 4 * P:(c % 4 + 1) * P], hT_s[:, c, :], ident)
            last.then_inc(s_hst, 1)

            g = 0
            for t in range(2):
                pe.wait_ge(s_x2, t + 1)
                for half in range(2):
                    for c in range(4):
                        d0 = (half * 4 + c) * P
                        last = nc.tensor.transpose(PS[:, ACC + g, c * P:(c + 1) * P], x2_rows[:, t, d0:d0 + P], ident)
                    last.then_inc(s_x2tr, 1)
                    g += 1
            pe.wait_ge(s_x2, 3)
            for c in range(KC):
                last = nc.tensor.transpose(PS[:, 0, c * NS:(c + 1) * NS], x2_rows[0:NS, 2, c * P:(c + 1) * P],
                                           ident[0:NS, 0:NS])
            last.then_inc(s_x2tr, 1)
            pe.wait_ge(s_x2T, 5)
            pe.wait_ge(s_wr, 16 * (NG + 3))
            for t, (t0, n) in enumerate(TILES):
                for k in range(KC):
                    last = nc.tensor.matmul(PS[0:n, 1, t * 36:(t + 1) * 36], xT[:, k, t0:t0 + n], w_r[:, k, :],
                                            start=(k == 0), stop=(k == KC - 1))
            last.then_inc(s_rl, 1)
            pe.wait_ge(s_re, 1)
            for t, (t0, n) in enumerate(TILES):
                for u in range(t):
                    nc.tensor.matmul(PS[0:n, 2, t * NE:(t + 1) * NE], const("ones")[:, 0:n], mask_12[:, u, :],
                                     start=(u == 0), stop=False)
                nc.tensor.matmul(PS[0:n, 2, t * NE:(t + 1) * NE], const("before")[0:n, 0:n], mask_12[0:n, t, :],
                                 start=(t == 0), stop=True)
            for t, (t0, n) in enumerate(TILES):
                last = nc.tensor.matmul(PS[:, 2, 3 * NE:4 * NE], const("ones")[0:n, :], mask_12[0:n, t, :],
                                        start=(t == 0), stop=(t == 2))
            last.then_inc(s_rank, 1)

            def turn_pair(i, par):
                pe.wait_ge(s_xg[par], i * 16 + 16)
                for half in range(2):
                    for c in range(4):
                        last = nc.tensor.transpose(PS[:, half, c * PAIR:(c + 1) * PAIR],
                                                   xg[par][0:PAIR, half * 4 + c:D:KC], ident[0:PAIR, 0:PAIR])
                last.then_inc(s_gtr, 1)

            def pair(i, par):
                turn_pair(i, par)
                pe.wait_ge(s_gT, i * 2 + (par + 1))
                for e in range(2):
                    k = 2 * par + e
                    pe.wait_ge(s_we[k], i * 48 + 48)
                    for c in range(4):
                        for d in range(KC):
                            w0 = c // 2 * 8 * DE + d * DE + c % 2 * P
                            last = nc.tensor.matmul(PS[:, 2 + e, c * CAP:(c + 1) * CAP], slots[k][:, w0:w0 + P],
                                                    xgT[par][:, d, e * CAP:(e + 1) * CAP],
                                                    start=(d == 0), stop=(d == KC - 1))
                    last.then_inc(s_gu, 1)
                for e in range(2):
                    k = 2 * par + e
                    pe.wait_ge(s_hid, i * 4 + (2 * par + e + 1))
                    for n in range(2):
                        for c in range(2):
                            w0 = 16 * DE + c * D + n * 512
                            last = nc.tensor.matmul(PS[e * CAP:(e + 1) * CAP, ACC + 2 * par + n, :],
                                                    hid[:, e, c * CAP:(c + 1) * CAP], slots[k][:, w0:w0 + 512],
                                                    start=(c == 0), stop=(c == 1))
                    last.then_inc(s_down, 1)

            pe.wait_ge(s_rd, 1)
            pair(0, 0)
            pair(0, 1)
            with pe.Fori(1, NE // 4) as i:
                for par in range(2):
                    pe.wait_ge(s_ycopy, i * 2 + (par - 1))
                    pair(i, par)
            pe.wait_ge(s_ovf, 2)
            n_extra = pe.value_load(ovf_i[0:1, 0:1], min_val=0, max_val=NOVF)
            with pe.If(n_extra > 0):
                for t in range(NE // 2, NPAIR):
                    pe.wait_ge(s_ycopy, t - 1)
                    pair(t // 2, t % 2)

        @block.scalar
        def _(act):
            act.dma_start(g1T[:, :], a["ln1_g"][0].rearrange("(c p) -> p c", p=P),
                          allow_slow_non_contiguous=True).then_inc(s_g1, 16)
            act.wait_ge(s_prep, 1)
            act.wait_ge(s_x, 32)
            for t, (_, n) in enumerate(TILES):
                nc.scalar.activation(xn_rows[0:n, t, :], x_rows[0:n, t, :], ACT.Square,
                                     accum_out=ssq[0:n, t:t + 1]).then_inc(s_ssq, 1)

            def evac(n, dst, rows=P):
                act.wait_ge(s_proj, n + 1)
                nc.scalar.copy(dst, PS[0:rows, n % 2, 0:T]).then_inc(s_evac, 1)

            for n in range(4):
                evac(n, qiT[:, n, :])
            act.wait_ge(s_proj, 5)
            nc.scalar.copy(kiT[0:HD, :], PS[0:HD, 0, 0:T])
            nc.scalar.copy(kiT[HD:P, :], PS[0:HD, 0, 0:T]).then_inc(s_evac, 1)
            act.wait_ge(s_tr, 1)
            nc.scalar.copy(wi_rows[:, 0:2, :], PS[:, 2, 0:2 * H].rearrange("p (t h) -> p t h", t=2))
            nc.scalar.copy(wi_rows[0:NS, 2, :], PS[0:NS, 2, 2 * H:3 * H]).then_inc(s_trf, 1)
            for n in range(5, 9):
                evac(n, qaT[:, n - 5, :])
            evac(9, kaT)
            evac(10, vaT)

            def turned(m, j):
                act.wait_ge(s_tr, m + 1)
                if j >= 2:
                    act.wait_ge(s_kT_used, j - 1)
                nc.scalar.copy(kT_s[:, m % 2, :], PS[:, 2 + m % 2, :]).then_inc(s_trf, 1)

            for j in range(2 * NS):
                turned(M_KIDX + j, j)
            m = M_KIDX + 2 * NS
            act.wait_ge(s_tr, m + 1)
            nc.scalar.activation(relu_new, PS[0:64, 2 + m % 2, 0:NS], ACT.Relu).then_inc(s_trf, 1)
            for j in range(4):
                nc.scalar.activation(relu_s[:, j, :], PS[0:64, ACC + j, :], ACT.Relu).then_inc(s_relc, 1)
            m += 1
            act.wait_ge(s_tr, m + 1)
            act.wait_ge(s_wcol, 1)
            nc.scalar.copy(tmp8, PS[0:NS, 2 + m % 2, 0:NS]).then_inc(s_trf, 1)
            for j in range(4 * NS):
                turned(M_KA + j, 2 * NS + j)
            m = M_KA + 4 * NS
            act.wait_ge(s_tr, m + 1)
            nc.scalar.copy(tmp64, PS[0:64, 2 + m % 2, 0:NS]).then_inc(s_trf, 1)
            for j in range(4):
                nc.scalar.copy(logit_s[:, j * 512:(j + 1) * 512], PS[0:64, ACC + j, :]).then_inc(s_lgc, 1)

            for n in range(11, 15):
                evac(n, qbT[:, n - 11, :])
            for c in range(8):
                evac(N_PEEL + c, projected[:, c, :])
            with act.Fori(1, NLOOP) as i:
                for c in range(8):
                    n = N_PEEL + c
                    act.wait_ge(s_proj, i * 8 + (n + 1))
                    nc.scalar.activation(projected[:, bass.ds(i * 8 + c, 1), :], PS[:, n % 2:n % 2 + 1, 0:T],
                                         ACT.Exp, scale=-1.0).then_inc(s_evac, 1)

            m = M_ROWS
            outs = (("k_a", "v_a"), ("k_b",), ("v_b",), ("kidx",))
            places = (rows_kva, rows_kb, rows_vb, rows_ki)
            for dst in places:
                for t, (t0, n) in enumerate(TILES):
                    act.wait_ge(s_tr, m + 1)
                    nc.scalar.copy(dst[0:n, t, :], PS[0:n, 2 + m % 2, 0:dst.shape[2]]).then_inc(s_trf, 1)
                    m += 1
            act.wait_ge(s_trf, m)
            for names, dst in zip(outs, places):
                for k, name in enumerate(names):
                    w = dst.shape[2] // len(names)
                    act.dma_start(out[name + "_p"].rearrange("(t p) n -> p t n", p=P),
                                  dst[:, 0:2, k * w:(k + 1) * w]).then_inc(s_out, 16)
                    act.dma_start(out[name + "_s"], dst[0:NS, 2, k * w:(k + 1) * w]).then_inc(s_out, 16)

            act.wait_ge(s_brow, 1)
            nc.scalar.copy(bias_row[:, :], PS[0:H, 0, :]).then_inc(s_browc, 1)

            act.wait_ge(s_mx, 1)
            nc.scalar.activation(logit_s[:, 0:PAST + 1], logit_s[:, 0:PAST + 1], ACT.Exp, bias=mx_s,
                                 accum_out=sum_s).then_inc(s_exp_s, 1)
            for g in range(2):
                m = M_SOFT + g
                act.wait_ge(s_tr, m + 1)
                nc.scalar.copy(pT_s[:, g * 8:(g + 1) * 8, :],
                               PS[:, 2 + m % 2, :].rearrange("p (r n) -> p r n", r=8)).then_inc(s_trf, 1)
            m = M_SOFT + 2
            act.wait_ge(s_tr, m + 1)
            nc.scalar.copy(new_pT, PS[0:NS, 2 + m % 2, 0:64]).then_inc(s_trf, 1)

            for i in range(2):
                if i:
                    act.wait_ge(s_sp, 1)
                for k in range(4):
                    act.wait_ge(s_ip, i * 4 + k + 1)
                    nc.scalar.activation(relu_p[:, 2 * k:2 * k + 2, :],
                                         PS[:, ACC + k, :].rearrange("p (h s) -> p h s", h=2),
                                         ACT.Relu).then_inc(s_ipr, 1)
                act.wait_ge(s_mxp, i + 1)
                for ho in range(H):
                    nc.scalar.activation(prob_p[:, ho, :], prob_p[:, ho, :], ACT.Exp, bias=mx_p[:, ho:ho + 1],
                                         accum_out=sum_p[:, ho:ho + 1]).then_inc(s_ep, 1)
                for g in range(5):
                    m = M_PR + 5 * i + g
                    act.wait_ge(s_tr, m + 1)
                    if g < 4:
                        if 4 * i + g >= 2:
                            act.wait_ge(s_pT_used, 4 * i + g - 1)
                        nc.scalar.copy(pT_p[:, m % 2, :], PS[:, 2 + m % 2, :]).then_inc(s_trf, 1)
                    else:
                        nc.scalar.copy(oaT[:, :, i * P:(i + 1) * P],
                                       PS[:, 2 + m % 2, :].rearrange("p (c q) -> p c q", c=4)).then_inc(s_trf, 1)

            for par in range(2):
                act.wait_ge(s_zpc, par + 1)
                nc.scalar.activation(e_p, z_p, ACT.Abs).then_inc(s_lnp, 1)
                act.wait_ge(s_lnp, 3 * par + 1)
                nc.scalar.activation(e_p, e_p, ACT.Exp, scale=-1.0).then_inc(s_lnp, 1)
                act.wait_ge(s_lnp, 3 * par + 2)
                nc.scalar.activation(e_p, e_p, ACT.Ln, bias=1.0).then_inc(s_lnp, 1)
                act.wait_ge(s_tp, par + 1)
                nc.scalar.activation(z_p, z_p, ACT.Exp).then_inc(s_ap, 1)
                act.wait_ge(s_obp, par + 1)
                half = slice(par * HD, (par + 1) * HD)
                for k in range(2):
                    last = nc.scalar.copy(obT[half, 2 * k:2 * k + 2, 0:NP_TOK],
                                          PS[half, k, :].rearrange("p (c q) -> p c q", c=2))
                last.then_inc(s_obT, 1)

            m = M_QROW
            act.wait_ge(s_tr, m + 1)
            nc.scalar.activation(q_row, PS[0:NS, 2 + m % 2, :], ACT.Copy, scale=HD ** -0.5).then_inc(s_trf, 1)
            for b in range(NS):
                act.wait_ge(s_qall, b + 1)
                nc.scalar.copy(q_all[:, b, :], PS[:, b % 2, :]).then_inc(s_qallc, 1)
            with act.Fori(0, NS) as b:
                act.wait_ge(s_kused, b * 4 + 4)
                nc.scalar.activation(e_s, z_s, ACT.Abs).then_inc(s_ls, 1)
                act.wait_ge(s_ls, b * 3 + 1)
                nc.scalar.activation(e_s, e_s, ACT.Exp, scale=-1.0).then_inc(s_ls, 1)
                act.wait_ge(s_ls, b * 3 + 2)
                nc.scalar.activation(e_s, e_s, ACT.Ln, bias=1.0).then_inc(s_ls, 1)
                act.wait_ge(s_ts, b + 1)
                nc.scalar.activation(a_s, z_s, ACT.Exp).then_inc(s_as, 1)

            for t, (_, n) in enumerate(TILES):
                act.wait_ge(s_hadd, (2, 4, 6)[t])
                if t:
                    act.wait_ge(s_ssq2, t)
                nc.scalar.activation(junk_rows[0:n, :], x_rows[0:n, t, :], ACT.Square,
                                     accum_out=ssq[0:n, t:t + 1]).then_inc(s_ssq2, 1)
            for t, (t0, n) in enumerate(TILES):
                act.wait_ge(s_x2, t + 1)
                act.dma_start(x2_dram[t0:t0 + n, :], x2_rows[0:n, t, :]).then_inc(s_x2d, 16)
            act.wait_ge(s_rd, 2)
            nc.scalar.activation(exp_g, exp_g, ACT.Exp).then_inc(s_gexp2, 1)
            act.wait_ge(s_rd, 3)
            nc.scalar.activation(e_2, e_2, ACT.Exp).then_inc(s_gexp2, 1)

            def pair(i, par, first=False):
                act.wait_ge(s_gtr, i * 2 + (par + 1))
                for half in range(2):
                    last = nc.scalar.copy(xgT[par][:, half * 4:half * 4 + 4, 0:PAIR],
                                          PS[:, half, 0:4 * PAIR].rearrange("p (c n) -> p c n", c=4))
                last.then_inc(s_gT, 1)
                for e in range(2):
                    act.wait_ge(s_gu, i * 4 + (2 * par + e + 1))
                    nc.scalar.activation(act_e[:, e, :], PS[:, 2 + e, 0:2 * CAP], ACT.Exp, scale=-1.0
                                         ).then_inc(s_act, 1)
                if not first:
                    act.wait_ge(s_yout[par], i * 16)
                act.wait_ge(s_down, i * 4 + (2 * par + 2))
                nc.scalar.copy(y_sb[par][0:PAIR, :].rearrange("p (b n) -> p b n", b=2),
                               PS[0:PAIR, ACC + 2 * par:ACC + 2 * par + 2, :]).then_inc(s_ycopy, 1)
                act.wait_ge(s_ycopy, i * 2 + (par + 1))
                act.dma_start(y_dram[bass.ds(i * (2 * PAIR) + par * PAIR, PAIR), :] if not first else
                              y_dram[par * PAIR:(par + 1) * PAIR, :], y_sb[par][0:PAIR, :]).then_inc(s_yout[par], 16)

            act.wait_ge(s_y0, 16)
            act.wait_ge(s_x2T, 5)
            pair(0, 0, True)
            pair(0, 1, True)
            with act.Fori(1, NE // 4) as i:
                for par in range(2):
                    pair(i, par)
            act.wait_ge(s_ovf, 2)
            n_extra = act.value_load(ovf_i[0:1, 0:1], min_val=0, max_val=NOVF)
            with act.If(n_extra > 0):
                for t in range(NE // 2, NPAIR):
                    pair(t // 2, t % 2)
            for t, (_, n) in enumerate(TILES):
                act.wait_ge(s_fin, t + 1)
                nc.scalar.activation(y_1[0:n, t, :], x_rows[0:n, t, :], ACT.Square,
                                     accum_out=ssq[0:n, t:t + 1]).then_inc(s_ssq3, 1)
            for t, (_, n) in enumerate(TILES):
                act.wait_ge(s_yo, t + 1)
                act.dma_start(out["y_p"][t * P:(t + 1) * P, :] if t < 2 else out["y_s"], y_2[0:n, t, :]
                              ).then_inc(s_done, 16)
            act.wait_ge(s_done, 48)
            act.wait_ge(s_out, 160)

        @block.vector
        def _(dve):
            chain = [0]

            def link(ins):
                chain[0] += 1
                ins.then_inc(s_chain, 1)
                dve.wait_ge(s_chain, chain[0])

            nc.vector.memset(ssq, 1.0).then_inc(s_prep, 1)
            dve.wait_ge(s_page, 16)
            dve.wait_ge(s_const, 16)
            link(nc.vector.tensor_scalar(page_idx[:, :], page_of[:, :], float(RB), const("row_block")[:, 0:1],
                                         ALU.mult, ALU.add))
            nc.vector.tensor_scalar(unit_idx[:, 0, :], page_idx[:, :], 4.0, None, ALU.mult).then_inc(s_idx, 1)
            for u in range(1, 4):
                nc.vector.tensor_scalar(unit_idx[:, u, :], page_idx[:, :], 4.0, float(u), ALU.mult, ALU.add
                                        ).then_inc(s_idx, 1)
            dve.wait_ge(s_ssq, 3)
            nc.vector.tensor_scalar(ms, ssq, 1.0 / D, EPS, ALU.mult, ALU.add).then_inc(s_ms, 1)
            dve.wait_ge(s_rstd, 1)
            for t, (_, n) in enumerate(TILES):
                nc.vector.tensor_scalar(xn_rows[0:n, t, :], x_rows[0:n, t, :], rstd[0:n, t:t + 1], None,
                                        ALU.mult).then_inc(s_xn, 1)
            dve.wait_ge(s_g1, 16)
            for g in range(4):
                t, half = g // 2, g % 2
                dve.wait_ge(s_xtr, g + 1)
                nc.vector.tensor_tensor(xT[:, half * 4:half * 4 + 4, t * P:(t + 1) * P],
                                        PS[:, 2 + g % 2, :].rearrange("p (c n) -> p c n", c=4),
                                        g1T[:, half * 4:half * 4 + 4].unsqueeze(2).to_broadcast([P, 4, P]),
                                        ALU.mult).then_inc(s_xT, 1)
            dve.wait_ge(s_xtr, 5)
            nc.vector.tensor_tensor(xT[:, :, NP_TOK:T], PS[:, 2, 0:KC * NS].rearrange("p (c n) -> p c n", c=KC),
                                    g1T[:, :].unsqueeze(2).to_broadcast([P, KC, NS]), ALU.mult).then_inc(s_xT, 1)

            link(nc.vector.memset(temp[:, 8208:9232 + 128], 0.0))
            pad = qiPad.rearrange("p b m -> p (b m)")
            dve.wait_ge(s_evac, 4)
            for par in range(2):
                src = qiT[par * HD:(par + 1) * HD, :, NP_TOK:T]
                for half in range(2):
                    for b in range(NS):
                        nc.vector.tensor_copy(pad[half * HD:(half + 1) * HD, b * 72 + par:b * 72 + par + 7:2],
                                              src[:, :, b])
                for b in range(NS):
                    last = nc.vector.tensor_copy(qiAll[:, b * H + par:b * H + par + 7:2], src[:, :, b])
            last.then_inc(s_qipad, 1)
            dve.wait_ge(s_wexp, 1)
            link(nc.vector.tensor_tensor(tmp64, PS[0:64, ACC, 0:H], const("same_h"), ALU.mult))
            link(nc.vector.tensor_reduce(wcol, tmp64, AX_X, ALU.add))
            nc.vector.tensor_scalar(w_blk, const("same_b"), wcol, float(H ** -0.5 * HD ** -0.5), ALU.mult, ALU.mult
                                    ).then_inc(s_wcol, 1)
            dve.wait_ge(s_evac, 9)
            pad = qaPad.rearrange("p b m -> p (b m)")
            for par in range(2):
                for kv in range(2):
                    src = qaT[par * HD:(par + 1) * HD, 2 * kv:2 * kv + 2, NP_TOK:T]
                    for b in range(NS):
                        for dst, at in ((pad, b * 72 + 4 * kv + par), (qaAll, b * H + 4 * kv + par)):
                            last = nc.vector.tensor_scalar(dst[kv * HD:(kv + 1) * HD, at:at + 3:2], src[:, :, b],
                                                           HD ** -0.5, None, ALU.mult)
            last.then_inc(s_qapad, 1)

            by_r = score_s[:, 0:PAST].rearrange("b (x r) -> b r x", r=R)
            for j in range(4):
                half, e = j // 2, j % 2
                dve.wait_ge(s_sc, j + 1)
                nc.vector.tensor_copy(by_r[:, half * 8 + e:half * 8 + e + 7:2, :],
                                      PS[0:NS, ACC + j, :].rearrange("b (q x) -> b q x", q=4)).then_inc(s_scc, 1)
            dve.wait_ge(s_trf, M_KA)
            link(nc.vector.tensor_tensor(tmp8, tmp8, ident[0:NS, 0:NS], ALU.mult))
            nc.vector.tensor_reduce(score_s[:, PAST:PAST + 1], tmp8, AX_X, ALU.add).then_inc(s_scc, 1)
            dve.wait_ge(s_scc, 5)
            with dve.Fori(0, TOPK_S // 8) as i:
                nc.vector.max(top8, score_s[:, 0:PAST + 1]).then_inc(s_top, 1)
                dve.wait_ge(s_top, i * 2 + 1)
                nc.vector.memset(small[0:1, 32:33], 0.0)
                nc.vector.match_replace(out=score_s[:, 0:PAST + 1], in_to_replace=top8,
                                        in_values=score_s[:, 0:PAST + 1], imm_value=GONE).then_inc(s_top, 1)
                dve.wait_ge(s_top, i * 2 + 2)
            nc.vector.memset(table33[NB:NB + 1, :], 1.0).then_inc(s_ones33, 1)
            dve.wait_ge(s_lgc, 4)
            by_r = score_s[:, 0:PAST].rearrange("b (x r) -> b r x", r=R)
            nc.vector.memset(taken_s[:, PAST:PAST + 8], 0.0)
            link(nc.vector.tensor_scalar(taken_s[:, 0:PAST].rearrange("b (r x) -> b r x", r=R), by_r, GONE, NEG,
                                         ALU.not_equal, ALU.mult))
            nc.vector.tensor_scalar(taken_s[:, PAST:PAST + 1], score_s[:, PAST:PAST + 1], GONE, NEG,
                                    ALU.not_equal, ALU.mult).then_inc(s_taken, 1)
            dve.wait_ge(s_trf, M_KA + 4 * NS + 1)
            link(nc.vector.tensor_tensor(tmp64, tmp64, const("same_b"), ALU.mult))
            link(nc.vector.tensor_reduce(logit_s[:, PAST:PAST + 1], tmp64, AX_X, ALU.add))
            for j in range(4):
                dve.wait_ge(s_nm, j + 1)
                cols = slice(j * 512, (j + 1) * 512)
                link(nc.vector.tensor_tensor(logit_s[:, cols], PS[0:64, ACC + j, :], logit_s[:, cols], ALU.add))
            dve.wait_ge(s_nm, 5)
            link(nc.vector.tensor_tensor(logit_s[:, PAST:PAST + 1], PS[0:64, 0, 0:1], logit_s[:, PAST:PAST + 1],
                                         ALU.add))
            link(nc.vector.tensor_reduce(mx_s, logit_s[:, 0:PAST + 1], AX_X, ALU.max))
            nc.vector.tensor_scalar(mx_s, mx_s, -1.0, None, ALU.mult).then_inc(s_mx, 1)
            dve.wait_ge(s_exp_s, 1)
            link(nc.vector.reciprocal(inv_s, sum_s))
            link(nc.vector.tensor_scalar(logit_s[:, 0:PAST + 1], logit_s[:, 0:PAST + 1], inv_s, None, ALU.mult))
            nc.vector.tensor_scalar(new_p, const("same_b"), logit_s[:, PAST:PAST + 1], None, ALU.mult
                                    ).then_inc(s_prob_s, 1)

            link(nc.vector.tensor_scalar(wi_scaled, wi_rows[:, 0:2, :], float(H ** -0.5 * HD ** -0.5), None, ALU.mult))
            nc.vector.tensor_copy(kaSwap[0:HD, :], kaT[HD:P, :])
            nc.vector.tensor_copy(kaSwap[HD:P, :], kaT[0:HD, :]).then_inc(s_swap, 1)
            for i in range(2):
                for ho in range(H):
                    h = 2 * (ho % 4) + ho // 4
                    if ho % 2 == 0:
                        dve.wait_ge(s_ipr, i * 4 + ho // 2 + 1)
                    link(nc.vector.scalar_tensor_tensor(
                        out=score_p, in0=relu_p[:, ho, :], scalar=wi_scaled[:, i, h:h + 1],
                        in1=const("causal")[:, (1 - i) * P:(1 - i) * P + 256] if ho == 0 else score_p,
                        op0=ALU.mult, op1=ALU.add))
                for k in range(TOPK_P // 8):
                    link(nc.vector.max(top_p, score_p))
                    link(nc.vector.match_replace(out=score_p, in_to_replace=top_p, in_values=score_p, imm_value=GONE))
                nc.vector.tensor_scalar(kept_p, score_p, GONE, NEG, ALU.not_equal, ALU.mult).then_inc(s_sp, 1)

                dve.wait_ge(s_biasp, 32)
                if i:
                    dve.wait_ge(s_trf, M_PR + 4)
                for k in range(4):
                    dve.wait_ge(s_lp, i * 4 + k + 1)
                    nc.vector.scalar_tensor_tensor(
                        out=prob_p[:, 2 * k:2 * k + 2, :], in0=PS[:, ACC + k, :].rearrange("p (h s) -> p h s", h=2),
                        scalar=HD ** -0.5, in1=bias_p[:, 2 * k:2 * k + 2, (1 - i) * P:(1 - i) * P + 256],
                        op0=ALU.mult, op1=ALU.add).then_inc(s_lpb, 1)
                dve.wait_ge(s_lpb, 4 * i + 4)
                dve.wait_ge(s_sp, i + 1)
                link(nc.vector.tensor_tensor(prob_p, prob_p, kept_p.unsqueeze(1).to_broadcast([P, H, 256]), ALU.add))
                link(nc.vector.tensor_reduce(mx_p, prob_p, AX_X, ALU.max))
                nc.vector.tensor_scalar(mx_p, mx_p, -1.0, None, ALU.mult).then_inc(s_mxp, 1)
                dve.wait_ge(s_ep, (i + 1) * H)
                link(nc.vector.reciprocal(inv_p, sum_p))
                dve.wait_ge(s_pT_used, 4 * i + 4)
                if i:
                    dve.wait_ge(s_trf, M_PR + 5)
                nc.vector.tensor_tensor(
                    o_rows.rearrange("p (c e d) -> p e c d", c=4, e=2),
                    PS[:, 1, :].rearrange("p (c e d) -> p e c d", c=4, e=2),
                    inv_p.rearrange("p (e c) -> p e c", e=2).unsqueeze(3).to_broadcast([P, 2, 4, HD]),
                    ALU.mult).then_inc(s_onorm, 1)

            for par in range(2):
                dve.wait_ge(s_zp, par + 1)
                if par:
                    dve.wait_ge(s_obp, 1)
                nc.vector.scalar_tensor_tensor(
                    out=z_p[:, 0:1024].rearrange("p (c q) -> p c q", c=4),
                    in0=PS[:, ACC:ACC + 2, :].rearrange("p k (c q) -> p (k c) q", c=2), scalar=HD ** -0.5,
                    in1=const("strict").unsqueeze(1).to_broadcast([P, 4, 256]), op0=ALU.mult, op1=ALU.add)
                nc.vector.scalar_tensor_tensor(
                    out=z_p[:, 1024:1536].rearrange("p (c q) -> p c q", c=4),
                    in0=PS[:, ACC + 2, :].rearrange("p (c q) -> p c q", c=4), scalar=HD ** -0.5,
                    in1=const("strict")[:, 0:P].unsqueeze(1).to_broadcast([P, 4, P]), op0=ALU.mult, op1=ALU.add
                ).then_inc(s_zpc, 1)
                dve.wait_ge(s_lnp, 3 * par + 3)
                nc.vector.scalar_tensor_tensor(out=e_p, in0=z_p, scalar=0.0, in1=e_p, op0=ALU.max, op1=ALU.add
                                               ).then_inc(s_spp, 1)
                dve.wait_ge(s_spp, par + 1)
                link(nc.vector.tensor_tensor(z_p, z_p, e_p, ALU.subtract))
                dve.wait_ge(s_aft, par + 1)
                nc.vector.tensor_tensor(z_p.rearrange("p (k n) -> p k n", k=3), PS[:, ACC:ACC + 3, :],
                                        z_p.rearrange("p (k n) -> p k n", k=3), ALU.add).then_inc(s_tp, 1)

            h_r = lambda t: t.rearrange("p (h r) -> p h r", r=R)
            dve.wait_ge(s_qallc, NS)
            with dve.Fori(0, NS) as b:
                for u in range(4):
                    dve.wait_ge(s_k[u], b * 16 + 16)
                    nc.vector.tensor_tensor(k_ring[:, u], k_ring[:, u],
                                            q_all[:, bass.ds(b, 1), :].to_broadcast([P, 4, H * HD]), ALU.mult
                                            ).then_inc(s_mul, 1)
                    dve.wait_ge(s_mul, b * 4 + (u + 1))
                    nc.vector.tensor_reduce(h_r(z_s).rearrange("p h r -> p r h")[:, 4 * u:4 * u + 4, :],
                                            k_ring[:, u].rearrange("p r (h d) -> p r h d", h=H), AX_X, ALU.add
                                            ).then_inc(s_kused, 1)
                dve.wait_ge(s_ls, b * 3 + 3)
                nc.vector.scalar_tensor_tensor(out=e_s, in0=z_s, scalar=0.0, in1=e_s, op0=ALU.max, op1=ALU.add
                                               ).then_inc(s_sps, 1)
                dve.wait_ge(s_sps, b * 4 + 1)
                nc.vector.tensor_tensor_scan(incl_s, const("segment"), e_s, 0.0, ALU.mult, ALU.add).then_inc(s_scan, 1)
                nc.vector.tensor_tensor(z_s, z_s, e_s, ALU.subtract).then_inc(s_sps, 1)
                dve.wait_ge(s_scan, b + 1)
                dve.wait_ge(s_sps, b * 4 + 2)
                nc.vector.tensor_tensor(z_s, z_s, incl_s, ALU.add).then_inc(s_sps, 1)
                dve.wait_ge(s_tot, b + 1)
                nc.vector.tensor_tensor(later_s, PS[:, ACC, 0:H], h_r(incl_s)[:, :, R - 1], ALU.subtract
                                        ).then_inc(s_sps, 1)
                dve.wait_ge(s_sps, b * 4 + 4)
                nc.vector.tensor_tensor(h_r(z_s), h_r(z_s), later_s.unsqueeze(2).to_broadcast([P, H, R]), ALU.add
                                        ).then_inc(s_ts, 1)
                dve.wait_ge(s_as, b + 1)
            dve.wait_ge(s_vused, 4 * NS)
            for par in range(2):
                half = slice(par * HD, (par + 1) * HD)
                src = PS[half, ACC + 1, 0:32 * NS].rearrange("p (b u c e) -> p b e c u", b=NS, u=4, c=4)
                for b in range(NS):
                    nc.vector.tensor_reduce(obT[half, :, NP_TOK + b], src[:, b, par], AX_X, ALU.add).then_inc(s_obs, 1)
            dve.wait_ge(s_vaused, NS)
            for kv in range(2):
                for par in range(2):
                    src = PS[kv * HD:(kv + 1) * HD, ACC + 2, 0:64].rearrange("p (b v c e) -> p v e c b", b=NS, v=2, c=2)
                    nc.vector.tensor_copy(oaT[par * HD:(par + 1) * HD, 2 * kv:2 * kv + 2, NP_TOK:T],
                                          src[:, kv, par]).then_inc(s_oas, 1)

            dve.wait_ge(s_evac, N_PEEL + 8 * NLOOP)
            link(nc.vector.tensor_scalar(gates, gates, 1.0, None, ALU.add))
            link(nc.vector.reciprocal(gates, gates))
            for c in range(KC):
                dve.wait_ge(s_pab, 2 * c + 1)
                nc.vector.tensor_tensor(part[:, 0, :], PS[:, c % 2, 0:T], gates[:, c, :], ALU.mult).then_inc(s_mixa, 1)
                dve.wait_ge(s_pab, 2 * c + 2)
                nc.vector.tensor_tensor(part[:, 1, :], PS[:, 2 + c % 2, 0:T], gates[:, KC + c, :], ALU.mult
                                        ).then_inc(s_mixa, 1)
                dve.wait_ge(s_mixa, 2 * c + 2)
                nc.vector.tensor_tensor(mixT[:, c, :], part[:, 0, :], part[:, 1, :], ALU.add).then_inc(s_mix, 1)
                dve.wait_ge(s_mix, c + 1)
            for j in range(4):
                t, n = j // 2, j % 2
                dve.wait_ge(s_h, j + 1)
                cols = slice(n * 512, (n + 1) * 512)
                nc.vector.tensor_tensor(x_rows[:, t, cols], PS[:, ACC + j, :], x_rows[:, t, cols], ALU.add
                                        ).then_inc(s_hadd, 1)
            dve.wait_ge(s_hs, 1)
            nc.vector.tensor_copy(hT_s.rearrange("p c n -> p (c n)"), PS[:, 0, 0:KC * NS]).then_inc(s_hsc, 1)
            dve.wait_ge(s_hst, 1)
            for n in range(2):
                cols = slice(n * 512, (n + 1) * 512)
                nc.vector.tensor_tensor(x_rows[0:NS, 2, cols], PS[0:NS, 2 + n, :], x_rows[0:NS, 2, cols], ALU.add
                                        ).then_inc(s_hadd, 1)
            dve.wait_ge(s_ssq2, 3)
            nc.vector.tensor_scalar(ms, ssq, 1.0 / D, EPS, ALU.mult, ALU.add).then_inc(s_ms2, 1)
            dve.wait_ge(s_rstd2, 1)
            dve.wait_ge(s_gains, 32)
            for t, (_, n) in enumerate(TILES):
                nc.vector.scalar_tensor_tensor(out=x2_rows[0:n, t, :], in0=x_rows[0:n, t, :], scalar=rstd[0:n, t:t + 1],
                                               in1=g2_all[0:n, :], op0=ALU.mult, op1=ALU.mult).then_inc(s_x2, 1)
            for g in range(4):
                t, half = g // 2, g % 2
                dve.wait_ge(s_x2tr, g + 1)
                nc.vector.tensor_copy(xT[:, half * 4:half * 4 + 4, t * P:(t + 1) * P],
                                      PS[:, ACC + g, :].rearrange("p (c n) -> p c n", c=4)).then_inc(s_x2T, 1)
            dve.wait_ge(s_x2tr, 5)
            nc.vector.tensor_copy(xT[:, :, NP_TOK:T], PS[:, 0, 0:KC * NS].rearrange("p (c n) -> p c n", c=KC)
                                  ).then_inc(s_x2T, 1)

            link(nc.vector.memset(rt[:, :], 0.0))
            dve.wait_ge(s_rl, 1)
            bc3 = lambda t, n: t.unsqueeze(2).to_broadcast([P, 3, n])
            link(nc.vector.tensor_tensor(lg[:, 0:2, :], PS[:, 1, 0:72].rearrange("p (t n) -> p t n", t=2),
                                         b_r[:, :].unsqueeze(1).to_broadcast([P, 2, NG + NE]), ALU.add))
            link(nc.vector.tensor_tensor(lg[0:NS, 2, :], PS[0:NS, 1, 72:108], b_r[0:NS, :], ALU.add))
            lg_g, lg_e = lg[:, :, 0:NG], lg[:, :, NG:NG + NE].rearrange("p t (g e) -> p t g e", g=NG)

            def first_max(val, top, eq, one, iota, n):
                link(nc.vector.tensor_reduce(top, val, AX_X, ALU.max))
                link(nc.vector.tensor_tensor(eq, val, bc3(top, n), ALU.is_equal))
                link(nc.vector.scalar_tensor_tensor(out=eq, in0=eq, scalar=-100.0,
                                                    in1=iota.rearrange("p (t n) -> p t n", t=3),
                                                    op0=ALU.mult, op1=ALU.add))
                link(nc.vector.tensor_reduce(small[:, 16:19], eq, AX_X, ALU.min))
                link(nc.vector.tensor_tensor(one, eq, bc3(small[:, 16:19], n), ALU.is_equal))

            first_max(lg_g, top_g, eq_g, one_g, const("iota_g"), NG)
            dve.wait_ge(s_x2T, 5)
            nc.vector.tensor_copy(small[:, 20:21], small[:, 16:17]).then_inc(s_rd, 1)
            nc.vector.tensor_tensor(exp_g, lg_g, bc3(top_g, NG), ALU.subtract).then_inc(s_rd, 1)
            for t in range(3):
                link(nc.vector.tensor_tensor(mask_1[:, t, :].rearrange("p (g e) -> p g e", g=NG), lg_e[:, t],
                                             one_g[:, t, :].unsqueeze(2).to_broadcast([P, NG, EG]), ALU.mult))
            link(nc.vector.tensor_reduce(le, mask_1.rearrange("p t (g e) -> p t e g", g=NG), AX_X, ALU.add))
            first_max(le, top_1, eq_e, one_1, const("iota_8"), EG)
            link(nc.vector.scalar_tensor_tensor(out=le, in0=one_1, scalar=NEG, in1=le, op0=ALU.mult, op1=ALU.add))
            first_max(le, top_2, eq_e, one_2, const("iota_8"), EG)
            nc.vector.tensor_tensor(e_2, top_2, top_1, ALU.subtract).then_inc(s_rd, 1)
            for one, mask in ((one_1, mask_1), (one_2, mask_2)):
                for t in range(3):
                    link(nc.vector.tensor_tensor(mask[:, t, :].rearrange("p (g e) -> p g e", g=NG),
                                                 one[:, t, :].unsqueeze(1).to_broadcast([P, NG, EG]),
                                                 one_g[:, t, :].unsqueeze(2).to_broadcast([P, NG, EG]), ALU.mult))
            nc.vector.tensor_tensor(mask_12, mask_1, mask_2, ALU.add).then_inc(s_re, 1)
            dve.wait_ge(s_gexp2, 2)
            link(nc.vector.tensor_reduce(g_w, exp_g, AX_X, ALU.add))
            link(nc.vector.tensor_scalar(wt_1, e_2, 1.0, None, ALU.add))
            link(nc.vector.tensor_tensor(wt_1, wt_1, g_w, ALU.mult))
            link(nc.vector.reciprocal(wt_1, wt_1))
            link(nc.vector.tensor_tensor(wt_2, wt_1, e_2, ALU.mult))
            dve.wait_ge(s_rank, 1)
            count = PS[:, 2, 3 * NE:4 * NE]
            link(nc.vector.tensor_scalar(extra, count, float(CAP), None, ALU.is_gt))
            for j in range(2, (T - 1) // CAP + 1):
                link(nc.vector.scalar_tensor_tensor(out=extra, in0=count, scalar=float(j * CAP), in1=extra,
                                                    op0=ALU.is_gt, op1=ALU.add))
            link(nc.vector.tensor_tensor_scan(upto, const("ones")[:, 0:NE], extra, 0.0, ALU.mult, ALU.add))
            link(nc.vector.tensor_tensor(before_e, upto, extra, ALU.subtract))
            link(nc.vector.scalar_tensor_tensor(out=base_e, in0=before_e, scalar=float(NE - 1), in1=const("iota_e"),
                                                op0=ALU.add, op1=ALU.subtract))
            rank = PS[:, 2, 0:3 * NE].rearrange("p (t n) -> p t n", t=3)
            for t, (_, n) in enumerate(TILES):
                link(nc.vector.tensor_scalar(ROW[0:n, t, :], rank[0:n, t, :], float(CAP), None, ALU.is_ge))
                link(nc.vector.tensor_tensor(ROW[0:n, t, :], ROW[0:n, t, :], base_e[0:n, :], ALU.mult))
                link(nc.vector.tensor_tensor(ROW[0:n, t, :], ROW[0:n, t, :], const("iota_e")[0:n, :], ALU.add))
                link(nc.vector.scalar_tensor_tensor(out=ROW[0:n, t, :], in0=ROW[0:n, t, :], scalar=float(CAP),
                                                    in1=rank[0:n, t, :], op0=ALU.mult, op1=ALU.add))
            for k, mask in enumerate((mask_1, mask_2)):
                link(nc.vector.tensor_tensor(mask, mask, ROW, ALU.mult))
                link(nc.vector.tensor_reduce(row_f[:, k, :], mask, AX_X, ALU.add))
            link(nc.vector.tensor_copy(row_i[:, :, :], row_f))
            link(nc.vector.tensor_scalar(low_i[:, :, :], row_i[:, :, :], PAIR - 1, None, ALU.bitwise_and))
            link(nc.vector.tensor_scalar(high_i[:, :, :], row_i[:, :, :], PAIR.bit_length() - 1, None,
                                         ALU.logical_shift_right))
            nc.vector.scalar_tensor_tensor(out=addr_i[:, :, :], in0=low_i[:, :, :], scalar=float(NPAIR),
                                           in1=high_i[:, :, :], op0=ALU.mult, op1=ALU.add).then_inc(s_rowi, 1)
            nc.vector.tensor_copy(ovf_i[0:1, 0:1], upto[0:1, NE - 1:NE]).then_inc(s_ovf, 1)
            in_blk = blk_tmp.rearrange("p (k n) -> p k n", k=2)
            b_e = lambda t: t.rearrange("p (b e) -> p b e", b=NOVF)
            link(nc.vector.tensor_tensor(b_e(in_blk[:, 0]), b_e(const("iota_blk")),
                                         before_e[0:1, :].unsqueeze(1).to_broadcast([1, NOVF, NE]), ALU.is_ge))
            link(nc.vector.tensor_tensor(b_e(in_blk[:, 1]), b_e(const("iota_blk")),
                                         upto[0:1, :].unsqueeze(1).to_broadcast([1, NOVF, NE]), ALU.is_lt))
            link(nc.vector.tensor_tensor(in_blk[:, 0], in_blk[:, 0], in_blk[:, 1], ALU.mult))
            link(nc.vector.tensor_tensor(in_blk[:, 0], in_blk[:, 0], const("iota_e_blk"), ALU.mult))
            link(nc.vector.tensor_reduce(blk, b_e(in_blk[:, 0]), AX_X, ALU.add))
            nc.vector.tensor_copy(ovf_i[0:1, 1:NOVF + 1], blk).then_inc(s_ovf, 1)

            def pair(i, par):
                for e in range(2):
                    n = 2 * par + e
                    g, u = PS[:, 2 + e, 0:2 * CAP], PS[:, 2 + e, 2 * CAP:4 * CAP]
                    dve.wait_ge(s_act, i * 4 + (n + 1))
                    nc.vector.tensor_scalar(act_e[:, e, :], act_e[:, e, :], 1.0, None, ALU.add).then_inc(s_gp1, 1)
                    dve.wait_ge(s_gp1, i * 12 + (3 * n + 1))
                    nc.vector.reciprocal(act_e[:, e, :], act_e[:, e, :]).then_inc(s_gp1, 1)
                    dve.wait_ge(s_gp1, i * 12 + (3 * n + 2))
                    nc.vector.tensor_tensor(act_e[:, e, :], g, act_e[:, e, :], ALU.mult).then_inc(s_gp1, 1)
                    dve.wait_ge(s_gp1, i * 12 + (3 * n + 3))
                    nc.vector.tensor_tensor(hid[:, e, :], u, act_e[:, e, :], ALU.mult).then_inc(s_hid, 1)

            with dve.Fori(0, NE // 4) as i:
                for par in range(2):
                    pair(i, par)
            dve.wait_ge(s_ovf, 2)
            n_extra = dve.value_load(ovf_i[0:1, 0:1], min_val=0, max_val=NOVF)
            with dve.If(n_extra > 0):
                for t in range(NE // 2, NPAIR):
                    pair(t // 2, t % 2)
            dve.wait_ge(s_y12, 96)
            for t, (_, n) in enumerate(TILES):
                x = x_rows[0:n, t, :]
                link(nc.vector.scalar_tensor_tensor(out=x, in0=y_1[0:n, t, :], scalar=wt_1[0:n, t:t + 1], in1=x,
                                                    op0=ALU.mult, op1=ALU.add))
                nc.vector.scalar_tensor_tensor(out=x, in0=y_2[0:n, t, :], scalar=wt_2[0:n, t:t + 1], in1=x,
                                               op0=ALU.mult, op1=ALU.add).then_inc(s_fin, 1)
            dve.wait_ge(s_ssq3, 3)
            nc.vector.tensor_scalar(ms, ssq, 1.0 / D, EPS, ALU.mult, ALU.add).then_inc(s_ms3, 1)
            dve.wait_ge(s_rstd3, 1)
            for t, (_, n) in enumerate(TILES):
                nc.vector.scalar_tensor_tensor(out=y_2[0:n, t, :], in0=x_rows[0:n, t, :], scalar=rstd[0:n, t:t + 1],
                                               in1=gf_all[0:n, :], op0=ALU.mult, op1=ALU.mult).then_inc(s_yo, 1)


def kernel(**inputs):
    import concourse.bacc as bacc
    from concourse.bass_utils import run_bass_kernel_spmd

    nc = bacc.Bacc("TRN2", target_bir_lowering=False, num_devices=1)
    at, packed, sample_buckets, token_ids = shape_constants()
    arrays = {name: np.ascontiguousarray(inputs[name]) for name in inputs if name != "page_table"}
    arrays["pages"] = np.ascontiguousarray(np.repeat(inputs["page_table"], RB, axis=1).T)
    arrays.update(shape_consts=packed, sample_buckets=sample_buckets, token_ids=token_ids)
    a = {n: nc.dram_tensor(f"in_{n}", v.shape, mybir.dt.from_np(v.dtype), kind="ExternalInput").ap()
         for n, v in arrays.items()}
    rows = {"k_a": 2 * HD, "v_a": 2 * HD, "kidx": HD, "k_b": H * HD, "v_b": H * HD}
    shapes = {"y_p": (NP_TOK, D), "y_s": (NS, D)}
    shapes.update({f"{n}_p": (NP_TOK, w) for n, w in rows.items()})
    shapes.update({f"{n}_s": (NS, w) for n, w in rows.items()})
    out = {n: nc.dram_tensor(f"out_{n}", s, F32, kind="ExternalOutput").ap() for n, s in shapes.items()}
    decoder_step(nc, a, out, at)
    got = run_bass_kernel_spmd(nc, [{f"in_{n}": v for n, v in arrays.items()}], core_ids=[0]).results[0]

    def new_rows(name, batch, tokens):
        heads = {"k_a": (2, HD), "v_a": (2, HD), "kidx": (HD,), "k_b": (H, HD), "v_b": (H, HD)}[name[:-2]]
        return got[f"out_{name}"].reshape((1, batch, tokens) + heads)

    names = ("k_a", "v_a", "kidx", "k_b", "v_b")
    return ((got["out_y_p"].reshape(1, NP_TOK, D), got["out_y_s"].reshape(NS, 1, D))
            + tuple(new_rows(f"{n}_p", 1, NP_TOK) for n in names)
            + tuple(new_rows(f"{n}_s", NS, 1) for n in names))
```

```python
from contextlib import ExitStack

import numpy as np

import concourse.bass as bass
from concourse import mybir

F32 = mybir.dt.float32
I32 = mybir.dt.int32
ALU = mybir.AluOpType
ACT = mybir.ActivationFunctionType
AX_X = mybir.AxisListType.X

P = 128
D = 1024
KC = D // P
NP_TOK = 256
NS = 8
T = NP_TOK + NS
TILES = [(0, P), (P, P), (2 * P, NS)]
H = 8
HD = 64
PAST = 2048
PAGE = 128
R = PAST // P
RB = PAGE // R
TOPK_P = NP_TOK // 4
TOPK_S = 256
NB = 32
NE = 32
NG = 4
EG = 8
DE = 256
CAP = 32
QUAD = 4 * CAP
NQ = NE // 4
NOVF = 2 * T // (CAP + 1)
NOVF += -NOVF % 4
NQX = NQ + NOVF // 4
EPS = 1e-6
NEG = -1e30
GONE = -3e38

O_QA, O_KA, O_VA, O_QI, O_WI, O_KI, O_QB, O_KB, O_GA = 0, 512, 640, 768, 1280, 1288, 1352, 1864, 2888
G0W = O_QB - O_QI
D_IN = 4936


def bucket(dist):
    n = np.maximum(np.asarray(dist), 0)
    nf = np.maximum(n, NB // 2).astype(np.float32)
    big = NB // 2 + (np.log(nf / np.float32(16)) / np.float32(np.log(8.0)) * np.float32(16)).astype(np.int32)
    return np.where(n < NB // 2, n, np.minimum(big, NB - 1))


def shape_constants():
    i = np.arange(P)
    parts = {
        "ident": np.eye(P),
        "after": -(i[:, None] > i[None, :]).astype(float),
        "negones": -np.ones((P, P)),
        "before": (i[:, None] < i[None, :]).astype(float),
        "ones": np.ones((P, P)),
        "strict": np.where(i[:, None] < np.arange(2 * P)[None, :], 0.0, NEG),
        "expand": (np.arange(NS)[:, None] == np.arange(NS * H)[None, :] // H).astype(float),
        "same_h": (np.arange(NS * H)[:, None] % H == np.arange(H)[None, :]).astype(float),
        "same_b": (np.arange(NS * H)[:, None] // H == np.arange(NS)[None, :]).astype(float),
        "segment": np.tile((np.arange(H * R) % R != 0).astype(float), (P, 1)),
        "iota_g": np.tile(np.arange(NG, dtype=float), (P, 3)),
        "iota_8": np.tile(np.arange(EG, dtype=float), (P, 3)),
        "iota_e": np.tile(np.arange(NE, dtype=float), (P, 1)),
        "iota_blk": np.arange(NOVF, dtype=float)[None, :],
        "row_block": (i % RB).astype(float)[:, None],
        "causal": np.where(np.arange(3 * P)[None, :] - P <= i[:, None], 0.0, NEG),
        "fold": (i[:, None] % 32 == np.arange(32)[None, :]).astype(float),
        "half": np.full((P, 3), -0.5),
        "zeros": np.zeros((P, P)),
        "bucket0": np.concatenate([np.ones((1, NS)), np.zeros((NB - 1, NS))]),
    }
    dist = NP_TOK - 1 - np.arange(2 * NP_TOK)
    hot = (bucket(dist)[None, :] == np.arange(NB)[:, None]) & (dist >= 0)[None, :]
    parts["prompt_buckets"] = np.concatenate([hot.astype(float), np.where(dist < 0, NEG, 0.0)[None, :]])
    at, cols = {}, 0
    for name, a in parts.items():
        at[name] = (cols, a.shape[0], a.shape[1])
        cols += a.shape[1]
    packed = np.zeros((P, cols), np.float32)
    for name, a in parts.items():
        c, r, n = at[name]
        packed[:r, c:c + n] = a
    s = np.arange(P)[None, :] * R + np.arange(R)[:, None]
    sample = (bucket(PAST - s.reshape(-1))[None, :] == np.arange(NB)[:, None]).astype(np.float32)
    ids = (np.arange(3)[None, :] * P + i[:, None]).astype(np.int32)
    return at, packed, sample, ids


def decoder_step(nc, a, out, CONST_AT):
    ctx = ExitStack()
    with ctx:
        def sb(name, shape, dt=F32):
            return ctx.enter_context(nc.sbuf_tensor(name, shape, dt))

        def sem(name):
            return ctx.enter_context(nc.semaphore(name))

        consts = sb("consts", [P, a["shape_consts"].shape[1]])

        def const(name):
            c, r, n = CONST_AT[name]
            return consts[0:r, c:c + n]

        ident = const("ident")
        x_rows = sb("x_rows", [P, 3, D])
        xT = sb("xT", [P, KC, T])
        g1T = sb("g1T", [P, KC])
        rows_kva = sb("rows_kva", [P, 3, 2 * P])
        rows_ki = sb("rows_ki", [P, 3, HD])
        rows_vb = sb("rows_vb", [P, 3, H * HD])
        oaT = sb("oaT", [P, 4, T])
        obT = sb("obT", [P, 4, T])
        wi_rows = sb("wi_rows", [P, 3, H])
        small = sb("small", [P, 64])
        page_idx = sb("page_idx", [P, NS], I32)
        unit_idx = sb("unit_idx", [P, 4, NS], I32)
        page_of = sb("page_of", [P, NS], I32)

        RING = 2 * 4 * 4 * H * HD
        arena = sb("arena", [P, RING + 40 * T])
        k_ring = arena[:, 0:RING // 2].rearrange("p (u r n) -> p u r n", u=4, r=4)
        v_ring = arena[:, RING // 2:RING].rearrange("p (u r n) -> p u r n", u=4, r=4)
        projected = arena[:, RING:RING + 24 * T].rearrange("p (c t) -> p c t", t=T)
        kbT, vbT = projected[:, 0:4, :], projected[:, 4:8, :]
        gates = projected[:, 8:24, :]
        qaT = arena[:, RING + 24 * T:RING + 28 * T].rearrange("p (c t) -> p c t", t=T)
        qiT = arena[:, RING + 28 * T:RING + 32 * T].rearrange("p (c t) -> p c t", t=T)
        qbT = arena[:, RING + 32 * T:RING + 36 * T].rearrange("p (c t) -> p c t", t=T)
        kaT = arena[:, RING + 36 * T:RING + 37 * T]
        vaT = arena[:, RING + 37 * T:RING + 38 * T]
        kiT = arena[:, RING + 38 * T:RING + 39 * T]
        w_a = arena[:, RING // 2:RING // 2 + KC * 512].rearrange("p (k n) -> p k n", k=KC)
        w_b = arena[:, RING // 2 + KC * 512:RING].rearrange("p (k n) -> p k n", k=KC)
        kidx_ring = arena[:, 0:2 * R * HD].rearrange("p (s n) -> p s n", s=2)
        ka_ring = arena[:, 2 * R * HD:2 * R * HD + 2 * R * P].rearrange("p (s n) -> p s n", s=2)

        temp = sb("temp", [P, 12288])
        w_ki = sb("w_ki", [P, KC, H + HD])
        xn_rows = temp[:, 0:3 * D].rearrange("p (t n) -> p t n", t=3)
        sample_buckets = temp[0:NB, 3072:3072 + PAST]
        kT_s = temp[:, 5120:6144].rearrange("p (s n) -> p s n", s=2)
        relu_s = temp[0:64, 0:2048].rearrange("p (j n) -> p j n", j=4)
        score_s = temp[0:NS, 6144:6144 + PAST + 8]
        logit_s = temp[0:64, 0:PAST + 8]
        qiPad = temp[:, 8208:8208 + NS * 64].rearrange("p (b m) -> p b m", b=NS)
        qaPad = temp[:, 8720:8720 + NS * 64].rearrange("p (b m) -> p b m", b=NS)
        qiAll = temp[0:HD, 9232:9296]
        qaAll = temp[:, 9296:9360]
        relu_new = temp[0:64, 9360:9368]
        tmp64 = temp[0:64, 9368:9376]
        wcol = temp[0:64, 9376:9377]
        w_blk = temp[0:64, 9384:9392]
        tmp8 = temp[0:NS, 9392:9400]
        top8 = temp[0:NS, 9400:9408]
        bias_bh = temp[0:NB, 9408:9472]
        rows_kb = temp[:, 9472:9472 + 3 * H * HD].rearrange("p (t n) -> p t n", t=3)
        taken_s = temp[0:NS, 3072:3072 + PAST + 8]
        mx_s, sum_s, inv_s = temp[0:64, 12112:12113], temp[0:64, 12113:12114], temp[0:64, 12114:12115]
        new_p = temp[0:64, 12120:12128]
        pT_s = temp[:, 11008:12032].rearrange("p (r m) -> p r m", r=R)
        new_pT = temp[0:NS, 12032:12096]
        relu_p = temp[:, 0:2048].rearrange("p (h s) -> p h s", h=H)
        prob_p = temp[:, 2056:4104].rearrange("p (h s) -> p h s", h=H)
        bias_p = temp[:, 5128:8200].rearrange("p (h j) -> p h j", h=H)
        pT_p = temp[:, 8200:9224].rearrange("p (s n) -> p s n", s=2)
        score_p = temp[:, 4104:4360]
        kept_p = temp[:, 4360:4616]
        o_rows = temp[:, 4616:5128]
        stat_p = sb("stat_p", [P, 64])
        mx_p, sum_p, inv_p, top_p = stat_p[:, 0:8], stat_p[:, 8:16], stat_p[:, 16:24], stat_p[:, 24:32]
        wi_scaled = stat_p[:, 32:48].rearrange("p (t h) -> p t h", t=2)
        kaSwap = arena[:, RING + 39 * T:RING + 40 * T]
        wide_a = temp[:, 8200:8200 + KC * P]
        table33 = sb("table33", [NB + 1, H])
        bias_row = sb("bias_row", [H, 2 * NP_TOK])
        bias_dram = nc.dram_tensor("bias_dram", [H * P * 2 * NP_TOK], F32).ap()
        z_p = temp[:, 0:1536]
        e_p = temp[:, 1536:3072]
        flat = xT.rearrange("p k t -> p (k t)")
        q_all = flat[:, 0:2 * 512].rearrange("p (s n) -> p s n", s=2)
        o_wide = flat[:, 1024:1536]
        a_pad = flat[:, 1536:2048].rearrange("p (r m) -> p r m", r=R)
        q_row = bias_row
        flat = w_ki.rearrange("p k n -> p (k n)")
        z_s, e_s, incl_s = (flat[:, k * H * R:(k + 1) * H * R] for k in range(3))
        later_s, tot_s = flat[:, 384:392], flat[:, 392:400]
        q_dram = nc.dram_tensor("q_dram", [NS, H * HD], F32).ap()
        w_pa = arena[:, RING // 2:RING // 2 + 4 * D].rearrange("p (k n) -> p k n", k=4)
        w_pb = arena[:, RING // 2 + 4 * D:RING].rearrange("p (k n) -> p k n", k=4)
        w_o = temp[:, 0:KC * D].rearrange("p (k n) -> p k n", k=KC)
        mixT = xT
        junk_rows = temp[:, 8192:9216]
        late = arena[:, RING + 32 * T:RING + 40 * T]
        part = late[:, 0:2 * T].rearrange("p (k t) -> p k t", k=2)
        g2_all, gf_all = temp[:, 10240:11264], temp[:, 11264:12288]
        x2_rows = temp[:, 0:3 * D].rearrange("p (t n) -> p t n", t=3)
        w_r = late[:, 528:816].rearrange("p (k e) -> p k e", k=KC)
        b_r = late[:, 816:852]
        rt = late[:, 856:856 + 1152]
        at = [0]

        def piece(n):
            at[0] += n
            return rt[:, at[0] - n:at[0]]

        lg = piece(3 * (NG + NE)).rearrange("p (t n) -> p t n", t=3)
        one_g, eq_g, exp_g = (piece(3 * NG).rearrange("p (t n) -> p t n", t=3) for _ in range(3))
        le, one_1, one_2, eq_e = (piece(3 * EG).rearrange("p (t n) -> p t n", t=3) for _ in range(4))
        mask_1, mask_2, mask_12, ROW = (piece(3 * NE).rearrange("p (t n) -> p t n", t=3) for _ in range(4))
        top_g, top_1, top_2, g_w, e_2, wt_1, wt_2 = (piece(3) for _ in range(7))
        extra, upto, before_e, base_e = (piece(NE) for _ in range(4))
        row_f = piece(6).rearrange("p (k t) -> p k t", k=2)
        blk = rt[0:1, 1152 - NOVF:1152]
        row_i, low_i, high_i, addr_i = (sb(n, [P, 2, 3], I32) for n in ("row_i", "low_i", "high_i", "addr_i"))
        tok_i = sb("tok_i", [P, 3], I32)
        slot_tok = sb("slot_tok", [QUAD, NQX], I32)
        zero_i = sb("zero_i", [QUAD, NQX], I32)
        ovf_i = sb("ovf_i", [1, NOVF + 1], I32)
        blk_tmp = temp[0:1, 9216:9216 + 2 * NOVF * NE]
        SLOT = 3 * 8 * DE
        slots = [arena[:, k * SLOT:(k + 1) * SLOT] for k in range(4)]
        xg = temp[:, 3072:3072 + D]
        xgT = temp[:, 4096:4096 + KC * QUAD].rearrange("p (c n) -> p c n", c=KC)
        y_sb = temp[:, 5120:5120 + D]
        act_e, hid = temp[:, 6144:6400], temp[:, 6400:6656]
        hidT = temp[:, 6656:6656 + 4 * CAP].rearrange("p (f n) -> p f n", f=2)
        y_1 = arena[:, 0:3 * D].rearrange("p (t n) -> p t n", t=3)
        y_2 = arena[:, 3 * D:6 * D].rearrange("p (t n) -> p t n", t=3)
        x2_dram = nc.dram_tensor("x2_dram", [T, D], F32).ap()
        table_dram = nc.dram_tensor("table_dram", [QUAD * NQX, 1], I32).ap()
        y_dram = nc.dram_tensor("y_dram", [QUAD * NQX, D], F32).ap()
        ssq, ms, rstd = small[:, 0:3], small[:, 3:6], small[:, 6:9]

        PS = ctx.enter_context(nc.psum_tensor("PS", [P, 8, 512], F32))
        ACC = 4

        s_const, s_x, s_g1, s_tab = sem("s_const"), sem("s_x"), sem("s_g1"), sem("s_tab")
        s_wki, s_wa, s_wb = sem("s_wki"), sem("s_wa"), sem("s_wb")
        s_kidx = [sem(f"s_kidx{i}") for i in range(2)]
        s_ka = [sem(f"s_ka{i}") for i in range(2)]
        s_page, s_idx = sem("s_page"), sem("s_idx")
        s_prep, s_ssq, s_ms, s_rstd, s_xn = sem("s_prep"), sem("s_ssq"), sem("s_ms"), sem("s_rstd"), sem("s_xn")
        s_xtr, s_xT = sem("s_xtr"), sem("s_xT")
        s_proj, s_evac = sem("s_proj"), sem("s_evac")
        s_tr, s_trf = sem("s_tr"), sem("s_trf")
        s_wexp, s_wcol, s_qipad, s_qapad = sem("s_wexp"), sem("s_wcol"), sem("s_qipad"), sem("s_qapad")
        s_kT_used = sem("s_kT_used")
        s_relc, s_sc, s_scc = sem("s_relc"), sem("s_sc"), sem("s_scc")
        s_lg, s_lgc, s_top = sem("s_lg"), sem("s_lgc"), sem("s_top")
        s_chain = sem("s_chain")
        s_rows, s_rowsT, s_out = sem("s_rows"), sem("s_rowsT"), sem("s_out")

        s_tab33, s_ones33, s_brow, s_browc, s_bdram, s_biasp = (sem(n) for n in (
            "s_tab33", "s_ones33", "s_brow", "s_browc", "s_bdram", "s_biasp"))
        s_taken, s_nm, s_mx, s_exp_s, s_prob_s = (sem(n) for n in (
            "s_taken", "s_nm", "s_mx", "s_exp_s", "s_prob_s"))
        s_swap, s_ip, s_ipr, s_sp, s_lp, s_lpb, s_mxp, s_ep, s_avp, s_onorm, s_oaT = (sem(n) for n in (
            "s_swap", "s_ip", "s_ipr", "s_sp", "s_lp", "s_lpb", "s_mxp", "s_ep", "s_avp", "s_onorm", "s_oaT"))
        s_pT_used = sem("s_pT_used")
        s_zp, s_zpc, s_lnp, s_spp, s_aft, s_tp, s_ap, s_obp, s_obT = (sem(n) for n in (
            "s_zp", "s_zpc", "s_lnp", "s_spp", "s_aft", "s_tp", "s_ap", "s_obp", "s_obT"))

        s_k = [sem(f"s_k{u}") for u in range(4)]
        s_v = [sem(f"s_v{u}") for u in range(4)]
        s_va = [sem(f"s_va{u}") for u in range(4)]
        s_q = [sem(f"s_q{i}") for i in range(2)]
        s_qdram, s_mul, s_kused, s_ls, s_sps, s_scan, s_ts, s_as, s_vused, s_owide, s_apad = (sem(n) for n in (
            "s_qdram", "s_mul", "s_kused", "s_ls", "s_sps", "s_scan", "s_ts", "s_as", "s_vused", "s_owide", "s_apad"))
        s_vaused, s_oas, s_wide = sem("s_vaused"), sem("s_oas"), sem("s_wide")

        s_wp, s_wo, s_gains, s_wr, s_gexp, s_gp1, s_gate, s_pab, s_mixa, s_mix = (sem(n) for n in (
            "s_wp", "s_wo", "s_gains", "s_wr", "s_gexp", "s_gp1", "s_gate", "s_pab", "s_mixa", "s_mix"))
        s_h, s_hadd = sem("s_h"), sem("s_hadd")
        s_ssq2, s_ms2, s_rstd2, s_x2, s_x2d, s_x2tr, s_x2T = (sem(n) for n in (
            "s_ssq2", "s_ms2", "s_rstd2", "s_x2", "s_x2d", "s_x2tr", "s_x2T"))
        s_rl, s_rd, s_re, s_rank, s_rowi, s_tokz, s_zero, s_tokid, s_scat, s_slot, s_ovf = (sem(n) for n in (
            "s_rl", "s_rd", "s_re", "s_rank", "s_rowi", "s_tokz", "s_zero", "s_tokid", "s_scat", "s_slot", "s_ovf"))
        s_we = [sem(f"s_we{k}") for k in range(4)]
        s_wd = [sem(f"s_wd{k}") for k in range(4)]
        s_xg, s_yout, s_hT, s_hTc = sem("s_xg"), sem("s_yout"), sem("s_hT"), sem("s_hTc")
        s_gtr, s_gT, s_gu, s_gexp2, s_act, s_hid, s_down, s_ycopy = (sem(n) for n in (
            "s_gtr", "s_gT", "s_gu", "s_gexp2", "s_act", "s_hid", "s_down", "s_ycopy"))
        s_y12, s_fin, s_ssq3, s_ms3, s_rstd3, s_yo, s_done = (sem(n) for n in (
            "s_y12", "s_fin", "s_ssq3", "s_ms3", "s_rstd3", "s_yo", "s_done"))

        w_in = a["w_in"][0].rearrange("(k p) n -> p k n", p=P)
        we_gate = a["w_gate"].rearrange("o g e d f -> (o g e) d f")
        we_up = a["w_up"].rearrange("o g e d f -> (o g e) d f")
        we_down = a["w_down"].rearrange("o g e f d -> (o g e) f d")
        kidx_rows = a["cache_kidx_a"][0].rearrange("n (q r) d -> (n q) (r d)", r=R)
        ka_rows = a["cache_k_a"][0].rearrange("n (q r) h d -> (n q) (r h d)", r=R)
        va_rows = a["cache_v_a"][0].rearrange("n (q r) h d -> (n q) (r h d)", r=R)
        kb_rows = a["cache_k_b"][0].rearrange("n (q r) h d -> (n q) (r h d)", r=4)
        vb_rows = a["cache_v_b"][0].rearrange("n (q r) h d -> (n q) (r h d)", r=4)

        M_KIDX = 1
        M_KA = M_KIDX + 2 * NS + 2
        M_ROWS = M_KA + 4 * NS + 1
        M_SOFT = M_ROWS + 12
        M_QROW = M_SOFT + 3
        M_PROB, M_OUT, M_SB = [0, 0], [0, 0], [0] * NS
        m = M_QROW + 1
        for step in range(NS + 1):
            if step in (1, 3):
                M_PROB[step // 2] = m
                m += 4
            if step in (2, 4):
                M_OUT[step // 2 - 1] = m
                m += 1
            if step < NS:
                M_SB[step] = m
                m += 2
        M_END = m
        NLOOP = 3
        N_PEEL = 15
        block = ctx.enter_context(nc.Block())

        @block.sync
        def _(sp):
            sp.dma_start(x_rows[:, 0:2, :], a["x_prompt"][0].rearrange("(t p) d -> p t d", p=P)).then_inc(s_x, 16)
            sp.dma_start(x_rows[0:NS, 2, :], a["x_sample"].rearrange("b o d -> (b o) d")).then_inc(s_x, 16)
            sp.dma_start(page_of[:, :], a["pages"]).then_inc(s_page, 16)
            sp.dma_start(consts[:, :], a["shape_consts"]).then_inc(s_const, 16)
            sp.dma_start(w_a[:, :, :], w_in[:, :, O_QI:O_QI + 512]).then_inc(s_wa, 16)
            sp.dma_start(w_ki[:, :, :], w_in[:, :, O_WI:O_QB]).then_inc(s_wki, 16)
            sp.dma_start(w_b[:, :, :], w_in[:, :, O_QA:O_QA + 512]).then_inc(s_wb, 16)
            for b in range(NS):
                sp.dma_start(bias_bh[:, b * H:(b + 1) * H], a["rel_bias_table"]).then_inc(s_tab, 16)
            sp.dma_start(sample_buckets, a["sample_buckets"]).then_inc(s_tab, 16)
            sp.dma_start(table33[0:NB, :], a["rel_bias_table"]).then_inc(s_tab33, 16)
            sp.wait_ge(s_const, 16)
            sp.dma_start(y_dram[NE * CAP:QUAD * NQX, :].rearrange("(p j) (k n) -> p (j k) n", p=P, n=P),
                         const("zeros").unsqueeze(1).to_broadcast([P, NOVF * CAP * D // P // P, P])).then_inc(s_yout, 16)
            sp.wait_ge(s_proj, 4)
            sp.dma_start(w_a[:, :, 0:256], w_in[:, :, O_KA:O_KA + 256]).then_inc(s_wa, 16)
            sp.wait_ge(s_proj, 9)
            sp.dma_start(w_b[:, :, :], w_in[:, :, O_QB:O_QB + 512]).then_inc(s_wb, 16)
            with sp.Fori(0, NLOOP) as i:
                sp.wait_ge(s_proj, i * 8 + 11)
                sp.dma_start(w_a[:, :, :], w_in[:, :, bass.ds(i * 1024 + O_KB, 512)]).then_inc(s_wa, 16)
                sp.wait_ge(s_proj, i * 8 + 15)
                sp.dma_start(w_b[:, :, :], w_in[:, :, bass.ds(i * 1024 + O_KB + 512, 512)]).then_inc(s_wb, 16)
            row = 2 * NP_TOK
            sp.wait_ge(s_browc, 1)
            sp.dma_start(bias_dram.rearrange("(h p j) -> h p j", h=H, p=P),
                         bias_row[:, :].unsqueeze(1).to_broadcast([H, P, row])).then_inc(s_bdram, 16)
            sp.wait_ge(s_bdram, 16)
            sp.wait_ge(s_prob_s, 1)
            for par in range(2):
                src = bass.AP(bias_dram.tensor, par * P * row + P - 1, [[row - 1, P], [2 * P * row, 4], [1, 3 * P]])
                sp.dma_start(bias_p[:, par * 4:par * 4 + 4, :], src).then_inc(s_biasp, 16)

            for b in range(NS):
                sp.wait_ge(s_qdram, 16)
                if b >= 2:
                    sp.wait_ge(s_mul, 4 * (b - 1))
                sp.dma_start(q_all[:, b % 2, :], q_dram[b:b + 1, :].to_broadcast([P, H * HD])).then_inc(s_q[b % 2], 16)
            sp.dma_start(tok_i[:, :], a["token_ids"]).then_inc(s_tokid, 16)
            sp.wait_ge(s_zero, 1)
            sp.dma_start(table_dram.rearrange("(p t) o -> p (t o)", p=QUAD), zero_i[:, :]).then_inc(s_tokz, 16)

            def gate_up(e, k):
                both = slots[k][:, 0:16 * DE].rearrange("p (c g f) -> p c g f", c=KC, g=2)
                for g, w in enumerate((we_gate, we_up)):
                    sp.dma_start(both[:, :, g, :], w[e].rearrange("o (p c) f -> (o p) c f", p=P)).then_inc(s_we[k], 16)

            def down(e, k):
                sp.dma_start(slots[k][:, 16 * DE:24 * DE].rearrange("p (c d) -> p c d", c=2),
                             we_down[e].rearrange("o (c p) d -> (o p) c d", p=P)).then_inc(s_wd[k], 16)

            def expert(e, k):
                gate_up(e, k)
                down(e, k)

            sp.wait_ge(s_vused, 4 * NS)
            sp.dma_start(w_pa, a["w_proj_a"][0].rearrange("(k p) n -> p k n", p=P)).then_inc(s_wp, 16)
            sp.dma_start(w_pb, a["w_proj_b"][0].rearrange("(k p) n -> p k n", p=P)).then_inc(s_wp, 16)
            sp.wait_ge(s_obT, 2)
            for g in range(NG):
                sp.dma_start(w_r[:, :, NG + g * EG:NG + (g + 1) * EG],
                             a["w_router_expert"][0, g].rearrange("(k p) e -> p k e", p=P)).then_inc(s_wr, 16)
            sp.dma_start(w_r[:, :, 0:NG], a["w_router_group"][0].rearrange("(k p) g -> p k g", p=P)).then_inc(s_wr, 16)
            sp.dma_start(b_r[:, 0:NG], a["b_router_group"].to_broadcast([P, NG])).then_inc(s_wr, 16)
            sp.dma_start(b_r[:, NG:NG + NE], a["b_router_expert"].rearrange("o g e -> o (g e)").to_broadcast([P, NE])
                         ).then_inc(s_wr, 16)
            sp.dma_start(w_o, a["w_out"][0].rearrange("(k p) n -> p k n", p=P)).then_inc(s_wo, 16)
            sp.wait_ge(s_oas, 4)
            sp.wait_ge(s_out, 160)
            sp.dma_start(g2_all, a["ln2_g"].to_broadcast([P, D])).then_inc(s_gains, 16)
            sp.dma_start(gf_all, a["ln_f_g"].unsqueeze(0).to_broadcast([P, D])).then_inc(s_gains, 16)
            expert(slice(0, 1), 0)
            sp.wait_ge(s_pab, 2 * KC)
            expert(slice(1, 2), 1)
            sp.wait_ge(s_mix, KC)
            expert(slice(2, 3), 2)
            expert(slice(3, 4), 3)
            with sp.Fori(1, NQ) as i:
                for n in range(2):
                    sp.wait_ge(s_gu, i * 2 + (n - 1))
                    for k in (2 * n, 2 * n + 1):
                        gate_up(bass.ds(i * 4 + k, 1), k)
                    sp.wait_ge(s_down, i * 2 + (n - 1))
                    for k in (2 * n, 2 * n + 1):
                        down(bass.ds(i * 4 + k, 1), k)
            sp.wait_ge(s_ovf, 2)
            n_extra = sp.value_load(ovf_i[0:1, 0:1], min_val=0, max_val=NOVF)
            for q in range(NOVF // 4):
                with sp.If(n_extra > 4 * q):
                    for k in range(4):
                        j = 4 * q + k
                        sp.wait_ge(s_down, NE // 2 + j // 2 - 1)
                        e = sp.value_load(ovf_i[0:1, 1 + j:2 + j], min_val=0, max_val=NE - 1)
                        expert(bass.ds(e, 1), k)

        @block.gpsimd
        def _(pool):
            def fetch(dst, src, idx, landed):
                pool.indirect_dma_start(out=dst, out_offset=None, in_=src,
                                        in_offset=bass.IndirectOffsetOnAxis(ap=idx, axis=0)).then_inc(landed, 16)

            pool.wait_ge(s_idx, 1)
            for b in range(2):
                fetch(kidx_ring[:, b, :], kidx_rows, page_idx[:, b:b + 1], s_kidx[b])
            pool.wait_ge(s_ms, 1)
            nc.gpsimd.tensor_tensor(rstd, ms, const("half"), ALU.pow).then_inc(s_rstd, 1)
            for b in range(2):
                fetch(ka_ring[:, b, :], ka_rows, page_idx[:, b:b + 1], s_ka[b])
            for b in range(2, NS):
                pool.wait_ge(s_tr, M_KIDX + 2 * (b - 1))
                fetch(kidx_ring[:, b % 2, :], kidx_rows, page_idx[:, b:b + 1], s_kidx[b % 2])
            for b in range(2, NS):
                pool.wait_ge(s_tr, M_KA + 4 * (b - 1))
                fetch(ka_ring[:, b % 2, :], ka_rows, page_idx[:, b:b + 1], s_ka[b % 2])

            pool.wait_ge(s_tr, M_KA + 4 * NS)
            for b in range(NS + 1):
                for u in range(4):
                    if b < NS:
                        if b:
                            pool.wait_ge(s_kused, 4 * (b - 1) + u + 1)
                        fetch(k_ring[:, u].rearrange("p r n -> p (r n)"), kb_rows, unit_idx[:, u, b:b + 1], s_k[u])
                    if b:
                        if b == 1 and u == 0:
                            pool.wait_ge(s_proj, N_PEEL + 8 * NLOOP)
                        if b > 1:
                            pool.wait_ge(s_vused, 4 * (b - 2) + u + 1)
                        fetch(v_ring[:, u].rearrange("p r n -> p (r n)"), vb_rows, unit_idx[:, u, b - 1:b], s_v[u])
            for b in range(NS):
                if b < 4:
                    pool.wait_ge(s_kused, 4 * (NS - 1) + b + 1)
                else:
                    pool.wait_ge(s_vaused, b - 3)
                fetch(k_ring[:, b % 4].rearrange("p r n -> p (r n)"), va_rows, page_idx[:, b:b + 1], s_va[b % 4])

            nc.gpsimd.memset(zero_i[:, :], 0).then_inc(s_zero, 1)
            pool.wait_ge(s_ms2, 1)
            nc.gpsimd.tensor_tensor(rstd, ms, const("half"), ALU.pow).then_inc(s_rstd2, 1)
            pool.wait_ge(s_tokz, 16)
            pool.wait_ge(s_tokid, 16)
            pool.wait_ge(s_rowi, 1)
            for k in range(2):
                for t, (_, n) in enumerate(TILES):
                    pool.indirect_dma_start(out=table_dram,
                                            out_offset=bass.IndirectOffsetOnAxis(ap=addr_i[0:n, k, t:t + 1], axis=0),
                                            in_=tok_i[0:n, t:t + 1], in_offset=None).then_inc(s_scat, 16)
            pool.wait_ge(s_scat, 96)
            pool.dma_start(slot_tok[:, :], table_dram.rearrange("(p t) o -> p (t o)", p=QUAD)).then_inc(s_slot, 16)
            pool.wait_ge(s_slot, 16)
            pool.wait_ge(s_x2d, 48)

            def gather(t):
                if t:
                    pool.wait_ge(s_gtr, t)
                fetch(xg, x2_dram, slot_tok[:, t:t + 1], s_xg)

            for t in range(NQ + 1):
                gather(t)
            pool.wait_ge(s_yout, 16 * (NQ + 1))
            pool.wait_ge(s_ovf, 2)
            n_extra = pool.value_load(ovf_i[0:1, 0:1], min_val=0, max_val=NOVF)
            for t in range(NQ, NQX):
                with pool.If(n_extra > 4 * (t - NQ)):
                    if t + 1 < NQX:
                        gather(t + 1)
                    pool.wait_ge(s_yout, 16 * (t + 2))
            for k, y in enumerate((y_1, y_2)):
                for t, (_, n) in enumerate(TILES):
                    fetch(y[0:n, t, :], y_dram, row_i[0:n, k, t:t + 1], s_y12)
            pool.wait_ge(s_ms3, 1)
            nc.gpsimd.tensor_tensor(rstd, ms, const("half"), ALU.pow).then_inc(s_rstd3, 1)

        @block.tensor
        def _(pe):
            def chunk(w, c0, bank, m=P):
                for k in range(KC):
                    last = nc.tensor.matmul(PS[0:m, bank, 0:T], w[:, k, c0:c0 + m], xT[:, k, :],
                                            start=(k == 0), stop=(k == KC - 1))
                return last

            pe.wait_ge(s_const, 16)
            for g in range(4):
                t, half = g // 2, g % 2
                pe.wait_ge(s_xn, t + 1)
                if g >= 2:
                    pe.wait_ge(s_xT, g - 1)
                for c in range(4):
                    d0 = (half * 4 + c) * P
                    last = nc.tensor.transpose(PS[:, 2 + g % 2, c * P:(c + 1) * P], xn_rows[:, t, d0:d0 + P], ident)
                last.then_inc(s_xtr, 1)
            pe.wait_ge(s_xn, 3)
            pe.wait_ge(s_xT, 3)
            for c in range(KC):
                last = nc.tensor.transpose(PS[:, 2, c * NS:(c + 1) * NS],
                                           xn_rows[0:NS, 2, c * P:(c + 1) * P], ident[0:NS, 0:NS])
            last.then_inc(s_xtr, 1)

            pe.wait_ge(s_xT, 5)
            pe.wait_ge(s_wa, 16)
            for n in range(4):
                if n >= 2:
                    pe.wait_ge(s_evac, n - 1)
                chunk(w_a, n * P, n % 2).then_inc(s_proj, 1)
            pe.wait_ge(s_wki, 16)
            pe.wait_ge(s_evac, 3)
            chunk(w_ki, H, 0, HD).then_inc(s_proj, 1)
            for t, (t0, n) in enumerate(TILES):
                for k in range(KC):
                    last = nc.tensor.matmul(PS[0:n, 2, t * H:(t + 1) * H], xT[:, k, t0:t0 + n], w_ki[:, k, 0:H],
                                            start=(k == 0), stop=(k == KC - 1))
            last.then_inc(s_tr, 1)
            pe.wait_ge(s_trf, 1)
            nc.tensor.matmul(PS[0:64, ACC, 0:H], const("expand"), wi_rows[0:NS, 2, :], start=True, stop=True
                             ).then_inc(s_wexp, 1)

            def group(w, n0, count):
                for c in range(count):
                    n = n0 + c
                    pe.wait_ge(s_evac, n - 1)
                    chunk(w, c * P, n % 2).then_inc(s_proj, 1)

            pe.wait_ge(s_wb, 16)
            group(w_b, 5, 4)
            pe.wait_ge(s_wa, 32)
            group(w_a, 9, 2)

            pe.wait_ge(s_qipad, 1)
            pe.wait_ge(s_wcol, 1)
            for b in range(NS):
                pe.wait_ge(s_kidx[b % 2], 16 * (b // 2 + 1))
                for half in range(2):
                    m = M_KIDX + 2 * b + half
                    if m >= 2:
                        pe.wait_ge(s_trf, m - 1)
                    for q in range(4):
                        c = (half * 4 + q) * P
                        last = nc.tensor.transpose(PS[:, 2 + m % 2, q * P:(q + 1) * P],
                                                   kidx_ring[:, b % 2, c:c + P], ident)
                    last.then_inc(s_tr, 1)
                for half in range(2):
                    m = M_KIDX + 2 * b + half
                    pe.wait_ge(s_trf, m + 1)
                    for e in range(2):
                        last = nc.tensor.matmul(PS[0:64, ACC + half * 2 + e, :], qiPad[e * HD:(e + 1) * HD, b, :],
                                                kT_s[e * HD:(e + 1) * HD, m % 2, :],
                                                start=(b == 0), stop=(b == NS - 1))
                    last.then_inc(s_kT_used, 1)
            m = M_KIDX + 2 * NS
            pe.wait_ge(s_trf, m - 1)
            nc.tensor.matmul(PS[0:64, 2 + m % 2, 0:NS], qiAll, kiT[0:HD, NP_TOK:T], start=True, stop=True
                             ).then_inc(s_tr, 1)
            m += 1
            for j in range(4):
                pe.wait_ge(s_relc, j + 1)
                nc.tensor.matmul(PS[0:NS, ACC + j, :], w_blk, relu_s[:, j, :], start=True, stop=True
                                 ).then_inc(s_sc, 1)
            pe.wait_ge(s_trf, m)
            nc.tensor.matmul(PS[0:NS, 2 + m % 2, 0:NS], w_blk, relu_new, start=True, stop=True).then_inc(s_tr, 1)

            pe.wait_ge(s_qapad, 1)
            pe.wait_ge(s_tab, 16 * (NS + 1))
            pe.wait_ge(s_scc, 4)
            for j in range(4):
                nc.tensor.matmul(PS[0:64, ACC + j, :], bias_bh, sample_buckets[:, j * 512:(j + 1) * 512],
                                 start=True, stop=False)

            def turn_ka(b, j):
                m = M_KA + 4 * b + j
                pe.wait_ge(s_trf, m - 1)
                for r in range(4):
                    c = (j * 4 + r) * P
                    last = nc.tensor.transpose(PS[:, 2 + m % 2, r * P:(r + 1) * P], ka_ring[:, b % 2, c:c + P], ident)
                last.then_inc(s_tr, 1)

            for b in range(NS):
                pe.wait_ge(s_ka[b % 2], 16 * (b // 2 + 1))
                turn_ka(b, 0)
                for j in range(4):
                    if j < 3:
                        turn_ka(b, j + 1)
                    m = M_KA + 4 * b + j
                    pe.wait_ge(s_trf, m + 1)
                    nc.tensor.matmul(PS[0:64, ACC + j, :], qaPad[:, b, :], kT_s[:, m % 2, :],
                                     start=False, stop=(b == NS - 1)).then_inc(s_kT_used, 1)
            m = M_KA + 4 * NS
            pe.wait_ge(s_trf, m - 1)
            nc.tensor.matmul(PS[0:64, 2 + m % 2, 0:NS], bias_bh, const("bucket0"), start=True, stop=False)
            nc.tensor.matmul(PS[0:64, 2 + m % 2, 0:NS], qaAll, kaT[:, NP_TOK:T], start=False, stop=True
                             ).then_inc(s_tr, 1)

            pe.wait_ge(s_wb, 32)
            group(w_b, 11, 4)
            with pe.Fori(0, NLOOP) as i:
                for w, s_w, half in ((w_a, s_wa, 0), (w_b, s_wb, 1)):
                    pe.wait_ge(s_w, i * 16 + 48)
                    for c in range(4):
                        n = N_PEEL + 4 * half + c
                        pe.wait_ge(s_evac, i * 8 + (n - 1))
                        chunk(w, c * P, n % 2).then_inc(s_proj, 1)

            m = M_ROWS
            pe.wait_ge(s_evac, N_PEEL + 8)
            for srcs in ([kaT, vaT], [kbT[:, c, :] for c in range(4)], [vbT[:, c, :] for c in range(4)], [kiT]):
                rows = HD if srcs[0] is kiT else P
                for t0, n in TILES:
                    pe.wait_ge(s_trf, m - 1)
                    for c, src in enumerate(srcs):
                        last = nc.tensor.transpose(PS[0:n, 2 + m % 2, c * P:c * P + rows], src[0:rows, t0:t0 + n],
                                                   ident[0:rows, 0:rows])
                    last.then_inc(s_tr, 1)
                    m += 1

            pe.wait_ge(s_tab33, 16)
            pe.wait_ge(s_ones33, 1)
            nc.tensor.matmul(PS[0:H, 0, :], table33[:, :], const("prompt_buckets"), start=True, stop=True
                             ).then_inc(s_brow, 1)

            pe.wait_ge(s_taken, 1)
            pe.wait_ge(s_lgc, 4)
            for j in range(4):
                nc.tensor.matmul(PS[0:64, ACC + j, :], const("expand"), taken_s[:, j * 512:(j + 1) * 512],
                                 start=True, stop=True).then_inc(s_nm, 1)
            pe.wait_ge(s_browc, 1)
            nc.tensor.matmul(PS[0:64, 0, 0:2], const("expand"), taken_s[:, PAST:PAST + 2], start=True, stop=True
                             ).then_inc(s_nm, 1)
            pe.wait_ge(s_prob_s, 1)
            for g in range(2):
                m = M_SOFT + g
                pe.wait_ge(s_trf, m - 1)
                for r in range(8):
                    c = (g * 8 + r) * P
                    last = nc.tensor.transpose(PS[:, 2 + m % 2, r * 64:(r + 1) * 64], logit_s[:, c:c + P],
                                               ident[0:64, 0:64])
                last.then_inc(s_tr, 1)
            m = M_SOFT + 2
            pe.wait_ge(s_trf, m - 1)
            nc.tensor.transpose(PS[0:NS, 2 + m % 2, 0:64], new_p, ident[0:64, 0:64]).then_inc(s_tr, 1)

            m = M_QROW
            pe.wait_ge(s_trf, m - 1)
            for c in range(4):
                last = nc.tensor.transpose(PS[0:NS, 2 + m % 2, c * P:(c + 1) * P], qbT[:, c, NP_TOK:T], ident)
            last.then_inc(s_tr, 1)

            def prompt_a_logits(i):
                q0 = i * P
                pe.wait_ge(s_swap, 1)
                pe.wait_ge(s_mx, 1)
                if i:
                    pe.wait_ge(s_lpb, 4)
                for ho in range(H):
                    par, c = ho // 4, ho % 4
                    half = slice(par * HD, (par + 1) * HD)
                    last = nc.tensor.matmul(PS[:, ACC + ho // 2, ho % 2 * 256:(ho % 2 + 1) * 256],
                                            qiT[half, c, q0:q0 + P], kiT[half, 0:NP_TOK], start=True, stop=True)
                    if ho % 2:
                        last.then_inc(s_ip, 1)
                for ho in range(H):
                    par, c = ho // 4, ho % 4
                    half = slice(par * HD, (par + 1) * HD)
                    keys = kaT if c // 2 == par else kaSwap
                    if ho % 2 == 0:
                        pe.wait_ge(s_ipr, i * 4 + ho // 2 + 1)
                    last = nc.tensor.matmul(PS[:, ACC + ho // 2, ho % 2 * 256:(ho % 2 + 1) * 256],
                                            qaT[half, c, q0:q0 + P], keys[half, 0:NP_TOK], start=True, stop=True)
                    if ho % 2:
                        last.then_inc(s_lp, 1)

            def prompt_a_values(i):
                def turn_p(g):
                    m = M_PROB[i] + g
                    pe.wait_ge(s_trf, m - 1)
                    pe.wait_ge(s_ep, i * H + 2 * g + 2)
                    for k in range(4):
                        last = nc.tensor.transpose(PS[:, 2 + m % 2, k * P:(k + 1) * P],
                                                   prob_p[:, 2 * g + k // 2, k % 2 * P:(k % 2 + 1) * P], ident)
                    last.then_inc(s_tr, 1)

                turn_p(0)
                if i:
                    pe.wait_ge(s_onorm, 1)
                for g in range(4):
                    if g < 3:
                        turn_p(g + 1)
                    m = M_PROB[i] + g
                    pe.wait_ge(s_trf, m + 1)
                    for k in range(4):
                        ho, chunk_s = 2 * g + k // 2, k % 2
                        h = 2 * (ho % 4) + ho // 4
                        last = nc.tensor.matmul(PS[:, 1, h * HD:(h + 1) * HD], pT_p[:, m % 2, k * P:(k + 1) * P],
                                                rows_kva[:, chunk_s, P + h // 4 * HD:P + h // 4 * HD + HD],
                                                start=(chunk_s == 0), stop=(chunk_s == 1))
                    last.then_inc(s_pT_used, 1)

            def prompt_a_turn(i):
                m = M_OUT[i]
                pe.wait_ge(s_onorm, i + 1)
                pe.wait_ge(s_trf, m - 1)
                for c in range(4):
                    last = nc.tensor.transpose(PS[:, 2 + m % 2, c * P:(c + 1) * P], o_rows[:, c * P:(c + 1) * P], ident)
                last.then_inc(s_tr, 1)

            def prompt_b_logits(par):
                half = slice(par * HD, (par + 1) * HD)
                pe.wait_ge(s_lpb, 8)
                if par:
                    pe.wait_ge(s_tp, 1)
                for c in range(4):
                    nc.tensor.matmul(PS[:, ACC + c // 2, c % 2 * 256:(c % 2 + 1) * 256], kbT[half, c, 0:P],
                                     qbT[half, c, 0:NP_TOK], start=True, stop=True)
                for c in range(4):
                    last = nc.tensor.matmul(PS[:, ACC + 2, c * P:(c + 1) * P], kbT[half, c, P:2 * P],
                                            qbT[half, c, P:2 * P], start=True, stop=True)
                last.then_inc(s_zp, 1)

            def prompt_b_after(par):
                pe.wait_ge(s_spp, par + 1)
                late = e_p[:, 1024:1536].rearrange("p (c q) -> p c q", c=4)
                for k in range(2):
                    bank = PS[:, ACC + k, :]
                    nc.tensor.matmul(bank, const("after"), e_p[:, k * 512:(k + 1) * 512], start=True, stop=False)
                    nc.tensor.matmul(bank.rearrange("p (c q) -> p c q", c=2)[:, :, P:2 * P], const("negones"),
                                     late[:, 2 * k:2 * k + 2, :], start=False, stop=True)
                nc.tensor.matmul(PS[:, ACC + 2, :], const("after"), e_p[:, 1024:1536], start=True, stop=True
                                 ).then_inc(s_aft, 1)

            def prompt_b_values(par):
                half = slice(par * HD, (par + 1) * HD)
                pe.wait_ge(s_ap, par + 1)
                pe.wait_ge(s_onorm, 2)
                if par:
                    pe.wait_ge(s_obT, 1)
                for c in range(4):
                    h = 2 * c + par
                    o = PS[half, 1 if c < 2 else ACC + 3, c % 2 * 256:(c % 2 + 1) * 256]
                    nc.tensor.matmul(o, rows_vb[:, 0, h * HD:(h + 1) * HD], z_p[:, c * 256:(c + 1) * 256],
                                     start=True, stop=False)
                    last = nc.tensor.matmul(o[:, P:2 * P], rows_vb[:, 1, h * HD:(h + 1) * HD],
                                            z_p[:, 1024 + c * P:1024 + (c + 1) * P], start=False, stop=True)
                last.then_inc(s_obp, 1)

            def sample(b):
                m = M_SB[b]
                pe.wait_ge(s_scan, b + 1)
                pe.wait_ge(s_trf, m - 1)
                nc.tensor.matmul(PS[:, 2 + m % 2, 0:H], const("after"),
                                 incl_s.rearrange("p (h r) -> p h r", r=R)[:, :, R - 1], start=True, stop=True
                                 ).then_inc(s_tr, 1)
                pe.wait_ge(s_as, b + 1)
                if b:
                    pe.wait_ge(s_owide, b)
                for u in range(4):
                    pe.wait_ge(s_v[u], b * 16 + 16)
                    for r in range(4):
                        last = nc.tensor.matmul(PS[r * 32:(r + 1) * 32, 0, :], a_pad[:, 4 * u + r, :],
                                                v_ring[:, u, r, :], start=(u == 0), stop=(u == 3))
                    last.then_inc(s_vused, 1)
                pe.wait_ge(s_owide, b + 1)
                pe.wait_ge(s_trf, m)
                for c in range(4):
                    last = nc.tensor.matmul(PS[:, 2 + (m + 1) % 2, c * H:(c + 1) * H], o_wide[:, c * P:(c + 1) * P],
                                            const("fold")[:, 0:H], start=True, stop=True)
                last.then_inc(s_tr, 1)

            pe.wait_ge(s_trf, M_QROW)
            pe.wait_ge(s_browc, 1)
            prompt_a_logits(0)
            sample(0)
            prompt_a_values(0)
            prompt_a_logits(1)
            sample(1)
            prompt_a_turn(0)
            sample(2)
            prompt_a_values(1)
            sample(3)
            prompt_a_turn(1)
            prompt_b_logits(0)
            sample(4)
            sample(5)
            prompt_b_after(0)
            prompt_b_values(0)
            prompt_b_logits(1)
            sample(6)
            sample(7)
            prompt_b_after(1)
            prompt_b_values(1)

            pe.wait_ge(s_owide, NS)
            pe.wait_ge(s_tp, 2)
            for b in range(NS):
                pe.wait_ge(s_va[b % 4], 16 * (b // 4 + 1))
                for r in range(R):
                    last = nc.tensor.matmul(PS[r % 4 * 32:(r % 4 + 1) * 32, ACC + b // 4, b % 4 * P:(b % 4 + 1) * P],
                                            pT_s[:, r, b // 4 * 32:(b // 4 + 1) * 32],
                                            k_ring[:, b % 4].rearrange("p r n -> p (r n)")[:, r * P:(r + 1) * P],
                                            start=(r < 4), stop=(r >= R - 4))
                last.then_inc(s_vaused, 1)
            nc.tensor.matmul(PS[:, ACC + 2, 0:64], rows_kva[0:NS, 2, P:2 * P], new_pT, start=True, stop=False)
            pe.wait_ge(s_wide, 1)
            for b in range(NS):
                last = nc.tensor.matmul(PS[:, ACC + 2, b * H:(b + 1) * H], wide_a[:, b * P:(b + 1) * P],
                                        const("fold")[:, b % 4 * H:(b % 4 + 1) * H], start=False, stop=(b == NS - 1))
            last.then_inc(s_vaused, 1)

            pe.wait_ge(s_wp, 32)
            pe.wait_ge(s_oas, 4)
            pe.wait_ge(s_trf, M_END)
            pe.wait_ge(s_obT, 2)
            for c in range(KC):
                if c >= 2:
                    pe.wait_ge(s_mixa, 2 * (c - 1))
                for w, o, bank in ((w_pa, oaT, 0), (w_pb, obT, 2)):
                    for k in range(4):
                        last = nc.tensor.matmul(PS[:, bank + c % 2, 0:T], w[:, k, c * P:(c + 1) * P], o[:, k, :],
                                                start=(k == 0), stop=(k == 3))
                    last.then_inc(s_pab, 1)
            pe.wait_ge(s_wo, 16)
            pe.wait_ge(s_mix, KC)
            for t, (t0, m) in enumerate(TILES):
                for n in range(2):
                    for k in range(KC):
                        last = nc.tensor.matmul(PS[0:m, (ACC + 2 * t + n) % 8, :], mixT[:, k, t0:t0 + m],
                                                w_o[:, k, n * 512:(n + 1) * 512], start=(k == 0), stop=(k == KC - 1))
                    last.then_inc(s_h, 1)

            g = 0
            for t in range(2):
                pe.wait_ge(s_x2, t + 1)
                for half in range(2):
                    for c in range(4):
                        d0 = (half * 4 + c) * P
                        last = nc.tensor.transpose(PS[:, ACC + g, c * P:(c + 1) * P], x2_rows[:, t, d0:d0 + P], ident)
                    last.then_inc(s_x2tr, 1)
                    g += 1
            pe.wait_ge(s_x2, 3)
            for c in range(KC):
                last = nc.tensor.transpose(PS[:, 0, c * NS:(c + 1) * NS], x2_rows[0:NS, 2, c * P:(c + 1) * P],
                                           ident[0:NS, 0:NS])
            last.then_inc(s_x2tr, 1)
            pe.wait_ge(s_x2T, 5)
            pe.wait_ge(s_wr, 16 * (NG + 3))
            for t, (t0, n) in enumerate(TILES):
                for k in range(KC):
                    last = nc.tensor.matmul(PS[0:n, 1, t * 36:(t + 1) * 36], xT[:, k, t0:t0 + n], w_r[:, k, :],
                                            start=(k == 0), stop=(k == KC - 1))
            last.then_inc(s_rl, 1)
            pe.wait_ge(s_re, 1)
            for t, (t0, n) in enumerate(TILES):
                for u in range(t):
                    nc.tensor.matmul(PS[0:n, 2, t * NE:(t + 1) * NE], const("ones")[:, 0:n], mask_12[:, u, :],
                                     start=(u == 0), stop=False)
                nc.tensor.matmul(PS[0:n, 2, t * NE:(t + 1) * NE], const("before")[0:n, 0:n], mask_12[0:n, t, :],
                                 start=(t == 0), stop=True)
            for t, (t0, n) in enumerate(TILES):
                last = nc.tensor.matmul(PS[:, 2, 3 * NE:4 * NE], const("ones")[0:n, :], mask_12[0:n, t, :],
                                        start=(t == 0), stop=(t == 2))
            last.then_inc(s_rank, 1)

            def two_experts(i, n):
                experts = (2 * n, 2 * n + 1)
                for k in experts:
                    pe.wait_ge(s_we[k], i * 32 + 32)
                for d in range(KC):
                    for k in experts:
                        last = nc.tensor.matmul(PS[k * CAP:(k + 1) * CAP, 2 + n, :], xgT[:, d, k * CAP:(k + 1) * CAP],
                                                slots[k][:, d * 2 * DE:(d + 1) * 2 * DE],
                                                start=(d == 0), stop=(d == KC - 1))
                last.then_inc(s_gu, 1)
                if n == 1 and not (isinstance(i, int) and i == NQX - 1):
                    turn(i + 1)
                pe.wait_ge(s_hid, i * 2 + (n + 1))
                for f in range(2):
                    last = nc.tensor.transpose(PS[:, ACC + 2, f * P:(f + 1) * P], hid[:, f * P:(f + 1) * P], ident)
                last.then_inc(s_hT, 1)
                pe.wait_ge(s_hTc, i * 2 + (n + 1))
                for k in experts:
                    pe.wait_ge(s_wd[k], i * 16 + 16)
                for half in range(2):
                    for f in range(2):
                        for k in experts:
                            w0 = 16 * DE + f * D + half * 512
                            last = nc.tensor.matmul(PS[k * CAP:(k + 1) * CAP, ACC + half, :],
                                                    hidT[:, f, k % 2 * CAP:(k % 2 + 1) * CAP],
                                                    slots[k][:, w0:w0 + 512], start=(f == 0), stop=(f == 1))
                last.then_inc(s_down, 1)

            def turn(i):
                pe.wait_ge(s_xg, i * 16 + 16)
                for c in range(KC):
                    last = nc.tensor.transpose(PS[:, c // 4, c % 4 * QUAD:(c % 4 + 1) * QUAD], xg[:, c:D:KC], ident)
                last.then_inc(s_gtr, 1)

            def quad(i):
                pe.wait_ge(s_gT, i + 1)
                two_experts(i, 0)
                two_experts(i, 1)

            pe.wait_ge(s_rd, 1)
            turn(0)
            with pe.Fori(0, NQ) as i:
                quad(i)
            pe.wait_ge(s_ovf, 2)
            n_extra = pe.value_load(ovf_i[0:1, 0:1], min_val=0, max_val=NOVF)
            for t in range(NQ, NQX):
                with pe.If(n_extra > 4 * (t - NQ)):
                    quad(t)

        @block.scalar
        def _(act):
            act.dma_start(g1T[:, :], a["ln1_g"][0].rearrange("(c p) -> p c", p=P),
                          allow_slow_non_contiguous=True).then_inc(s_g1, 16)
            act.wait_ge(s_prep, 1)
            act.wait_ge(s_x, 32)
            for t, (_, n) in enumerate(TILES):
                nc.scalar.activation(xn_rows[0:n, t, :], x_rows[0:n, t, :], ACT.Square,
                                     accum_out=ssq[0:n, t:t + 1]).then_inc(s_ssq, 1)

            def evac(n, dst, rows=P):
                act.wait_ge(s_proj, n + 1)
                nc.scalar.copy(dst, PS[0:rows, n % 2, 0:T]).then_inc(s_evac, 1)

            for n in range(4):
                evac(n, qiT[:, n, :])
            act.wait_ge(s_proj, 5)
            nc.scalar.copy(kiT[0:HD, :], PS[0:HD, 0, 0:T])
            nc.scalar.copy(kiT[HD:P, :], PS[0:HD, 0, 0:T]).then_inc(s_evac, 1)
            act.wait_ge(s_tr, 1)
            nc.scalar.copy(wi_rows[:, 0:2, :], PS[:, 2, 0:2 * H].rearrange("p (t h) -> p t h", t=2))
            nc.scalar.copy(wi_rows[0:NS, 2, :], PS[0:NS, 2, 2 * H:3 * H]).then_inc(s_trf, 1)
            for n in range(5, 9):
                evac(n, qaT[:, n - 5, :])
            evac(9, kaT)
            evac(10, vaT)

            def turned(m, j):
                act.wait_ge(s_tr, m + 1)
                if j >= 2:
                    act.wait_ge(s_kT_used, j - 1)
                nc.scalar.copy(kT_s[:, m % 2, :], PS[:, 2 + m % 2, :]).then_inc(s_trf, 1)

            for j in range(2 * NS):
                turned(M_KIDX + j, j)
            m = M_KIDX + 2 * NS
            act.wait_ge(s_tr, m + 1)
            nc.scalar.activation(relu_new, PS[0:64, 2 + m % 2, 0:NS], ACT.Relu).then_inc(s_trf, 1)
            for j in range(4):
                nc.scalar.activation(relu_s[:, j, :], PS[0:64, ACC + j, :], ACT.Relu).then_inc(s_relc, 1)
            m += 1
            act.wait_ge(s_tr, m + 1)
            act.wait_ge(s_wcol, 1)
            nc.scalar.copy(tmp8, PS[0:NS, 2 + m % 2, 0:NS]).then_inc(s_trf, 1)
            for j in range(4 * NS):
                turned(M_KA + j, 2 * NS + j)
            m = M_KA + 4 * NS
            act.wait_ge(s_tr, m + 1)
            nc.scalar.copy(tmp64, PS[0:64, 2 + m % 2, 0:NS]).then_inc(s_trf, 1)
            for j in range(4):
                nc.scalar.copy(logit_s[:, j * 512:(j + 1) * 512], PS[0:64, ACC + j, :]).then_inc(s_lgc, 1)

            for n in range(11, 15):
                evac(n, qbT[:, n - 11, :])
            for c in range(8):
                evac(N_PEEL + c, projected[:, c, :])
            with act.Fori(1, NLOOP) as i:
                for c in range(8):
                    n = N_PEEL + c
                    act.wait_ge(s_proj, i * 8 + (n + 1))
                    nc.scalar.activation(projected[:, bass.ds(i * 8 + c, 1), :], PS[:, n % 2:n % 2 + 1, 0:T],
                                         ACT.Exp, scale=-1.0).then_inc(s_evac, 1)

            m = M_ROWS
            outs = (("k_a", "v_a"), ("k_b",), ("v_b",), ("kidx",))
            places = (rows_kva, rows_kb, rows_vb, rows_ki)
            for dst in places:
                for t, (t0, n) in enumerate(TILES):
                    act.wait_ge(s_tr, m + 1)
                    nc.scalar.copy(dst[0:n, t, :], PS[0:n, 2 + m % 2, 0:dst.shape[2]]).then_inc(s_trf, 1)
                    m += 1
            act.wait_ge(s_trf, m)
            for names, dst in zip(outs, places):
                for k, name in enumerate(names):
                    w = dst.shape[2] // len(names)
                    act.dma_start(out[name + "_p"].rearrange("(t p) n -> p t n", p=P),
                                  dst[:, 0:2, k * w:(k + 1) * w]).then_inc(s_out, 16)
                    act.dma_start(out[name + "_s"], dst[0:NS, 2, k * w:(k + 1) * w]).then_inc(s_out, 16)

            act.wait_ge(s_brow, 1)
            nc.scalar.copy(bias_row[:, :], PS[0:H, 0, :]).then_inc(s_browc, 1)

            act.wait_ge(s_mx, 1)
            nc.scalar.activation(logit_s[:, 0:PAST + 1], logit_s[:, 0:PAST + 1], ACT.Exp, bias=mx_s,
                                 accum_out=sum_s).then_inc(s_exp_s, 1)
            for g in range(2):
                m = M_SOFT + g
                act.wait_ge(s_tr, m + 1)
                nc.scalar.copy(pT_s[:, g * 8:(g + 1) * 8, :],
                               PS[:, 2 + m % 2, :].rearrange("p (r n) -> p r n", r=8)).then_inc(s_trf, 1)
            m = M_SOFT + 2
            act.wait_ge(s_tr, m + 1)
            nc.scalar.copy(new_pT, PS[0:NS, 2 + m % 2, 0:64]).then_inc(s_trf, 1)

            m = M_QROW
            act.wait_ge(s_bdram, 16)
            act.wait_ge(s_tr, m + 1)
            nc.scalar.activation(q_row[:, :], PS[0:NS, 2 + m % 2, :], ACT.Copy, scale=HD ** -0.5).then_inc(s_trf, 1)
            act.wait_ge(s_trf, m + 1)
            act.dma_start(q_dram, q_row[:, :]).then_inc(s_qdram, 16)

            def prompt_a_relu(i):
                if i:
                    act.wait_ge(s_sp, 1)
                for k in range(4):
                    act.wait_ge(s_ip, i * 4 + k + 1)
                    nc.scalar.activation(relu_p[:, 2 * k:2 * k + 2, :],
                                         PS[:, ACC + k, :].rearrange("p (h s) -> p h s", h=2),
                                         ACT.Relu).then_inc(s_ipr, 1)

            def prompt_a_exp(i):
                act.wait_ge(s_mxp, i + 1)
                for ho in range(H):
                    nc.scalar.activation(prob_p[:, ho, :], prob_p[:, ho, :], ACT.Exp, bias=mx_p[:, ho:ho + 1],
                                         accum_out=sum_p[:, ho:ho + 1]).then_inc(s_ep, 1)
                for g in range(4):
                    m = M_PROB[i] + g
                    act.wait_ge(s_tr, m + 1)
                    if 4 * i + g >= 2:
                        act.wait_ge(s_pT_used, 4 * i + g - 1)
                    nc.scalar.copy(pT_p[:, m % 2, :], PS[:, 2 + m % 2, :]).then_inc(s_trf, 1)

            def prompt_a_turned(i):
                m = M_OUT[i]
                act.wait_ge(s_tr, m + 1)
                nc.scalar.copy(oaT[:, :, i * P:(i + 1) * P],
                               PS[:, 2 + m % 2, :].rearrange("p (c q) -> p c q", c=4)).then_inc(s_trf, 1)

            def prompt_b_ln(par):
                act.wait_ge(s_zpc, par + 1)
                nc.scalar.activation(e_p, z_p, ACT.Abs).then_inc(s_lnp, 1)
                act.wait_ge(s_lnp, 3 * par + 1)
                nc.scalar.activation(e_p, e_p, ACT.Exp, scale=-1.0).then_inc(s_lnp, 1)
                act.wait_ge(s_lnp, 3 * par + 2)
                nc.scalar.activation(e_p, e_p, ACT.Ln, bias=1.0).then_inc(s_lnp, 1)

            def prompt_b_out(par):
                act.wait_ge(s_tp, par + 1)
                nc.scalar.activation(z_p, z_p, ACT.Exp).then_inc(s_ap, 1)
                act.wait_ge(s_obp, par + 1)
                half = slice(par * HD, (par + 1) * HD)
                for k in range(2):
                    last = nc.scalar.copy(obT[half, 2 * k:2 * k + 2, 0:NP_TOK],
                                          PS[half, 1 if k == 0 else ACC + 3, :].rearrange("p (c q) -> p c q", c=2))
                last.then_inc(s_obT, 1)

            def sample_ln(b):
                act.wait_ge(s_kused, b * 4 + 4)
                nc.scalar.activation(e_s, z_s, ACT.Abs).then_inc(s_ls, 1)
                act.wait_ge(s_ls, b * 3 + 1)
                nc.scalar.activation(e_s, e_s, ACT.Exp, scale=-1.0).then_inc(s_ls, 1)
                act.wait_ge(s_ls, b * 3 + 2)
                nc.scalar.activation(e_s, e_s, ACT.Ln, bias=1.0).then_inc(s_ls, 1)
                m = M_SB[b]
                act.wait_ge(s_tr, m + 1)
                nc.scalar.copy(tot_s, PS[:, 2 + m % 2, 0:H]).then_inc(s_trf, 1)
                act.wait_ge(s_apad, 1)
                act.wait_ge(s_ts, b + 1)
                nc.scalar.activation(a_pad[:, :, 0:H], z_s.rearrange("p (h r) -> p r h", r=R), ACT.Exp
                                     ).then_inc(s_as, 1)

            def sample_out(b):
                m = M_SB[b] + 1
                act.wait_ge(s_vused, 4 * b + 4)
                nc.scalar.copy(o_wide, PS[:, 0, :]).then_inc(s_owide, 1)
                act.wait_ge(s_tr, m + 1)
                for par in range(2):
                    half = slice(par * HD, (par + 1) * HD)
                    last = nc.scalar.copy(obT[half, :, NP_TOK + b], PS[half, 2 + m % 2, par:par + 31:H + 2])
                last.then_inc(s_trf, 1)

            def sample(b):
                sample_ln(b)
                sample_out(b)

            prompt_a_relu(0)
            sample(0)
            prompt_a_exp(0)
            prompt_a_relu(1)
            sample(1)
            prompt_a_turned(0)
            sample(2)
            prompt_a_exp(1)
            sample(3)
            prompt_a_turned(1)
            sample(4)
            prompt_b_ln(0)
            sample(5)
            prompt_b_out(0)
            sample(6)
            prompt_b_ln(1)
            sample(7)
            prompt_b_out(1)

            act.wait_ge(s_vaused, NS)
            nc.scalar.copy(wide_a.rearrange("p (b n) -> p b n", b=2), PS[:, ACC:ACC + 2, :]).then_inc(s_wide, 1)

            for t, (_, n) in enumerate(TILES):
                act.wait_ge(s_hadd, (2, 4, 6)[t])
                if t:
                    act.wait_ge(s_ssq2, t)
                nc.scalar.activation(junk_rows[0:n, :], x_rows[0:n, t, :], ACT.Square,
                                     accum_out=ssq[0:n, t:t + 1]).then_inc(s_ssq2, 1)
            for t, (t0, n) in enumerate(TILES):
                act.wait_ge(s_x2, t + 1)
                act.dma_start(x2_dram[t0:t0 + n, :], x2_rows[0:n, t, :]).then_inc(s_x2d, 16)
            act.wait_ge(s_rd, 2)
            nc.scalar.activation(exp_g, exp_g, ACT.Exp).then_inc(s_gexp2, 1)
            act.wait_ge(s_rd, 3)
            nc.scalar.activation(e_2, e_2, ACT.Exp).then_inc(s_gexp2, 1)

            def turned_tokens(i):
                act.wait_ge(s_gtr, i + 1)
                nc.scalar.copy(xgT.rearrange("p (b c) n -> p b (c n)", b=2), PS[:, 0:2, :]).then_inc(s_gT, 1)

            def quad(i):
                for n in range(2):
                    rows = slice(2 * n * CAP, 2 * (n + 1) * CAP)
                    act.wait_ge(s_gu, i * 2 + (n + 1))
                    nc.scalar.activation(act_e[rows, :], PS[rows, 2 + n, 0:DE], ACT.Exp, scale=-1.0).then_inc(s_act, 1)
                    if n == 1 and not (isinstance(i, int) and i == NQX - 1):
                        turned_tokens(i + 1)
                    act.wait_ge(s_hT, i * 2 + (n + 1))
                    nc.scalar.copy(hidT, PS[:, ACC + 2, 0:2 * P].rearrange("p (f m) -> p f m", f=2)[:, :, rows]
                                   ).then_inc(s_hTc, 1)
                act.wait_ge(s_yout, i * 16 + 16)
                act.wait_ge(s_down, i * 2 + 2)
                nc.scalar.copy(y_sb.rearrange("p (b n) -> p b n", b=2), PS[:, ACC:ACC + 2, :]).then_inc(s_ycopy, 1)
                act.wait_ge(s_ycopy, i + 1)
                rows = slice(i * QUAD, (i + 1) * QUAD) if isinstance(i, int) else bass.ds(i * QUAD, QUAD)
                act.dma_start(y_dram[rows, :], y_sb).then_inc(s_yout, 16)

            act.wait_ge(s_x2T, 5)
            turned_tokens(0)
            with act.Fori(0, NQ) as i:
                quad(i)
            act.wait_ge(s_ovf, 2)
            n_extra = act.value_load(ovf_i[0:1, 0:1], min_val=0, max_val=NOVF)
            for t in range(NQ, NQX):
                with act.If(n_extra > 4 * (t - NQ)):
                    quad(t)
            for t, (_, n) in enumerate(TILES):
                act.wait_ge(s_fin, t + 1)
                nc.scalar.activation(y_1[0:n, t, :], x_rows[0:n, t, :], ACT.Square,
                                     accum_out=ssq[0:n, t:t + 1]).then_inc(s_ssq3, 1)
            for t, (_, n) in enumerate(TILES):
                act.wait_ge(s_yo, t + 1)
                act.dma_start(out["y_p"][t * P:(t + 1) * P, :] if t < 2 else out["y_s"], y_2[0:n, t, :]
                              ).then_inc(s_done, 16)
            act.wait_ge(s_done, 48)
            act.wait_ge(s_out, 160)

        @block.vector
        def _(dve):
            chain = [0]

            def link(ins):
                chain[0] += 1
                ins.then_inc(s_chain, 1)
                dve.wait_ge(s_chain, chain[0])

            nc.vector.memset(ssq, 1.0).then_inc(s_prep, 1)
            dve.wait_ge(s_page, 16)
            dve.wait_ge(s_const, 16)
            link(nc.vector.tensor_scalar(page_idx[:, :], page_of[:, :], float(RB), const("row_block")[:, 0:1],
                                         ALU.mult, ALU.add))
            nc.vector.tensor_scalar(unit_idx[:, 0, :], page_idx[:, :], 4.0, None, ALU.mult).then_inc(s_idx, 1)
            for u in range(1, 4):
                nc.vector.tensor_scalar(unit_idx[:, u, :], page_idx[:, :], 4.0, float(u), ALU.mult, ALU.add
                                        ).then_inc(s_idx, 1)
            dve.wait_ge(s_ssq, 3)
            nc.vector.tensor_scalar(ms, ssq, 1.0 / D, EPS, ALU.mult, ALU.add).then_inc(s_ms, 1)
            dve.wait_ge(s_rstd, 1)
            for t, (_, n) in enumerate(TILES):
                nc.vector.tensor_scalar(xn_rows[0:n, t, :], x_rows[0:n, t, :], rstd[0:n, t:t + 1], None,
                                        ALU.mult).then_inc(s_xn, 1)
            dve.wait_ge(s_g1, 16)
            for g in range(4):
                t, half = g // 2, g % 2
                dve.wait_ge(s_xtr, g + 1)
                nc.vector.tensor_tensor(xT[:, half * 4:half * 4 + 4, t * P:(t + 1) * P],
                                        PS[:, 2 + g % 2, :].rearrange("p (c n) -> p c n", c=4),
                                        g1T[:, half * 4:half * 4 + 4].unsqueeze(2).to_broadcast([P, 4, P]),
                                        ALU.mult).then_inc(s_xT, 1)
            dve.wait_ge(s_xtr, 5)
            nc.vector.tensor_tensor(xT[:, :, NP_TOK:T], PS[:, 2, 0:KC * NS].rearrange("p (c n) -> p c n", c=KC),
                                    g1T[:, :].unsqueeze(2).to_broadcast([P, KC, NS]), ALU.mult).then_inc(s_xT, 1)

            link(nc.vector.memset(temp[:, 8208:9232 + 128], 0.0))
            pad = qiPad.rearrange("p b m -> p (b m)")
            dve.wait_ge(s_evac, 4)
            for par in range(2):
                src = qiT[par * HD:(par + 1) * HD, :, NP_TOK:T]
                for half in range(2):
                    for b in range(NS):
                        nc.vector.tensor_copy(pad[half * HD:(half + 1) * HD, b * 72 + par:b * 72 + par + 7:2],
                                              src[:, :, b])
                for b in range(NS):
                    last = nc.vector.tensor_copy(qiAll[:, b * H + par:b * H + par + 7:2], src[:, :, b])
            last.then_inc(s_qipad, 1)
            dve.wait_ge(s_wexp, 1)
            link(nc.vector.tensor_tensor(tmp64, PS[0:64, ACC, 0:H], const("same_h"), ALU.mult))
            link(nc.vector.tensor_reduce(wcol, tmp64, AX_X, ALU.add))
            nc.vector.tensor_scalar(w_blk, const("same_b"), wcol, float(H ** -0.5 * HD ** -0.5), ALU.mult, ALU.mult
                                    ).then_inc(s_wcol, 1)
            dve.wait_ge(s_evac, 9)
            pad = qaPad.rearrange("p b m -> p (b m)")
            for par in range(2):
                for kv in range(2):
                    src = qaT[par * HD:(par + 1) * HD, 2 * kv:2 * kv + 2, NP_TOK:T]
                    for b in range(NS):
                        for dst, at in ((pad, b * 72 + 4 * kv + par), (qaAll, b * H + 4 * kv + par)):
                            last = nc.vector.tensor_scalar(dst[kv * HD:(kv + 1) * HD, at:at + 3:2], src[:, :, b],
                                                           HD ** -0.5, None, ALU.mult)
            last.then_inc(s_qapad, 1)

            by_r = score_s[:, 0:PAST].rearrange("b (x r) -> b r x", r=R)
            for j in range(4):
                half, e = j // 2, j % 2
                dve.wait_ge(s_sc, j + 1)
                nc.vector.tensor_copy(by_r[:, half * 8 + e:half * 8 + e + 7:2, :],
                                      PS[0:NS, ACC + j, :].rearrange("b (q x) -> b q x", q=4)).then_inc(s_scc, 1)
            dve.wait_ge(s_trf, M_KA)
            link(nc.vector.tensor_tensor(tmp8, tmp8, ident[0:NS, 0:NS], ALU.mult))
            nc.vector.tensor_reduce(score_s[:, PAST:PAST + 1], tmp8, AX_X, ALU.add).then_inc(s_scc, 1)
            dve.wait_ge(s_scc, 5)
            with dve.Fori(0, TOPK_S // 8) as i:
                nc.vector.max(top8, score_s[:, 0:PAST + 1]).then_inc(s_top, 1)
                dve.wait_ge(s_top, i * 2 + 1)
                nc.vector.memset(small[0:1, 32:33], 0.0)
                nc.vector.match_replace(out=score_s[:, 0:PAST + 1], in_to_replace=top8,
                                        in_values=score_s[:, 0:PAST + 1], imm_value=GONE).then_inc(s_top, 1)
                dve.wait_ge(s_top, i * 2 + 2)
            nc.vector.memset(table33[NB:NB + 1, :], 1.0).then_inc(s_ones33, 1)
            dve.wait_ge(s_lgc, 4)
            by_r = score_s[:, 0:PAST].rearrange("b (x r) -> b r x", r=R)
            nc.vector.memset(taken_s[:, PAST:PAST + 8], 0.0)
            link(nc.vector.tensor_scalar(taken_s[:, 0:PAST].rearrange("b (r x) -> b r x", r=R), by_r, GONE, NEG,
                                         ALU.not_equal, ALU.mult))
            nc.vector.tensor_scalar(taken_s[:, PAST:PAST + 1], score_s[:, PAST:PAST + 1], GONE, NEG,
                                    ALU.not_equal, ALU.mult).then_inc(s_taken, 1)
            dve.wait_ge(s_trf, M_KA + 4 * NS + 1)
            link(nc.vector.tensor_tensor(tmp64, tmp64, const("same_b"), ALU.mult))
            link(nc.vector.tensor_reduce(logit_s[:, PAST:PAST + 1], tmp64, AX_X, ALU.add))
            for j in range(4):
                dve.wait_ge(s_nm, j + 1)
                cols = slice(j * 512, (j + 1) * 512)
                link(nc.vector.tensor_tensor(logit_s[:, cols], PS[0:64, ACC + j, :], logit_s[:, cols], ALU.add))
            dve.wait_ge(s_nm, 5)
            link(nc.vector.tensor_tensor(logit_s[:, PAST:PAST + 1], PS[0:64, 0, 0:1], logit_s[:, PAST:PAST + 1],
                                         ALU.add))
            link(nc.vector.tensor_reduce(mx_s, logit_s[:, 0:PAST + 1], AX_X, ALU.max))
            nc.vector.tensor_scalar(mx_s, mx_s, -1.0, None, ALU.mult).then_inc(s_mx, 1)
            dve.wait_ge(s_exp_s, 1)
            link(nc.vector.reciprocal(inv_s, sum_s))
            link(nc.vector.tensor_scalar(logit_s[:, 0:PAST + 1], logit_s[:, 0:PAST + 1], inv_s, None, ALU.mult))
            nc.vector.tensor_scalar(new_p, const("same_b"), logit_s[:, PAST:PAST + 1], None, ALU.mult
                                    ).then_inc(s_prob_s, 1)

            link(nc.vector.tensor_scalar(wi_scaled, wi_rows[:, 0:2, :], float(H ** -0.5 * HD ** -0.5), None, ALU.mult))
            nc.vector.tensor_copy(kaSwap[0:HD, :], kaT[HD:P, :])
            nc.vector.tensor_copy(kaSwap[HD:P, :], kaT[0:HD, :]).then_inc(s_swap, 1)
            dve.wait_ge(s_evac, N_PEEL + 8 * NLOOP)
            nc.vector.memset(a_pad, 0.0).then_inc(s_apad, 1)

            def prompt_a_scores(i):
                for ho in range(H):
                    h = 2 * (ho % 4) + ho // 4
                    if ho % 2 == 0:
                        dve.wait_ge(s_ipr, i * 4 + ho // 2 + 1)
                    link(nc.vector.scalar_tensor_tensor(
                        out=score_p, in0=relu_p[:, ho, :], scalar=wi_scaled[:, i, h:h + 1],
                        in1=const("causal")[:, (1 - i) * P:(1 - i) * P + 256] if ho == 0 else score_p,
                        op0=ALU.mult, op1=ALU.add))
                for k in range(TOPK_P // 8):
                    link(nc.vector.max(top_p, score_p))
                    link(nc.vector.match_replace(out=score_p, in_to_replace=top_p, in_values=score_p, imm_value=GONE))
                nc.vector.tensor_scalar(kept_p, score_p, GONE, NEG, ALU.not_equal, ALU.mult).then_inc(s_sp, 1)

            def prompt_a_logits(i):
                dve.wait_ge(s_biasp, 32)
                if i:
                    dve.wait_ge(s_trf, M_PROB[0] + 4)
                for k in range(4):
                    dve.wait_ge(s_lp, i * 4 + k + 1)
                    nc.vector.scalar_tensor_tensor(
                        out=prob_p[:, 2 * k:2 * k + 2, :], in0=PS[:, ACC + k, :].rearrange("p (h s) -> p h s", h=2),
                        scalar=HD ** -0.5, in1=bias_p[:, 2 * k:2 * k + 2, (1 - i) * P:(1 - i) * P + 256],
                        op0=ALU.mult, op1=ALU.add).then_inc(s_lpb, 1)
                dve.wait_ge(s_lpb, 4 * i + 4)
                dve.wait_ge(s_sp, i + 1)
                link(nc.vector.tensor_tensor(prob_p, prob_p, kept_p.unsqueeze(1).to_broadcast([P, H, 256]), ALU.add))
                link(nc.vector.tensor_reduce(mx_p, prob_p, AX_X, ALU.max))
                nc.vector.tensor_scalar(mx_p, mx_p, -1.0, None, ALU.mult).then_inc(s_mxp, 1)

            def prompt_a_norm(i):
                dve.wait_ge(s_ep, (i + 1) * H)
                link(nc.vector.reciprocal(inv_p, sum_p))
                dve.wait_ge(s_pT_used, 4 * i + 4)
                if i:
                    dve.wait_ge(s_trf, M_OUT[0] + 1)
                nc.vector.tensor_tensor(
                    o_rows.rearrange("p (c e d) -> p e c d", c=4, e=2),
                    PS[:, 1, :].rearrange("p (c e d) -> p e c d", c=4, e=2),
                    inv_p.rearrange("p (e c) -> p e c", e=2).unsqueeze(3).to_broadcast([P, 2, 4, HD]),
                    ALU.mult).then_inc(s_onorm, 1)

            def prompt_b_logits(par):
                dve.wait_ge(s_zp, par + 1)
                if par:
                    dve.wait_ge(s_obp, 1)
                else:
                    dve.wait_ge(s_trf, M_PROB[1] + 4)
                nc.vector.scalar_tensor_tensor(
                    out=z_p[:, 0:1024].rearrange("p (c q) -> p c q", c=4),
                    in0=PS[:, ACC:ACC + 2, :].rearrange("p k (c q) -> p (k c) q", c=2), scalar=HD ** -0.5,
                    in1=const("strict").unsqueeze(1).to_broadcast([P, 4, 256]), op0=ALU.mult, op1=ALU.add)
                nc.vector.scalar_tensor_tensor(
                    out=z_p[:, 1024:1536].rearrange("p (c q) -> p c q", c=4),
                    in0=PS[:, ACC + 2, :].rearrange("p (c q) -> p c q", c=4), scalar=HD ** -0.5,
                    in1=const("strict")[:, 0:P].unsqueeze(1).to_broadcast([P, 4, P]), op0=ALU.mult, op1=ALU.add
                ).then_inc(s_zpc, 1)

            def prompt_b_after(par):
                dve.wait_ge(s_lnp, 3 * par + 3)
                nc.vector.scalar_tensor_tensor(out=e_p, in0=z_p, scalar=0.0, in1=e_p, op0=ALU.max, op1=ALU.add
                                               ).then_inc(s_spp, 1)
                dve.wait_ge(s_spp, par + 1)
                link(nc.vector.tensor_tensor(z_p, z_p, e_p, ALU.subtract))
                dve.wait_ge(s_aft, par + 1)
                nc.vector.tensor_tensor(z_p.rearrange("p (k n) -> p k n", k=3), PS[:, ACC:ACC + 3, :],
                                        z_p.rearrange("p (k n) -> p k n", k=3), ALU.add).then_inc(s_tp, 1)

            h_r = lambda t: t.rearrange("p (h r) -> p h r", r=R)

            def sample(b):
                dve.wait_ge(s_q[b % 2], 16 * (b // 2 + 1))
                if b:
                    dve.wait_ge(s_as, b)
                for u in range(4):
                    dve.wait_ge(s_k[u], b * 16 + 16)
                    nc.vector.tensor_tensor(k_ring[:, u], k_ring[:, u],
                                            q_all[:, b % 2:b % 2 + 1, :].to_broadcast([P, 4, H * HD]), ALU.mult
                                            ).then_inc(s_mul, 1)
                    dve.wait_ge(s_mul, b * 4 + (u + 1))
                    nc.vector.tensor_reduce(h_r(z_s).rearrange("p h r -> p r h")[:, 4 * u:4 * u + 4, :],
                                            k_ring[:, u].rearrange("p r (h d) -> p r h d", h=H), AX_X, ALU.add
                                            ).then_inc(s_kused, 1)
                dve.wait_ge(s_ls, b * 3 + 3)
                nc.vector.scalar_tensor_tensor(out=e_s, in0=z_s, scalar=0.0, in1=e_s, op0=ALU.max, op1=ALU.add
                                               ).then_inc(s_sps, 1)
                dve.wait_ge(s_sps, b * 4 + 1)
                nc.vector.tensor_tensor_scan(incl_s, const("segment"), e_s, 0.0, ALU.mult, ALU.add).then_inc(s_scan, 1)
                nc.vector.tensor_tensor(z_s, z_s, e_s, ALU.subtract).then_inc(s_sps, 1)
                dve.wait_ge(s_scan, b + 1)
                dve.wait_ge(s_sps, b * 4 + 2)
                nc.vector.tensor_tensor(z_s, z_s, incl_s, ALU.add).then_inc(s_sps, 1)
                dve.wait_ge(s_trf, M_SB[b] + 1)
                nc.vector.tensor_tensor(later_s, tot_s, h_r(incl_s)[:, :, R - 1], ALU.subtract).then_inc(s_sps, 1)
                dve.wait_ge(s_sps, b * 4 + 4)
                nc.vector.tensor_tensor(h_r(z_s), h_r(z_s), later_s.unsqueeze(2).to_broadcast([P, H, R]), ALU.add
                                        ).then_inc(s_ts, 1)

            prompt_a_scores(0)
            sample(0)
            prompt_a_logits(0)
            sample(1)
            prompt_a_norm(0)
            prompt_a_scores(1)
            sample(2)
            prompt_a_logits(1)
            sample(3)
            prompt_a_norm(1)
            sample(4)
            prompt_b_logits(0)
            sample(5)
            prompt_b_after(0)
            sample(6)
            prompt_b_logits(1)
            sample(7)
            prompt_b_after(1)
            link(nc.vector.tensor_scalar(gates, gates, 1.0, None, ALU.add))
            link(nc.vector.reciprocal(gates, gates))
            dve.wait_ge(s_vaused, NS + 1)
            for kv in range(2):
                for par in range(2):
                    src = PS[kv * HD:(kv + 1) * HD, ACC + 2, 0:64].rearrange("p (b v c e) -> p v e c b", b=NS, v=2, c=2)
                    nc.vector.tensor_copy(oaT[par * HD:(par + 1) * HD, 2 * kv:2 * kv + 2, NP_TOK:T],
                                          src[:, kv, par]).then_inc(s_oas, 1)

            for c in range(KC):
                dve.wait_ge(s_pab, 2 * c + 1)
                nc.vector.tensor_tensor(part[:, 0, :], PS[:, c % 2, 0:T], gates[:, c, :], ALU.mult).then_inc(s_mixa, 1)
                dve.wait_ge(s_pab, 2 * c + 2)
                nc.vector.tensor_tensor(part[:, 1, :], PS[:, 2 + c % 2, 0:T], gates[:, KC + c, :], ALU.mult
                                        ).then_inc(s_mixa, 1)
                dve.wait_ge(s_mixa, 2 * c + 2)
                nc.vector.tensor_tensor(mixT[:, c, :], part[:, 0, :], part[:, 1, :], ALU.add).then_inc(s_mix, 1)
                dve.wait_ge(s_mix, c + 1)
            for j in range(6):
                t, n = j // 2, j % 2
                rows, cols = TILES[t][1], slice(n * 512, (n + 1) * 512)
                dve.wait_ge(s_h, j + 1)
                nc.vector.tensor_tensor(x_rows[0:rows, t, cols], PS[0:rows, (ACC + j) % 8, :], x_rows[0:rows, t, cols],
                                        ALU.add).then_inc(s_hadd, 1)
            dve.wait_ge(s_ssq2, 3)
            nc.vector.tensor_scalar(ms, ssq, 1.0 / D, EPS, ALU.mult, ALU.add).then_inc(s_ms2, 1)
            dve.wait_ge(s_rstd2, 1)
            dve.wait_ge(s_gains, 32)
            for t, (_, n) in enumerate(TILES):
                nc.vector.scalar_tensor_tensor(out=x2_rows[0:n, t, :], in0=x_rows[0:n, t, :], scalar=rstd[0:n, t:t + 1],
                                               in1=g2_all[0:n, :], op0=ALU.mult, op1=ALU.mult).then_inc(s_x2, 1)
            for g in range(4):
                t, half = g // 2, g % 2
                dve.wait_ge(s_x2tr, g + 1)
                nc.vector.tensor_copy(xT[:, half * 4:half * 4 + 4, t * P:(t + 1) * P],
                                      PS[:, ACC + g, :].rearrange("p (c n) -> p c n", c=4)).then_inc(s_x2T, 1)
            dve.wait_ge(s_x2tr, 5)
            nc.vector.tensor_copy(xT[:, :, NP_TOK:T], PS[:, 0, 0:KC * NS].rearrange("p (c n) -> p c n", c=KC)
                                  ).then_inc(s_x2T, 1)

            link(nc.vector.memset(rt[:, :], 0.0))
            dve.wait_ge(s_rl, 1)
            bc3 = lambda t, n: t.unsqueeze(2).to_broadcast([P, 3, n])
            link(nc.vector.tensor_tensor(lg[:, 0:2, :], PS[:, 1, 0:72].rearrange("p (t n) -> p t n", t=2),
                                         b_r[:, :].unsqueeze(1).to_broadcast([P, 2, NG + NE]), ALU.add))
            link(nc.vector.tensor_tensor(lg[0:NS, 2, :], PS[0:NS, 1, 72:108], b_r[0:NS, :], ALU.add))
            lg_g, lg_e = lg[:, :, 0:NG], lg[:, :, NG:NG + NE].rearrange("p t (g e) -> p t g e", g=NG)

            def first_max(val, top, eq, one, iota, n):
                link(nc.vector.tensor_reduce(top, val, AX_X, ALU.max))
                link(nc.vector.tensor_tensor(eq, val, bc3(top, n), ALU.is_equal))
                link(nc.vector.scalar_tensor_tensor(out=eq, in0=eq, scalar=-100.0,
                                                    in1=iota.rearrange("p (t n) -> p t n", t=3),
                                                    op0=ALU.mult, op1=ALU.add))
                link(nc.vector.tensor_reduce(small[:, 16:19], eq, AX_X, ALU.min))
                link(nc.vector.tensor_tensor(one, eq, bc3(small[:, 16:19], n), ALU.is_equal))

            first_max(lg_g, top_g, eq_g, one_g, const("iota_g"), NG)
            dve.wait_ge(s_x2T, 5)
            nc.vector.tensor_copy(small[:, 20:21], small[:, 16:17]).then_inc(s_rd, 1)
            nc.vector.tensor_tensor(exp_g, lg_g, bc3(top_g, NG), ALU.subtract).then_inc(s_rd, 1)
            for t in range(3):
                link(nc.vector.tensor_tensor(mask_1[:, t, :].rearrange("p (g e) -> p g e", g=NG), lg_e[:, t],
                                             one_g[:, t, :].unsqueeze(2).to_broadcast([P, NG, EG]), ALU.mult))
            link(nc.vector.tensor_reduce(le, mask_1.rearrange("p t (g e) -> p t e g", g=NG), AX_X, ALU.add))
            first_max(le, top_1, eq_e, one_1, const("iota_8"), EG)
            link(nc.vector.scalar_tensor_tensor(out=le, in0=one_1, scalar=NEG, in1=le, op0=ALU.mult, op1=ALU.add))
            first_max(le, top_2, eq_e, one_2, const("iota_8"), EG)
            nc.vector.tensor_tensor(e_2, top_2, top_1, ALU.subtract).then_inc(s_rd, 1)
            for one, mask in ((one_1, mask_1), (one_2, mask_2)):
                for t in range(3):
                    link(nc.vector.tensor_tensor(mask[:, t, :].rearrange("p (g e) -> p g e", g=NG),
                                                 one[:, t, :].unsqueeze(1).to_broadcast([P, NG, EG]),
                                                 one_g[:, t, :].unsqueeze(2).to_broadcast([P, NG, EG]), ALU.mult))
            nc.vector.tensor_tensor(mask_12, mask_1, mask_2, ALU.add).then_inc(s_re, 1)
            dve.wait_ge(s_gexp2, 2)
            link(nc.vector.tensor_reduce(g_w, exp_g, AX_X, ALU.add))
            link(nc.vector.tensor_scalar(wt_1, e_2, 1.0, None, ALU.add))
            link(nc.vector.tensor_tensor(wt_1, wt_1, g_w, ALU.mult))
            link(nc.vector.reciprocal(wt_1, wt_1))
            link(nc.vector.tensor_tensor(wt_2, wt_1, e_2, ALU.mult))
            dve.wait_ge(s_rank, 1)
            count = PS[:, 2, 3 * NE:4 * NE]
            link(nc.vector.tensor_scalar(extra, count, float(CAP), None, ALU.is_gt))
            for j in range(2, (T - 1) // CAP + 1):
                link(nc.vector.scalar_tensor_tensor(out=extra, in0=count, scalar=float(j * CAP), in1=extra,
                                                    op0=ALU.is_gt, op1=ALU.add))
            link(nc.vector.tensor_tensor_scan(upto, const("ones")[:, 0:NE], extra, 0.0, ALU.mult, ALU.add))
            link(nc.vector.tensor_tensor(before_e, upto, extra, ALU.subtract))
            link(nc.vector.scalar_tensor_tensor(out=base_e, in0=before_e, scalar=float(NE - 1), in1=const("iota_e"),
                                                op0=ALU.add, op1=ALU.subtract))
            rank = PS[:, 2, 0:3 * NE].rearrange("p (t n) -> p t n", t=3)
            for t, (_, n) in enumerate(TILES):
                link(nc.vector.tensor_scalar(ROW[0:n, t, :], rank[0:n, t, :], float(CAP), None, ALU.is_ge))
                link(nc.vector.tensor_tensor(ROW[0:n, t, :], ROW[0:n, t, :], base_e[0:n, :], ALU.mult))
                link(nc.vector.tensor_tensor(ROW[0:n, t, :], ROW[0:n, t, :], const("iota_e")[0:n, :], ALU.add))
                link(nc.vector.scalar_tensor_tensor(out=ROW[0:n, t, :], in0=ROW[0:n, t, :], scalar=float(CAP),
                                                    in1=rank[0:n, t, :], op0=ALU.mult, op1=ALU.add))
            for k, mask in enumerate((mask_1, mask_2)):
                link(nc.vector.tensor_tensor(mask, mask, ROW, ALU.mult))
                link(nc.vector.tensor_reduce(row_f[:, k, :], mask, AX_X, ALU.add))
            link(nc.vector.tensor_copy(row_i[:, :, :], row_f))
            link(nc.vector.tensor_scalar(low_i[:, :, :], row_i[:, :, :], QUAD - 1, None, ALU.bitwise_and))
            link(nc.vector.tensor_scalar(high_i[:, :, :], row_i[:, :, :], QUAD.bit_length() - 1, None,
                                         ALU.logical_shift_right))
            nc.vector.scalar_tensor_tensor(out=addr_i[:, :, :], in0=low_i[:, :, :], scalar=float(NQX),
                                           in1=high_i[:, :, :], op0=ALU.mult, op1=ALU.add).then_inc(s_rowi, 1)
            nc.vector.tensor_copy(ovf_i[0:1, 0:1], upto[0:1, NE - 1:NE]).then_inc(s_ovf, 1)
            in_blk = blk_tmp.rearrange("p (k n) -> p k n", k=2)
            b_e = lambda t: t.rearrange("p (b e) -> p b e", b=NOVF)
            link(nc.vector.tensor_tensor(b_e(in_blk[:, 0]), const("iota_blk").unsqueeze(2).to_broadcast([1, NOVF, NE]),
                                         before_e[0:1, :].unsqueeze(1).to_broadcast([1, NOVF, NE]), ALU.is_ge))
            link(nc.vector.tensor_tensor(b_e(in_blk[:, 1]), const("iota_blk").unsqueeze(2).to_broadcast([1, NOVF, NE]),
                                         upto[0:1, :].unsqueeze(1).to_broadcast([1, NOVF, NE]), ALU.is_lt))
            link(nc.vector.tensor_tensor(in_blk[:, 0], in_blk[:, 0], in_blk[:, 1], ALU.mult))
            link(nc.vector.tensor_tensor(b_e(in_blk[:, 0]), b_e(in_blk[:, 0]),
                                         const("iota_e")[0:1, :].unsqueeze(1).to_broadcast([1, NOVF, NE]), ALU.mult))
            link(nc.vector.tensor_reduce(blk, b_e(in_blk[:, 0]), AX_X, ALU.add))
            nc.vector.tensor_copy(ovf_i[0:1, 1:NOVF + 1], blk).then_inc(s_ovf, 1)

            def quad(i):
                for n in range(2):
                    rows = slice(2 * n * CAP, 2 * (n + 1) * CAP)
                    g, u = PS[rows, 2 + n, 0:DE], PS[rows, 2 + n, DE:2 * DE]
                    e = act_e[rows, :]
                    dve.wait_ge(s_act, i * 2 + (n + 1))
                    nc.vector.tensor_scalar(e, e, 1.0, None, ALU.add).then_inc(s_gp1, 1)
                    dve.wait_ge(s_gp1, i * 6 + (3 * n + 1))
                    nc.vector.reciprocal(e, e).then_inc(s_gp1, 1)
                    dve.wait_ge(s_gp1, i * 6 + (3 * n + 2))
                    nc.vector.tensor_tensor(e, g, e, ALU.mult).then_inc(s_gp1, 1)
                    dve.wait_ge(s_gp1, i * 6 + (3 * n + 3))
                    nc.vector.tensor_tensor(hid[rows, :], u, e, ALU.mult).then_inc(s_hid, 1)

            link(nc.vector.memset(hid, 0.0))
            with dve.Fori(0, NQ) as i:
                quad(i)
            dve.wait_ge(s_ovf, 2)
            n_extra = dve.value_load(ovf_i[0:1, 0:1], min_val=0, max_val=NOVF)
            for t in range(NQ, NQX):
                with dve.If(n_extra > 4 * (t - NQ)):
                    quad(t)
            dve.wait_ge(s_y12, 96)
            for t, (_, n) in enumerate(TILES):
                x = x_rows[0:n, t, :]
                link(nc.vector.scalar_tensor_tensor(out=x, in0=y_1[0:n, t, :], scalar=wt_1[0:n, t:t + 1], in1=x,
                                                    op0=ALU.mult, op1=ALU.add))
                nc.vector.scalar_tensor_tensor(out=x, in0=y_2[0:n, t, :], scalar=wt_2[0:n, t:t + 1], in1=x,
                                               op0=ALU.mult, op1=ALU.add).then_inc(s_fin, 1)
            dve.wait_ge(s_ssq3, 3)
            nc.vector.tensor_scalar(ms, ssq, 1.0 / D, EPS, ALU.mult, ALU.add).then_inc(s_ms3, 1)
            dve.wait_ge(s_rstd3, 1)
            for t, (_, n) in enumerate(TILES):
                nc.vector.scalar_tensor_tensor(out=y_2[0:n, t, :], in0=x_rows[0:n, t, :], scalar=rstd[0:n, t:t + 1],
                                               in1=gf_all[0:n, :], op0=ALU.mult, op1=ALU.mult).then_inc(s_yo, 1)


def kernel(**inputs):
    import concourse.bacc as bacc
    from concourse.bass_utils import run_bass_kernel_spmd

    nc = bacc.Bacc("TRN2", target_bir_lowering=False, num_devices=1)
    at, packed, sample_buckets, token_ids = shape_constants()
    arrays = {name: np.ascontiguousarray(inputs[name]) for name in inputs if name != "page_table"}
    arrays["pages"] = np.ascontiguousarray(np.repeat(inputs["page_table"], RB, axis=1).T)
    arrays.update(shape_consts=packed, sample_buckets=sample_buckets, token_ids=token_ids)
    a = {n: nc.dram_tensor(f"in_{n}", v.shape, mybir.dt.from_np(v.dtype), kind="ExternalInput").ap()
         for n, v in arrays.items()}
    rows = {"k_a": 2 * HD, "v_a": 2 * HD, "kidx": HD, "k_b": H * HD, "v_b": H * HD}
    shapes = {"y_p": (NP_TOK, D), "y_s": (NS, D)}
    shapes.update({f"{n}_p": (NP_TOK, w) for n, w in rows.items()})
    shapes.update({f"{n}_s": (NS, w) for n, w in rows.items()})
    out = {n: nc.dram_tensor(f"out_{n}", s, F32, kind="ExternalOutput").ap() for n, s in shapes.items()}
    decoder_step(nc, a, out, at)
    got = run_bass_kernel_spmd(nc, [{f"in_{n}": v for n, v in arrays.items()}], core_ids=[0]).results[0]

    def new_rows(name, batch, tokens):
        heads = {"k_a": (2, HD), "v_a": (2, HD), "kidx": (HD,), "k_b": (H, HD), "v_b": (H, HD)}[name[:-2]]
        return got[f"out_{name}"].reshape((1, batch, tokens) + heads)

    names = ("k_a", "v_a", "kidx", "k_b", "v_b")
    return ((got["out_y_p"].reshape(1, NP_TOK, D), got["out_y_s"].reshape(NS, 1, D))
            + tuple(new_rows(f"{n}_p", 1, NP_TOK) for n in names)
            + tuple(new_rows(f"{n}_s", NS, 1) for n in names))
```
